# Optimizing a Trainium2 kernel written in Bass

```python
import jax, jax.numpy as jnp
from jax import lax
import numpy as np

D_MODEL = 1024
BATCH = 1
SEQ = 2048
DEPTH = 1

A_HEADS = 4
A_DK = 128
A_DV = 128
A_QK = A_HEADS * A_DK
A_WIDTH = A_HEADS * A_DV
CHUNK = 64
B_HEADS = 8
B_KV_HEADS = 2
B_HEAD_DIM = 64
B_GROUP = B_HEADS // B_KV_HEADS
B_WIDTH = B_HEADS * B_HEAD_DIM
B_KV = B_KV_HEADS * B_HEAD_DIM
WINDOW = 128
BLOCK = 128
MIX_WIDTH = A_WIDTH + B_WIDTH
D_FF = -(-8 * D_MODEL // (3 * 256)) * 256
EPS = 1e-6
IN_SIZES = (A_QK, A_QK, A_WIDTH, A_WIDTH, B_WIDTH, B_KV, B_KV)
IN_COLS = sum(IN_SIZES)
SPLITS = tuple(int(s) for s in np.cumsum(IN_SIZES)[:-1])

kernel_name = 'hymba_hgrn2_swa_sink_alibi_block'

def rmsnorm(x, g):
    xf = x.astype(jnp.float32)
    y = xf * lax.rsqrt(jnp.mean(xf * xf, axis=-1, keepdims=True) + EPS)
    return (y * g.astype(jnp.float32)).astype(x.dtype)

def hgrn2_mixer(q, f_logit, i, g, lb, norm_g):
    bsz, s, _ = q.shape
    n = s // CHUNK
    f32 = jnp.float32
    qf = jax.nn.silu(q.astype(f32))
    forget = lb + (1.0 - lb) * jax.nn.sigmoid(f_logit.astype(f32))
    key = 1.0 - forget
    log_f = jnp.log(forget)

    def chunks(t, d):
        return t.reshape(bsz, n, CHUNK, A_HEADS, d).transpose(0, 3, 1, 2, 4)

    q_c = chunks(qf, A_DK)
    k_c = chunks(key, A_DK)
    v_c = chunks(i.astype(f32), A_DV)
    b = jnp.cumsum(chunks(log_f, A_DK), axis=3)
    b_last = b[:, :, :, -1:, :]
    q_dec = q_c * jnp.exp(b)
    k_intra = k_c * jnp.exp(-b)
    k_state = k_c * jnp.exp(b_last - b)
    causal = jnp.tril(jnp.ones((CHUNK, CHUNK), dtype=bool))
    a = jnp.where(causal, jnp.einsum('bhnck,bhnsk->bhncs', q_dec, k_intra), 0.0)
    o_intra = jnp.einsum('bhncs,bhnsv->bhncv', a, v_c)
    upd = jnp.einsum('bhnsk,bhnsv->bhnkv', k_state, v_c)
    decay = jnp.exp(b_last[:, :, :, 0, :])

    def step(state, inp):
        dec, u = inp
        return dec[..., None] * state + u, state

    s0 = jnp.zeros((bsz, A_HEADS, A_DK, A_DV), f32)
    _, s_prev = lax.scan(step, s0, (jnp.moveaxis(decay, 2, 0), jnp.moveaxis(upd, 2, 0)))
    s_prev = jnp.moveaxis(s_prev, 0, 2)
    o = o_intra + jnp.einsum('bhnck,bhnkv->bhncv', q_dec, s_prev)
    o = o.transpose(0, 2, 3, 1, 4).reshape(bsz, s, A_HEADS, A_DV)
    o = o * lax.rsqrt(jnp.mean(o * o, axis=-1, keepdims=True) + EPS)
    o = o.reshape(bsz, s, A_WIDTH) * norm_g.astype(f32) * jax.nn.silu(g.astype(f32))
    return o.astype(q.dtype)

def alibi_slopes():
    return jnp.exp2(-(8.0 / B_HEADS) * jnp.arange(1, B_HEADS + 1, dtype=jnp.float32))

def swa_sink_attention(q, k, v, sinks, norm_g):
    bsz, s, _ = q.shape
    nb = s // BLOCK
    f32 = jnp.float32
    qb = q.reshape(bsz, nb, BLOCK, B_KV_HEADS, B_GROUP, B_HEAD_DIM)
    kb = k.reshape(bsz, nb, BLOCK, B_KV_HEADS, B_HEAD_DIM)
    vb = v.reshape(bsz, nb, BLOCK, B_KV_HEADS, B_HEAD_DIM)

    def with_prev(t):
        prev = jnp.pad(t, ((0, 0), (1, 0), (0, 0), (0, 0), (0, 0)))[:, :-1]
        return jnp.concatenate([prev, t], axis=2)

    kk = with_prev(kb)
    vv = with_prev(vb)
    scores = jnp.einsum('bnqhgd,bnshd->bnhgqs', qb, kk).astype(f32) * (B_HEAD_DIM ** -0.5)
    qi = jnp.arange(BLOCK)[:, None]
    kj = jnp.arange(2 * BLOCK)[None, :]
    dist = qi + BLOCK - kj
    key_pos = jnp.arange(nb)[:, None] * BLOCK - BLOCK + kj
    valid = ((dist >= 0) & (dist < WINDOW))[None] & (key_pos >= 0)[:, None, :]
    slopes = alibi_slopes().reshape(B_KV_HEADS, B_GROUP)
    scores = scores - slopes[:, :, None, None] * dist.astype(f32)
    scores = jnp.where(valid[None, :, None, None], scores, -jnp.inf)
    sink = sinks.astype(f32).reshape(B_KV_HEADS, B_GROUP)[None, None, :, :, None, None]
    m = jnp.maximum(jnp.max(scores, axis=-1, keepdims=True), sink)
    p = jnp.exp(scores - m)
    p = p / (jnp.sum(p, axis=-1, keepdims=True) + jnp.exp(sink - m))
    o = jnp.einsum('bnhgqs,bnshd->bnqhgd', p, vv.astype(f32))
    o = o.reshape(bsz, s, B_WIDTH)
    return rmsnorm(o, norm_g).astype(q.dtype)

def setup_inputs(seed: int = 0) -> dict:
    key = jax.random.key(seed)
    ks = jax.random.split(key, 13)
    f32 = jnp.float32
    nrm = lambda k, shape, scale: jax.random.normal(k, shape, f32) * scale
    return {
        'x': jax.random.normal(ks[0], (BATCH, SEQ, D_MODEL), f32),
        'ln1_g': 1.0 + nrm(ks[1], (DEPTH, D_MODEL), 0.02),
        'w_in': nrm(ks[2], (DEPTH, D_MODEL, IN_COLS), D_MODEL ** -0.5),
        'lb_logits': nrm(ks[3], (DEPTH + 1, A_QK), 0.1),
        'hgrn_norm_g': 1.0 + nrm(ks[4], (DEPTH, A_WIDTH), 0.02),
        'attn_sinks': nrm(ks[5], (DEPTH, B_HEADS), 0.5),
        'attn_norm_g': 1.0 + nrm(ks[6], (DEPTH, B_WIDTH), 0.02),
        'w_out': nrm(ks[7], (DEPTH, MIX_WIDTH, D_MODEL), MIX_WIDTH ** -0.5),
        'ln2_g': 1.0 + nrm(ks[8], (DEPTH, D_MODEL), 0.02),
        'w_gate': nrm(ks[9], (DEPTH, D_MODEL, D_FF), D_MODEL ** -0.5),
        'w_up': nrm(ks[10], (DEPTH, D_MODEL, D_FF), D_MODEL ** -0.5),
        'w_down': nrm(ks[11], (DEPTH, D_FF, D_MODEL), D_FF ** -0.5),
        'final_g': 1.0 + nrm(ks[12], (D_MODEL,), 0.02),
    }

def reference(x, ln1_g, w_in, lb_logits, hgrn_norm_g, attn_sinks, attn_norm_g, w_out, ln2_g, w_gate, w_up, w_down, final_g):
    lower_bounds = jnp.cumsum(jax.nn.softmax(lb_logits.astype(jnp.float32), axis=0), axis=0)
    h = x
    for l in range(DEPTH):
        u = rmsnorm(h, ln1_g[l])
        proj = u @ w_in[l]
        a_q, a_f, a_i, a_g, b_q, b_k, b_v = jnp.split(proj, SPLITS, axis=-1)
        y_a = hgrn2_mixer(a_q, a_f, a_i, a_g, lower_bounds[l], hgrn_norm_g[l])
        y_b = swa_sink_attention(b_q, b_k, b_v, attn_sinks[l], attn_norm_g[l])
        h = h + jnp.concatenate([y_a, y_b], axis=-1) @ w_out[l]
        u = rmsnorm(h, ln2_g[l])
        h = h + (jax.nn.silu(u @ w_gate[l]) * (u @ w_up[l])) @ w_down[l]
    return rmsnorm(h, final_g)


_drawn_inputs = setup_inputs


def setup_inputs(seed=0):
    import zlib

    import numpy as np

    out = dict(_drawn_inputs(seed))
    spreads = {}
    factors = {'lb_logits': 8.0,
     'hgrn_norm_g': 8.0,
     'attn_sinks': 3.336,
     'attn_norm_g': 4.602,
     'ln2_g': 4.975,
     'final_g': 2.888}
    for name, (base, spread) in spreads.items():
        noise = np.random.default_rng([zlib.crc32(name.encode()), seed]).standard_normal(out[name].shape)
        drawn = base * np.exp(spread * noise) if base else spread * noise
        out[name] = __import__('jax').numpy.asarray(drawn.astype(out[name].dtype))
    for name, factor in factors.items():
        out[name] = (out[name] * factor).astype(out[name].dtype)
    return out
```

```python
from contextlib import ExitStack

import concourse.bass as bass
from concourse import mybir

F32 = mybir.dt.float32
F32R = mybir.dt.float32r
I32 = mybir.dt.int32
ALU = mybir.AluOpType
ACT = mybir.ActivationFunctionType
AX_X = mybir.AxisListType.X

P = 128
T = 512
TB = T // P
CHUNK = 64
NCH = T // CHUNK
HEADS = 4
KV = 2
PAIRS = 4
BLOCK = 128
EPS = 1e-6
MASKED = -1e30
STEPS = PAIRS * TB

IN_GROUPS = 22
SLOTS = 27


def column_of(slot):
    if slot == 0:
        return 2560
    if slot == 1:
        return 2688
    if slot < 6:
        return 2048 + P * (slot - 2)
    a, part = divmod(slot - 6, 4)
    return (512, 0, 1024, 1536)[part] + P * a


def head_at(slot, first):
    a, r = divmod(slot - first, 4)
    return a if r == 0 and 0 <= a < HEADS else None


V_TURN, KEYS, UPDATE, OUTPUT, NORM_SUM, NORM_MUL = 9, 10, 11, 12, 13, 14
SCORE, P_TURN, PV = 6, 7, 8
SWA_SUM, SWA_MUL = 24, 25


def block_program(nc, x, ln1_g, w_in, lb_logits, hgrn_norm_g, attn_sinks, attn_norm_g, w_out, ln2_g,
                  w_gate, w_up, w_down, final_g, out):
    S, D = x.shape[1], x.shape[2]
    FF = w_gate.shape[2]
    NSB = S // T
    KD = D // P
    KF = FF // P
    CS = D // P
    assert S % T == 0 and KD == 8 and KF % 2 == 0

    DOWN_PARTS = [min(8, KF - k) for k in range(0, KF, 8)]
    ND = len(DOWN_PARTS)
    FFN0 = IN_GROUPS + CS
    DOWN0 = FFN0 + 2 * KF
    UNITS = DOWN0 + CS * ND
    assert UNITS % 2 == 0 and DOWN0 % 2 == 0 and FFN0 % 2 == 0 and (2 * ND) % 2 == 0
    UH = UNITS // 2
    GROUPS = IN_GROUPS + CS + 2 * KF
    DPARTS = CS * ND

    x_t = x.rearrange("o (n p) d -> (o n) p d", p=P)
    out_t = out.rearrange("o (n p) d -> (o n) p d", p=P)
    w_in_k = w_in.rearrange("o (k p) n -> (o p) k n", p=P)
    w_out_k = w_out.rearrange("o (k p) n -> (o p) k n", p=P)
    w_gate_k = w_gate.rearrange("o (k p) n -> (o p) k n", p=P)
    w_up_k = w_up.rearrange("o (k p) n -> (o p) k n", p=P)
    w_down_k = w_down.rearrange("o (k p) n -> (o p) k n", p=P)

    with ExitStack() as ctx:
        def sb(name, shape, dt=F32):
            return ctx.enter_context(nc.sbuf_tensor(name, shape, dt))

        def sem(name):
            return ctx.enter_context(nc.semaphore(name))

        def sems(name, n):
            return [sem(f"{name}{i}") for i in range(n)]

        h = sb("h", [P, KD, T])
        uhi = sb("uhi", [P, KD, T], F32R)
        ulo = sb("ulo", [P, KD, T], F32R)
        raw = [sb(f"raw{i}", [P, 8, P]) for i in range(2)]
        whi = [sb(f"whi{i}", [P, 8, P], F32R) for i in range(2)]
        wlo = [sb(f"wlo{i}", [P, 8, P], F32R) for i in range(2)]
        xs = [sb(f"xs{i}", [P, D]) for i in range(2)]
        os_ = [sb(f"os{i}", [P, D]) for i in range(2)]
        keyz = sb("keyz", [P, KV, 2, T + BLOCK])
        vals = sb("vals", [P, TB + 1, KV * 64])
        kstz = sb("kstz", [P, TB, 2, P])
        amask = sb("amask", [P, TB, P])
        state = sb("state", [P, HEADS, P])
        gu = [sb(f"gu{i}", [P, T]) for i in range(2)]
        dist = sb("dist", [P, 2 * BLOCK])
        dist0 = sb("dist0", [P, 2 * BLOCK])
        ident = sb("ident", [P, P])
        ones = sb("ones", [P, CHUNK])
        causal = sb("causal", [P, P])
        g1 = sb("g1", [P, KD]); g2 = sb("g2", [P, KD]); gf = sb("gf", [P, KD])
        ga = sb("ga", [P, HEADS]); gb = sb("gb", [P, PAIRS])
        lbl = sb("lbl", [P, 2, HEADS]); lbs = sb("lbs", [P, 4, HEADS])
        f_mul = sb("f_mul", [P, HEADS]); f_add = sb("f_add", [P, HEADS])
        sinks = sb("sinks", [P, 8]); nsinks = sb("nsinks", [P, 8])
        epst = sb("epst", [P, 1])
        zero = sb("zero", [P, 1])
        xss = sb("xss", [P, TB]); nrm = sb("nrm", [P, TB]); rnrm = sb("rnrm", [P, TB])
        snrm = sb("snrm", [P, TB]); srnrm = sb("srnrm", [P, TB])
        mx = sb("mx", [P, 2]); nm = sb("nm", [P, 2, 2]); nms = sb("nms", [P, 2])
        es = sb("es", [P, 2]); rs = sb("rs", [P, 2, 2]); den = sb("den", [P, 2]); rd = sb("rd", [P, 2])

        act_at = nc.sbuf_base
        act_at = (act_at + 31) // 32 * 32
        ctx.enter_context(nc.sbuf_tensor("arena", [P, 2 * KF, T], F32))
        ahi = nc.alloc_sbuf_tensor_at("ahi", [P, KF, T], F32R, offset=act_at)
        alo = nc.alloc_sbuf_tensor_at("alo", [P, KF, T], F32R, offset=act_at + KF * T * 4)
        yhi, ylo = ahi, alo
        free_tiles = [act_at + 4 * T * k for k in list(range(KD, KF)) + list(range(KF + KD, 2 * KF))]
        if len(free_tiles) < 28:
            extra = ctx.enter_context(nc.sbuf_tensor("extra", [P, 28 - len(free_tiles), T], F32))
            base = nc.sbuf_base - 4 * T * (28 - len(free_tiles))
            free_tiles += [base + 4 * T * k for k in range(28 - len(free_tiles))]

        def tile(name, shape=(P, T)):
            return nc.alloc_sbuf_tensor_at(name, list(shape), F32, offset=free_tiles.pop(0))

        forget, key, cuminv, kstate, gateq, ivT, iv, sqo = (
            tile(n) for n in ("forget", "key", "cuminv", "kstate", "gateq", "ivT", "iv", "sqo"))
        cum = [tile(f"cum{i}") for i in range(2)]
        qdec = [tile(f"qdec{i}") for i in range(2)]
        gate = [tile(f"gate{i}") for i in range(2)]
        qT = [tile(f"qT{i}") for i in range(PAIRS)]
        pr = [tile(f"pr{i}") for i in range(2)]
        pT = [tile(f"pT{i}") for i in range(2)]
        oT = [tile(f"oT{i}") for i in range(PAIRS)]
        dump_at = free_tiles[0]
        st = [tile(f"st{i}", (P, 4, P)) for i in range(2)]
        xdump = nc.alloc_sbuf_tensor_at("xdump", [P, D], F32, offset=dump_at)
        utmp = [key, cuminv]
        sqs = gu
        sacc = os_[0]
        M = [ctx.enter_context(nc.psum_tensor(f"M{i}", [P, T], F32)) for i in range(4)]
        X = [ctx.enter_context(nc.psum_tensor(f"X{i}", [P, T], F32)) for i in range(4)]

        s_par = sem("s_par")
        s_ini = sem("s_ini")
        s_ini2 = sem("s_ini2")
        s_ini3 = sem("s_ini3")
        s_dst = sem("s_dst")
        s_raw = sems("s_raw", 2)
        s_x = sems("s_x", 2)
        s_out = sems("s_out", 2)
        s_hi = sems("s_hi", 2)
        s_lo = sems("s_lo", 2)
        s_group = sem("s_group")
        s_dpart = sem("s_dpart")

        s_xtr = sem("s_xtr")
        s_xss = sem("s_xss")
        s_xT = sem("s_xT")
        s_root = sem("s_root")
        s_rroot = sem("s_rroot")
        s_nsum = sem("s_nsum")
        s_nmul = sem("s_nmul")
        s_u = sem("s_u")
        s_uhi = sem("s_uhi")
        s_ulo = sem("s_ulo")
        s_kcar = sem("s_kcar")
        s_vcar = sem("s_vcar")
        s_k = sem("s_k")
        s_bvT = sem("s_bvT")
        s_vtr = sem("s_vtr")
        s_vals = sem("s_vals")
        s_q = sem("s_q")
        s_score = sem("s_score")
        s_bias = sem("s_bias")
        s_mx = sem("s_mx")
        s_nm = sem("s_nm")
        s_nms = sem("s_nms")
        s_exp = sem("s_exp")
        s_den = sem("s_den")
        s_rd = sem("s_rd")
        s_prob = sem("s_prob")
        s_ptr = sem("s_ptr")
        s_pT = sem("s_pT")
        s_pv = sem("s_pv")
        s_oT = sem("s_oT")
        s_osq = sem("s_osq")
        s_ssum = sem("s_ssum")
        s_sroot = sem("s_sroot")
        s_srr = sem("s_srr")
        s_smul = sem("s_smul")
        s_yb = sem("s_yb")
        s_ybhi = sem("s_ybhi")
        s_yblo = sem("s_yblo")
        s_dist = sem("s_dist")
        s_tf = sem("s_tf")
        s_tq = sem("s_tq")
        s_iv = sem("s_iv")
        s_tg = sem("s_tg")
        s_f = sem("s_f")
        s_cum = sem("s_cum")
        s_inv = sem("s_inv")
        s_key0 = sem("s_key0")
        s_key = sem("s_key")
        s_kst = sem("s_kst")
        s_qs = sem("s_qs")
        s_qdec = sem("s_qdec")
        s_gs = sem("s_gs")
        s_ivtr = sem("s_ivtr")
        s_ivt = sem("s_ivt")
        s_ktr = sem("s_ktr")
        s_kz = sem("s_kz")
        s_a = sem("s_a")
        s_am = sem("s_am")
        s_upd = sem("s_upd")
        s_st = sem("s_st")
        s_scar = sem("s_scar")
        s_o = sem("s_o")
        s_sq = sem("s_sq")
        s_y1 = sem("s_y1")
        s_asum = sem("s_asum")
        s_aroot = sem("s_aroot")
        s_arr = sem("s_arr")
        s_amul = sem("s_amul")
        s_ya = sem("s_ya")
        s_yahi = sem("s_yahi")
        s_yalo = sem("s_yalo")
        s_h = sem("s_h")
        s_hsq = sem("s_hsq")
        s_hacc = sem("s_hacc")
        s_silu = sems("s_silu", 2)
        s_prod = sems("s_prod", 2)
        s_ahi = sems("s_ahi", 2)
        s_alo = sems("s_alo", 2)
        s_h2 = sems("s_h2", 2)
        s_h2sq = sems("s_h2sq", 2)
        s_h2acc = sems("s_h2acc", 2)
        s_fin = sem("s_fin")
        s_ftr = sem("s_ftr")
        s_osa = sem("s_osa")
        s_osb = sem("s_osb")
        INI = 14

        block = ctx.enter_context(nc.Block())

        def wait_group_read(eng, it, slot):
            a, part = divmod(slot - 6, 4)
            if slot == 0:
                eng.wait_ge(s_k, it * 4 + 4)
            elif slot == 1:
                eng.wait_ge(s_bvT, it + 1)
            elif slot < 6:
                eng.wait_ge(s_q, it * PAIRS + slot - 1)
            else:
                eng.wait_ge((s_tf, s_qs, s_iv, s_gs)[part], it * HEADS + a + 1)

        def wait_unit_used(eng, it, n):
            eng.wait_ge(s_group, it * GROUPS + max(n - 1, 0))

        @block.sync
        def _(sp):
            for dst, src in ((g1, ln1_g), (g2, ln2_g), (ga, hgrn_norm_g), (gb, attn_norm_g)):
                sp.dma_start(dst[:, :], src.rearrange("o (k p) -> p (o k)", p=P),
                             allow_slow_non_contiguous=True).then_inc(s_par, 16)
            sp.dma_start(gf[:, :], final_g.rearrange("(k p) -> p k", p=P),
                         allow_slow_non_contiguous=True).then_inc(s_par, 16)
            for l in range(2):
                sp.dma_start(lbl[:, l, :], lb_logits[l, :].rearrange("(k p) -> p k", p=P),
                             allow_slow_non_contiguous=True).then_inc(s_par, 16)
            sp.dma_start(sinks[:, :], attn_sinks[0, :].partition_broadcast(P)).then_inc(s_par, 16)

            def load(it, s, k, src, nb=8):
                sp.wait_ge(s_lo[s], it * UH + k)
                sp.dma_start(raw[s][:, 0:nb, :], src).then_inc(s_raw[s], 16)

            with sp.Fori(0, NSB) as it:
                for b in range(TB):
                    if b >= 2:
                        sp.wait_ge(s_xtr, it * 2 * TB + 2 * (b - 1))
                        sp.wait_ge(s_xss, it * TB + b - 1)
                    sp.dma_start(xs[b % 2][:, :], x_t[bass.ds(it * TB + b, 1), :, :].rearrange("o p d -> (o p) d")
                                 ).then_inc(s_x[b % 2], 16)
                    if b < 2:
                        load(it, b, 0, w_in_k[:, :, column_of(b):column_of(b) + P])
                for n in range(2, IN_GROUPS):
                    load(it, n % 2, n // 2, w_in_k[:, :, column_of(n):column_of(n) + P])
                for c in range(CS):
                    n = IN_GROUPS + c
                    load(it, n % 2, n // 2, w_out_k[:, :, c * P:(c + 1) * P])
                with sp.Fori(0, KF) as j:
                    load(it, 0, j + FFN0 // 2, w_gate_k[:, :, bass.ds(j * P, P)])
                    load(it, 1, j + FFN0 // 2, w_up_k[:, :, bass.ds(j * P, P)])
                with sp.Fori(0, CS // 2) as cc:
                    for m in range(2 * ND):
                        half, part = divmod(m, ND)
                        k0, nb = 8 * part, DOWN_PARTS[part]
                        load(it, m % 2, cc * ND + DOWN0 // 2 + m // 2,
                             w_down_k[:, k0:k0 + nb, bass.ds(cc * 2 * P + half * P, P)], nb)

        @block.tensor
        def _(pe):
            mm, tr = nc.tensor.matmul, nc.tensor.transpose

            def product(bank, s, hi, lo, kb, first, last):
                mm(bank, whi[s][:, kb, :], hi, start=first, stop=False)
                mm(bank, whi[s][:, kb, :], lo, start=False, stop=False)
                return mm(bank, wlo[s][:, kb, :], hi, start=False, stop=last)

            def spread(bank, factors, done):
                for b in range(TB):
                    last = mm(bank[:, b * P:(b + 1) * P], factors[:, b:b + 1].broadcast_to([P, P]), ident[:, :],
                              start=True, stop=True)
                last.then_inc(done, 1)

            def sums(bank, squares, done):
                for b in range(TB):
                    for n, sq in enumerate(squares):
                        last = mm(bank[:, b:b + 1], sq[:, b * P:(b + 1) * P], ones[:, 0:1],
                                  start=(n == 0), stop=(n == len(squares) - 1))
                last.then_inc(done, 1)

            pe.wait_ge(s_ini, INI)
            with pe.Fori(0, NSB) as it:
                for b in range(TB):
                    pe.wait_ge(s_x[b % 2], it * 32 + 16 * (b // 2 + 1))
                    for half in range(2):
                        if b:
                            pe.wait_ge(s_xT, it * 2 * TB + 2 * (b - 1) + half + 1)
                        for c in range(4):
                            k = 4 * half + c
                            last = tr(X[half][:, c * P:(c + 1) * P], xs[b % 2][:, k * P:(k + 1) * P], ident[:, :])
                        last.then_inc(s_xtr, 1)
                pe.wait_ge(s_rroot, it * 3 + 1)
                pe.wait_ge(s_osa, it * TB)
                spread(X[2], rnrm, s_nmul)

                def group(slot):
                    if slot >= 3:
                        wait_group_read(pe, it, slot - 3)
                    pe.wait_ge(s_lo[slot % 2], it * UH + slot // 2 + 1)
                    for k in range(KD):
                        if slot == 0:
                            pe.wait_ge(s_ulo, it * 2 * KD + k + 1)
                        last = product(M[slot % 3][:, :], slot % 2, uhi[:, k, :], ulo[:, k, :], k,
                                       k == 0, k == KD - 1)
                    last.then_inc(s_group, 1)

                def v_values():
                    pe.wait_ge(s_bvT, it + 1)
                    for b in range(TB):
                        last = tr(X[1][:, b * P:(b + 1) * P], ivT[:, b * P:(b + 1) * P], ident[:, :])
                    last.then_inc(s_vtr, 1)

                def scores(i):
                    p, b = divmod(i, TB)
                    if i == 0:
                        pe.wait_ge(s_k, it * 4 + 4)
                    if b == 0:
                        pe.wait_ge(s_q, it * PAIRS + p + 1)
                    if i:
                        pe.wait_ge(s_bias, it * STEPS + i)
                    for par in range(2):
                        last = mm(X[0][:, par * 2 * BLOCK:(par + 1) * 2 * BLOCK], qT[p][:, b * P:(b + 1) * P],
                                  keyz[:, p // 2, par, b * P:b * P + 2 * BLOCK], start=True, stop=True)
                    last.then_inc(s_score, 1)

                def p_turn(i):
                    pe.wait_ge(s_prob, it * STEPS + i + 1)
                    if i:
                        pe.wait_ge(s_pT, it * STEPS + i)
                    else:
                        pe.wait_ge(s_vals, it + 1)
                    for n in range(4):
                        last = tr(X[1][:, n * P:(n + 1) * P], pr[i % 2][:, n * P:(n + 1) * P], ident[:, :])
                    last.then_inc(s_ptr, 1)

                def pv(i):
                    p, b = divmod(i, TB)
                    g = p // 2
                    pe.wait_ge(s_pT, it * STEPS + i + 1)
                    if b == 0 and p:
                        pe.wait_ge(s_oT, it * PAIRS + p)
                    for par in range(2):
                        for kb in range(2):
                            last = mm(M[3][64 * par:64 * par + 64, b * P:(b + 1) * P],
                                      vals[:, b + kb, 64 * g:64 * g + 64],
                                      pT[i % 2][:, (2 * par + kb) * P:(2 * par + kb + 1) * P],
                                      start=(kb == 0), stop=(kb == 1))
                    last.then_inc(s_pv, 1)

                def iv_turn(a):
                    pe.wait_ge(s_iv, it * HEADS + a + 1)
                    if a:
                        pe.wait_ge(s_y1, it * HEADS + a)
                    for b in range(TB):
                        last = tr(X[2][:, b * P:(b + 1) * P], ivT[:, b * P:(b + 1) * P], ident[:, :])
                    last.then_inc(s_ivtr, 1)

                def keys(a):
                    pe.wait_ge(s_key, it * HEADS + a + 1)
                    pe.wait_ge(s_qdec, it * HEADS + a + 1)
                    pe.wait_ge(s_ivt, it * HEADS + a + 1)
                    for b in range(TB):
                        last = mm(X[2][:, b * P:(b + 1) * P], key[:, b * P:(b + 1) * P],
                                  qdec[a % 2][:, b * P:(b + 1) * P], start=True, stop=True)
                    last.then_inc(s_a, 1)
                    pe.wait_ge(s_kst, it * HEADS + a + 1)
                    if a:
                        pe.wait_ge(s_ya, it * HEADS + a)
                    else:
                        pe.wait_ge(s_osb, it * TB)
                    for b in range(TB):
                        last = tr(X[3][:, b * P:(b + 1) * P], kstate[:, b * P:(b + 1) * P], ident[:, :])
                    last.then_inc(s_ktr, 1)

                def update(a):
                    pe.wait_ge(s_kz, it * 2 * HEADS + 2 * a + 2)
                    pe.wait_ge(s_am, it * HEADS + a + 1)
                    for half in range(2):
                        for n in range(4):
                            b, c = divmod(4 * half + n, 2)
                            last = mm(X[2 + half][:, n * P:(n + 1) * P], kstz[:, b, c, :], iv[:, b * P:(b + 1) * P],
                                      start=True, stop=True)
                        last.then_inc(s_upd, 1)

                def output(a):
                    pe.wait_ge(s_st, it * NCH * HEADS + NCH * a + 4)
                    for b in range(TB):
                        mm(X[2][:, b * P:(b + 1) * P], iv[:, b * P:(b + 1) * P], amask[:, b, :],
                           start=(b == 0), stop=False, skip_group_check=True)
                    pe.wait_ge(s_scar, it * HEADS)
                    for n in range(NCH):
                        if n > 4:
                            pe.wait_ge(s_st, it * NCH * HEADS + NCH * a + n)
                        before = state[:, a, :] if n == 0 else st[(n - 1) // 4][:, (n - 1) % 4, :]
                        last = mm(X[2][:, n * CHUNK:(n + 1) * CHUNK], before,
                                  qdec[a % 2][:, n * CHUNK:(n + 1) * CHUNK],
                                  start=False, stop=(n == NCH - 1), skip_group_check=True)
                    last.then_inc(s_o, 1)

                def head_sum(a):
                    pe.wait_ge(s_sq, it * HEADS + a + 1)
                    pe.wait_ge(s_st, it * NCH * HEADS + NCH * a + NCH)
                    sums(X[3], [sqo], s_asum)

                def head_mul(a):
                    pe.wait_ge(s_arr, it * HEADS + a + 1)
                    spread(X[3], rnrm, s_amul)

                def out_part(c, ks, first, last_part):
                    for k in ks:
                        last = product(M[c % 4][:, :], (IN_GROUPS + c) % 2, yhi[:, k, :], ylo[:, k, :], k,
                                       first and k == ks[0], last_part and k == ks[-1])
                    return last

                EARLY = [0, 1]
                LATE = [3, 4, 5, 6, 7]
                for slot in range(SLOTS):
                    if slot < IN_GROUPS:
                        group(slot)
                    elif slot < IN_GROUPS + 2:
                        c = slot - IN_GROUPS
                        wait_group_read(pe, it, (21, 19)[c])
                        pe.wait_ge(s_lo[slot % 2], it * UH + slot // 2 + 1)
                        pe.wait_ge(s_yalo, it * HEADS + 2)
                        out_part(c, EARLY, True, False)
                    elif slot < IN_GROUPS + 4:
                        pe.wait_ge(s_yalo, it * HEADS + 3)
                        out_part(slot - IN_GROUPS - 2, [2], False, False)
                    if slot == 1:
                        v_values()
                    a = head_at(slot, NORM_MUL)
                    if a is not None:
                        head_mul(a)
                    if slot == SWA_SUM:
                        pe.wait_ge(s_osq, it * PAIRS + PAIRS)
                        sums(X[1], qT, s_ssum)
                    if slot == SWA_MUL:
                        pe.wait_ge(s_srr, it + 1)
                        spread(X[1], srnrm, s_smul)
                    if 0 <= slot - SCORE < STEPS:
                        scores(slot - SCORE)
                    if 0 <= slot - P_TURN < STEPS:
                        p_turn(slot - P_TURN)
                    if 0 <= slot - PV < STEPS:
                        pv(slot - PV)
                    for first, step in ((V_TURN, iv_turn), (KEYS, keys), (UPDATE, update), (OUTPUT, output),
                                        (NORM_SUM, head_sum)):
                        a = head_at(slot, first)
                        if a is not None:
                            step(a)

                pe.wait_ge(s_yalo, it * HEADS + HEADS)
                pe.wait_ge(s_yblo, it * PAIRS + PAIRS)
                for c in range(CS):
                    if c < 2:
                        last = out_part(c, LATE, False, True)
                    else:
                        if c == 2:
                            wait_group_read(pe, it, 20)
                        elif c == 3:
                            pe.wait_ge(s_oT, it * PAIRS + PAIRS)
                        else:
                            pe.wait_ge(s_h, it * KD + c - 3)
                        n = IN_GROUPS + c
                        pe.wait_ge(s_lo[n % 2], it * UH + n // 2 + 1)
                        last = out_part(c, list(range(8)), True, True)
                    last.then_inc(s_group, 1)
                pe.wait_ge(s_hacc, it * KD + KD)
                sums(X[0], [sacc], s_nsum)
                pe.wait_ge(s_rroot, it * 3 + 2)
                spread(X[0], rnrm, s_nmul)

                with pe.Fori(0, KF // 2) as jj:
                    pe.wait_ge(s_ulo, it * 2 * KD + 2 * KD)
                    for n in range(4):
                        pe.wait_ge((s_silu, s_prod)[n % 2][n // 2], it * (KF // 2) + jj)
                        pe.wait_ge(s_lo[n % 2], it * UH + FFN0 // 2 + 2 * jj + n // 2 + 1)
                        for k in range(KD):
                            last = product(M[n][:, :], n % 2, uhi[:, k, :], ulo[:, k, :], k, k == 0, k == KD - 1)
                        last.then_inc(s_group, 1)
                with pe.Fori(0, CS // 2) as cc:
                    for j in range(2):
                        pe.wait_ge(s_alo[j], (it + 1) * (KF // 2))
                    for half in range(2):
                        pe.wait_ge(s_h2[half], it * (KD // 2) + cc)
                        for part in range(ND):
                            m = half * ND + part
                            pe.wait_ge(s_lo[m % 2], it * UH + DOWN0 // 2 + cc * ND + m // 2 + 1)
                            for kb in range(DOWN_PARTS[part]):
                                k = 8 * part + kb
                                last = product(M[half][:, :], m % 2, ahi[:, k, :], alo[:, k, :], kb,
                                               k == 0, k == KF - 1)
                            last.then_inc(s_dpart, 1)

                for half in range(2):
                    pe.wait_ge(s_h2acc[half], (it + 1) * (KD // 2))
                sums(X[0], [sacc], s_nsum)
                pe.wait_ge(s_rroot, it * 3 + 3)
                spread(X[0], rnrm, s_nmul)
                pe.wait_ge(s_fin, it * KD + KD)
                for b in range(TB):
                    for half in range(2):
                        if b:
                            pe.wait_ge((s_osa, s_osb)[half], it * TB + b)
                        for c in range(4):
                            last = tr(X[2 + half][:, c * P:(c + 1) * P], h[:, 4 * half + c, b * P:(b + 1) * P],
                                      ident[:, :])
                        last.then_inc(s_ftr, 1)

        @block.scalar
        def _(act):
            A = nc.scalar.activation

            act.wait_ge(s_ini2, 3)
            A(lbs[:, 0:2, :], lbs[:, 2:4, :], ACT.Exp).then_inc(s_ini3, 1)
            act.wait_ge(s_ini, INI)

            def make_hi(it, s, k, nb=8):
                act.wait_ge(s_raw[s], it * (UH * 16) + k * 16 + 16)
                A(whi[s][:, 0:nb, :], raw[s][:, 0:nb, :], ACT.Copy).then_inc(s_hi[s], 1)

            with act.Fori(0, NSB) as it:
                for b in range(TB):
                    act.wait_ge(s_x[b % 2], it * 32 + 16 * (b // 2 + 1))
                    act.wait_ge(s_xss, it * TB + b)
                    A(xdump[:, :], xs[b % 2][:, :], ACT.Square, accum_out=xss[:, b:b + 1]).then_inc(s_xss, 1)
                    for half in range(2):
                        act.wait_ge(s_xtr, it * 2 * TB + 2 * b + half + 1)
                        A(h[:, 4 * half:4 * half + 4, b * P:(b + 1) * P],
                          X[half][:, :].rearrange("p (c t) -> p c t", c=4), ACT.Copy).then_inc(s_xT, 1)
                act.wait_ge(s_xss, it * TB + TB)
                A(nrm[:, :], xss[:, :], ACT.Sqrt, scale=1.0 / D, bias=epst[:, 0:1]).then_inc(s_root, 1)
                for s in range(2):
                    wait_unit_used(act, it, s)
                    make_hi(it, s, 0)
                for k in range(KD):
                    act.wait_ge(s_u, it * 2 * KD + k + 1)
                    A(uhi[:, k, :], utmp[k % 2][:, :], ACT.Copy).then_inc(s_uhi, 1)

                def head_group(a, part, bank):
                    if part == 0:
                        if a:
                            act.wait_ge(s_key0, it * HEADS + a)
                            act.wait_ge(s_cum, it * HEADS + a)
                        A(forget[:, :], M[bank][:, :], ACT.Tanh, scale=0.5).then_inc(s_tf, 1)
                    if part == 1:
                        if a:
                            act.wait_ge(s_qdec, it * HEADS + a)
                        A(gateq[:, :], M[bank][:, :], ACT.Tanh, scale=0.5).then_inc(s_tq, 1)
                    if part == 2:
                        if a:
                            act.wait_ge(s_ivtr, it * HEADS + a)
                        A(ivT[:, :], M[bank][:, :], ACT.Copy).then_inc(s_iv, 1)
                    if part == 3:
                        if a >= 2:
                            act.wait_ge(s_yalo, it * HEADS + a - 1)
                        A(gate[a % 2][:, :], M[bank][:, :], ACT.Tanh, scale=0.5).then_inc(s_tg, 1)

                def iv_turn(a):
                    act.wait_ge(s_ivtr, it * HEADS + a + 1)
                    if a:
                        act.wait_ge(s_o, it * HEADS + a)
                    A(iv[:, :], X[2][:, :], ACT.Copy).then_inc(s_ivt, 1)

                def keys(a):
                    act.wait_ge(s_ktr, it * HEADS + a + 1)
                    act.wait_ge(s_upd, it * 2 * HEADS + 2 * a)
                    for c in range(2):
                        r = slice(64 * c, 64 * c + 64)
                        A(kstz[r, :, c, :], X[3][r, :].rearrange("p (b k) -> p b k", b=TB),
                          ACT.Copy).then_inc(s_kz, 1)

                def output(a):
                    act.wait_ge(s_o, it * HEADS + a + 1)
                    if a:
                        act.wait_ge(s_asum, it * HEADS + a)
                    A(sqo[:, :], X[2][:, :], ACT.Square).then_inc(s_sq, 1)

                def head_sum(a):
                    act.wait_ge(s_asum, it * HEADS + a + 1)
                    if a:
                        act.wait_ge(s_arr, it * HEADS + a)
                    else:
                        act.wait_ge(s_rroot, it * 3 + 1)
                    A(nrm[:, :], X[3][:, 0:TB], ACT.Sqrt, scale=1.0 / P, bias=epst[:, 0:1]).then_inc(s_aroot, 1)

                def head_mul(a):
                    act.wait_ge(s_ya, it * HEADS + a + 1)
                    A(yhi[:, a, :], gate[a % 2][:, :], ACT.Copy).then_inc(s_yahi, 1)

                def scores(i):
                    w = i % 2
                    act.wait_ge(s_nms, it * STEPS + i + 1)
                    act.wait_ge(s_den, it * STEPS + i)
                    for par in range(2):
                        half = pr[w][:, par * 256:(par + 1) * 256]
                        A(half, half, ACT.Exp, scale=0.125, bias=nm[:, w, par:par + 1],
                          accum_out=rs[:, w, par:par + 1])
                    A(es[:, :], nms[:, :], ACT.Exp).then_inc(s_exp, 1)

                def p_turn(i):
                    act.wait_ge(s_ptr, it * STEPS + i + 1)
                    if i >= 2:
                        act.wait_ge(s_pv, it * STEPS + i - 1)
                    A(pT[i % 2][:, :], X[1][:, :], ACT.Copy).then_inc(s_pT, 1)

                for slot in range(SLOTS):
                    n = slot + 2
                    if n < IN_GROUPS + 2:
                        wait_unit_used(act, it, n)
                        make_hi(it, n % 2, n // 2)
                    bank = slot % 3
                    if slot < IN_GROUPS:
                        act.wait_ge(s_group, it * GROUPS + slot + 1)
                    if slot == 1:
                        A(ivT[:, :], M[bank][:, :], ACT.Copy).then_inc(s_bvT, 1)
                        act.wait_ge(s_vtr, it + 1)
                        act.wait_ge(s_vcar, it + 1)
                        A(vals[:, 1:TB + 1, :], X[1][:, :].rearrange("p (b k) -> p b k", b=TB),
                          ACT.Copy).then_inc(s_vals, 1)
                    elif 2 <= slot < 6:
                        A(qT[slot - 2][:, :], M[bank][:, :], ACT.Copy).then_inc(s_q, 1)
                    elif 6 <= slot < IN_GROUPS:
                        head_group((slot - 6) // 4, (slot - 6) % 4, bank)
                    a = head_at(slot, NORM_MUL)
                    if a is not None:
                        head_mul(a)
                    if slot == SWA_SUM:
                        act.wait_ge(s_ssum, it + 1)
                        A(snrm[:, :], X[1][:, 0:TB], ACT.Sqrt, scale=1.0 / (PAIRS * P),
                          bias=epst[:, 0:1]).then_inc(s_sroot, 1)
                    if slot == SWA_MUL:
                        for p in range(PAIRS):
                            act.wait_ge(s_yb, it * PAIRS + p + 1)
                            A(yhi[:, HEADS + p, :], oT[p][:, :], ACT.Copy).then_inc(s_ybhi, 1)
                    if 0 <= slot - SCORE < STEPS:
                        scores(slot - SCORE)
                    if 0 <= slot - P_TURN < STEPS:
                        p_turn(slot - P_TURN)
                    i = slot - PV
                    if 0 <= i < STEPS and i % TB == TB - 1:
                        p = i // TB
                        act.wait_ge(s_oT, it * PAIRS + p + 1)
                        A(qT[p][:, :], oT[p][:, :], ACT.Square).then_inc(s_osq, 1)
                    for first, step in ((V_TURN, iv_turn), (KEYS, keys), (OUTPUT, output), (NORM_SUM, head_sum)):
                        a = head_at(slot, first)
                        if a is not None:
                            step(a)

                for c in range(CS):
                    n = IN_GROUPS + 2 + c
                    wait_unit_used(act, it, n)
                    make_hi(it, n % 2, n // 2)
                    act.wait_ge(s_h, it * KD + c + 1)
                    if c >= 2:
                        act.wait_ge(s_hacc, it * KD + c - 1)
                    A(sqs[c % 2][:, :], h[:, c, :], ACT.Square).then_inc(s_hsq, 1)
                act.wait_ge(s_nsum, it * 2 + 1)
                act.wait_ge(s_arr, it * HEADS + HEADS)
                A(nrm[:, :], X[0][:, 0:TB], ACT.Sqrt, scale=1.0 / D, bias=epst[:, 0:1]).then_inc(s_root, 1)
                for k in range(KD):
                    act.wait_ge(s_u, it * 2 * KD + KD + k + 1)
                    A(uhi[:, k, :], utmp[k % 2][:, :], ACT.Copy).then_inc(s_uhi, 1)

                with act.Fori(0, KF // 2) as jj:
                    for m in range(4):
                        act.wait_ge(s_group, it * GROUPS + FFN0 + 4 * jj + m + 1)
                        make_hi(it, m % 2, 2 * jj + (FFN0 + 2 + m) // 2)
                        if m % 2 == 0:
                            act.wait_ge(s_alo[m // 2], it * (KF // 2) + jj)
                            A(gu[m // 2][:, :], M[m][:, :], ACT.Silu).then_inc(s_silu[m // 2], 1)

                def down_his(cc, ahead):
                    for m in range(2, ahead):
                        act.wait_ge(s_dpart, it * DPARTS + cc * (2 * ND) + m - 1)
                        make_hi(it, m % 2, cc * ND + DOWN0 // 2 + m // 2, DOWN_PARTS[m % ND])
                with act.Fori(0, CS // 2 - 1) as cc:
                    down_his(cc, 2 * ND + 2)
                down_his(CS // 2 - 1, 2 * ND)

                act.wait_ge(s_nsum, it * 2 + 2)
                act.wait_ge(s_rroot, it * 3 + 2)
                A(nrm[:, :], X[0][:, 0:TB], ACT.Sqrt, scale=1.0 / D, bias=epst[:, 0:1]).then_inc(s_root, 1)
                for b in range(TB):
                    act.wait_ge(s_ftr, it * 2 * TB + 2 * b + 1)
                    act.wait_ge(s_out[b % 2], it * 32 + 16 * (b // 2))
                    A(os_[b % 2][:, 0:D // 2], X[2][:, :], ACT.Copy).then_inc(s_osa, 1)
                    act.wait_ge(s_osa, it * TB + b + 1)
                    act.wait_ge(s_osb, it * TB + b + 1)
                    act.dma_start(out_t[bass.ds(it * TB + b, 1), :, :].rearrange("o p d -> (o p) d"),
                                  os_[b % 2][:, :]).then_inc(s_out[b % 2], 16)
            act.wait_ge(s_out[0], NSB * 32)
            act.wait_ge(s_out[1], NSB * 32)

        @block.vector
        def _(dve):
            V = nc.vector

            dve.wait_ge(s_par, 8 * 16)
            V.tensor_tensor(f_mul[:, :], lbl[:, 0, :], lbl[:, 1, :], ALU.max).then_inc(s_ini2, 1)
            dve.wait_ge(s_ini2, 1)
            for l in range(2):
                V.tensor_tensor(lbs[:, 2 + l, :], lbl[:, l, :], f_mul[:, :], ALU.subtract).then_inc(s_ini2, 1)
            dve.wait_ge(s_ini3, 1)
            V.tensor_tensor(f_add[:, :], lbs[:, 0, :], lbs[:, 1, :], ALU.add).then_inc(s_ini2, 1)
            dve.wait_ge(s_ini2, 4)
            V.reciprocal(f_mul[:, :], f_add[:, :]).then_inc(s_ini2, 1)
            dve.wait_ge(s_ini2, 5)
            V.tensor_tensor(lbs[:, 2, :], lbs[:, 0, :], f_mul[:, :], ALU.mult).then_inc(s_ini2, 1)
            dve.wait_ge(s_ini2, 6)
            V.tensor_scalar(f_mul[:, :], lbs[:, 2, :], -0.5, 0.5, ALU.mult, ALU.add).then_inc(s_ini2, 1)
            V.tensor_scalar(f_add[:, :], lbs[:, 2, :], 0.5, 0.5, ALU.mult, ALU.add).then_inc(s_ini2, 1)
            V.tensor_scalar(ga[:, :], ga[:, :], 0.5, None, ALU.mult).then_inc(s_ini2, 1)
            V.tensor_scalar(nsinks[:, :], sinks[:, :], -1.0, None, ALU.mult).then_inc(s_ini2, 1)
            dve.wait_ge(s_ini, INI - 1)
            V.tensor_copy(causal[:, :].bitcast(I32), causal[:, :]).then_inc(s_ini2, 1)
            dve.wait_ge(s_ini2, 11)
            dve.wait_ge(s_ini, INI)

            def make_lo(it, s, k, nb=8):
                dve.wait_ge(s_hi[s], it * UH + k + 1)
                V.tensor_tensor(wlo[s][:, 0:nb, :], raw[s][:, 0:nb, :], whi[s][:, 0:nb, :].bitcast(F32),
                                ALU.subtract).then_inc(s_lo[s], 1)

            def norm_factor(it, n):
                dve.wait_ge(s_root, it * 3 + n)
                if n == 2:
                    dve.wait_ge(s_amul, it * HEADS + HEADS)
                else:
                    dve.wait_ge(s_nmul, it * 3 + n - 1)
                V.reciprocal(rnrm[:, :], nrm[:, :]).then_inc(s_rroot, 1)

            def make_u(it, k0, g, bank):
                for k in range(KD):
                    if k >= 2:
                        dve.wait_ge(s_ulo, it * 2 * KD + k0 + k - 1)
                    V.scalar_tensor_tensor(out=utmp[k % 2][:, :], in0=h[:, k, :], scalar=g[:, k:k + 1],
                                           in1=bank[:, :], op0=ALU.mult, op1=ALU.mult).then_inc(s_u, 1)
                    if k:
                        u_lo(it, k0, k - 1)
                u_lo(it, k0, KD - 1)

            def u_lo(it, k0, k):
                dve.wait_ge(s_uhi, it * 2 * KD + k0 + k + 1)
                V.tensor_tensor(ulo[:, k, :], utmp[k % 2][:, :], uhi[:, k, :].bitcast(F32),
                                ALU.subtract).then_inc(s_ulo, 1)

            with dve.Fori(0, NSB) as it:
                norm_factor(it, 1)
                for s in range(2):
                    make_lo(it, s, 0)
                dve.wait_ge(s_xT, it * 2 * TB + 2 * TB)
                dve.wait_ge(s_nmul, it * 3 + 1)
                make_u(it, 0, g1, X[2])

                def denominators(i):
                    w = i % 2
                    dve.wait_ge(s_exp, it * STEPS + i + 1)
                    V.tensor_tensor(den[:, :], rs[:, w, :], es[:, :], ALU.add).then_inc(s_den, 1)
                    dve.wait_ge(s_den, it * STEPS + i + 1)
                    dve.wait_ge(s_prob, it * STEPS + i)
                    V.reciprocal(rd[:, :], den[:, :]).then_inc(s_rd, 1)

                def scores(i):
                    p, b = divmod(i, TB)
                    w = i % 2
                    dve.wait_ge(s_score, it * STEPS + i + 1)
                    if i >= 2:
                        dve.wait_ge(s_ptr, it * STEPS + i - 1)
                    if i == 0:
                        dve.wait_ge(s_dist, it)
                    d = dist0 if b == 0 else dist
                    for par in range(2):
                        slope = 2.0 ** -(2 * p + par + 1)
                        half = slice(par * 256, (par + 1) * 256)
                        last = V.scalar_tensor_tensor(out=pr[w][:, half], in0=d[:, :], scalar=8.0 * slope,
                                                      in1=X[0][:, half], op0=ALU.mult, op1=ALU.add)
                    last.then_inc(s_bias, 1)
                    dve.wait_ge(s_bias, it * STEPS + i + 1)
                    V.tensor_reduce(mx[:, :], pr[w][:, :].rearrange("p (h k) -> p h k", h=2), AX_X,
                                    ALU.max).then_inc(s_mx, 1)
                    dve.wait_ge(s_mx, it * STEPS + i + 1)
                    V.scalar_tensor_tensor(out=nm[:, w, :], in0=mx[:, :], scalar=-0.125,
                                           in1=nsinks[:, 2 * p:2 * p + 2], op0=ALU.mult,
                                           op1=ALU.min).then_inc(s_nm, 1)
                    dve.wait_ge(s_nm, it * STEPS + i + 1)
                    V.tensor_tensor(nms[:, :], nm[:, w, :], sinks[:, 2 * p:2 * p + 2], ALU.add).then_inc(s_nms, 1)

                def head_group(a, part, bank):
                    n = it * HEADS + a
                    w = a % 2
                    if part == 0:
                        dve.wait_ge(s_tf, n + 1)
                        V.tensor_scalar(forget[:, :], forget[:, :], f_mul[:, a:a + 1], f_add[:, a:a + 1],
                                        ALU.mult, ALU.add).then_inc(s_f, 1)
                        dve.wait_ge(s_f, n + 1)
                        if a >= 2:
                            dve.wait_ge(s_kst, n - 1)
                        for c in range(NCH):
                            r = slice(c * CHUNK, (c + 1) * CHUNK)
                            last = V.tensor_tensor_scan(cum[w][:, r], forget[:, r], ones[:, :], 1.0, ALU.mult, ALU.mult)
                        last.then_inc(s_cum, 1)
                        dve.wait_ge(s_cum, n + 1)
                        if a:
                            dve.wait_ge(s_key, n)
                        V.reciprocal(cuminv[:, :], cum[w][:, :]).then_inc(s_inv, 1)
                    if part == 1:
                        dve.wait_ge(s_tq, n + 1)
                        V.scalar_tensor_tensor(out=gateq[:, :], in0=gateq[:, :], scalar=1.0, in1=M[bank][:, :],
                                               op0=ALU.add, op1=ALU.mult).then_inc(s_qs, 1)
                        dve.wait_ge(s_qs, n + 1)
                        if a >= 2:
                            dve.wait_ge(s_o, n - 1)
                        V.scalar_tensor_tensor(out=qdec[w][:, :], in0=gateq[:, :], scalar=0.5, in1=cum[w][:, :],
                                               op0=ALU.mult, op1=ALU.mult).then_inc(s_qdec, 1)
                    if part == 3:
                        dve.wait_ge(s_tg, n + 1)
                        V.scalar_tensor_tensor(out=gate[w][:, :], in0=gate[w][:, :], scalar=1.0, in1=M[bank][:, :],
                                               op0=ALU.add, op1=ALU.mult).then_inc(s_gs, 1)

                def keys(a):
                    n = it * HEADS + a
                    dve.wait_ge(s_a, n + 1)
                    if a:
                        dve.wait_ge(s_o, n)
                    V.tensor_tensor(amask[:, :, :].bitcast(I32),
                                    X[2][:, :].rearrange("p (b c) -> p b c", b=TB).bitcast(I32),
                                    causal[:, :].bitcast(I32).rearrange("p (o c) -> p o c", o=1)
                                    .broadcast_to([P, TB, P]), ALU.bitwise_and).then_inc(s_am, 1)

                def update(a):
                    n = it * HEADS + a
                    s0 = it * (NCH * HEADS) + NCH * a
                    dve.wait_ge(s_scar, n if a else it * HEADS)
                    if a:
                        dve.wait_ge(s_o, n)
                    for c in range(NCH):
                        if c % 4 == 0:
                            dve.wait_ge(s_upd, it * 2 * HEADS + 2 * a + c // 4 + 1)
                        before = state[:, a, :] if c == 0 else st[(c - 1) // 4][:, (c - 1) % 4, :]
                        if c:
                            dve.wait_ge(s_st, s0 + c)
                        last_token = (c + 1) * CHUNK - 1
                        V.scalar_tensor_tensor(out=st[c // 4][:, c % 4, :], in0=before,
                                               scalar=cum[a % 2][:, last_token:last_token + 1],
                                               in1=X[2 + c // 4][:, (c % 4) * P:(c % 4 + 1) * P],
                                               op0=ALU.mult, op1=ALU.add).then_inc(s_st, 1)

                def output(a):
                    n = it * HEADS + a
                    dve.wait_ge(s_sq, n + 1)
                    dve.wait_ge(s_gs, n + 1)
                    V.scalar_tensor_tensor(out=gate[a % 2][:, :], in0=X[2][:, :], scalar=ga[:, a:a + 1],
                                           in1=gate[a % 2][:, :], op0=ALU.mult, op1=ALU.mult).then_inc(s_y1, 1)

                def head_sum(a):
                    n = it * HEADS + a
                    dve.wait_ge(s_aroot, n + 1)
                    if a:
                        dve.wait_ge(s_amul, n)
                    V.reciprocal(rnrm[:, :], nrm[:, :]).then_inc(s_arr, 1)

                def head_mul(a):
                    n = it * HEADS + a
                    dve.wait_ge(s_amul, n + 1)
                    dve.wait_ge(s_y1, n + 1)
                    V.tensor_tensor(gate[a % 2][:, :], gate[a % 2][:, :], X[3][:, :], ALU.mult).then_inc(s_ya, 1)
                    dve.wait_ge(s_yahi, n + 1)
                    V.tensor_tensor(ylo[:, a, :], gate[a % 2][:, :], yhi[:, a, :].bitcast(F32),
                                    ALU.subtract).then_inc(s_yalo, 1)

                for slot in range(SLOTS):
                    if 0 <= slot - P_TURN < STEPS:
                        denominators(slot - P_TURN)
                    n = slot + 2
                    if n < IN_GROUPS + 2:
                        wait_unit_used(dve, it, n)
                        make_lo(it, n % 2, n // 2)
                    if slot == 0:
                        dve.wait_ge(s_group, it * GROUPS + 1)
                        dve.wait_ge(s_kcar, it + 1)
                        for g in range(KV):
                            for par in range(2):
                                V.tensor_copy(keyz[64 * par:64 * par + 64, g, par, BLOCK:BLOCK + T],
                                              M[0][64 * g:64 * g + 64, :]).then_inc(s_k, 1)
                    elif 6 <= slot < IN_GROUPS:
                        head_group((slot - 6) // 4, (slot - 6) % 4, slot % 3)
                    a = head_at(slot, NORM_MUL)
                    if a is not None:
                        head_mul(a)
                    if slot == SWA_SUM:
                        dve.wait_ge(s_sroot, it + 1)
                        V.reciprocal(srnrm[:, :], snrm[:, :]).then_inc(s_srr, 1)
                    if slot == SWA_MUL:
                        dve.wait_ge(s_smul, it + 1)
                        for p in range(PAIRS):
                            dve.wait_ge(s_osq, it * PAIRS + p + 1)
                            V.scalar_tensor_tensor(out=oT[p][:, :], in0=oT[p][:, :], scalar=gb[:, p:p + 1],
                                                   in1=X[1][:, :], op0=ALU.mult, op1=ALU.mult).then_inc(s_yb, 1)
                        for p in range(PAIRS):
                            dve.wait_ge(s_ybhi, it * PAIRS + p + 1)
                            V.tensor_tensor(ylo[:, HEADS + p, :], oT[p][:, :], yhi[:, HEADS + p, :].bitcast(F32),
                                            ALU.subtract).then_inc(s_yblo, 1)
                    if 0 <= slot - SCORE < STEPS:
                        scores(slot - SCORE)
                    i = slot - PV
                    if 0 <= i < STEPS and i % TB == TB - 1:
                        dve.wait_ge(s_pv, it * STEPS + i + 1)
                        V.tensor_copy(oT[i // TB][:, :], M[3][:, :]).then_inc(s_oT, 1)
                    for first, step in ((KEYS, keys), (UPDATE, update), (OUTPUT, output), (NORM_SUM, head_sum)):
                        a = head_at(slot, first)
                        if a is not None:
                            step(a)

                for c in range(CS):
                    n = IN_GROUPS + 2 + c
                    wait_unit_used(dve, it, n)
                    make_lo(it, n % 2, n // 2)
                    dve.wait_ge(s_group, it * GROUPS + IN_GROUPS + c + 1)
                    V.tensor_tensor(h[:, c, :], h[:, c, :], M[c % 4][:, :], ALU.add).then_inc(s_h, 1)
                norm_factor(it, 2)
                dve.wait_ge(s_nmul, it * 3 + 2)
                make_u(it, KD, g2, X[0])

                with dve.Fori(0, KF // 2) as jj:
                    for m in range(4):
                        dve.wait_ge(s_group, it * GROUPS + FFN0 + 4 * jj + m + 1)
                        make_lo(it, m % 2, 2 * jj + (FFN0 + 2 + m) // 2)
                        if m % 2:
                            j = m // 2
                            done = it * (KF // 2) + jj + 1
                            dve.wait_ge(s_silu[j], done)
                            V.tensor_tensor(gu[j][:, :], gu[j][:, :], M[m][:, :], ALU.mult).then_inc(s_prod[j], 1)
                            dve.wait_ge(s_prod[j], done)
                            V.tensor_scalar(ahi[:, bass.ds(2 * jj + j, 1), :], gu[j][:, :].rearrange("p (o t) -> p o t", o=1),
                                            1.0, None, ALU.mult).then_inc(s_ahi[j], 1)
                            dve.wait_ge(s_ahi[j], done)
                            V.tensor_tensor(alo[:, bass.ds(2 * jj + j, 1), :], gu[j][:, :].rearrange("p (o t) -> p o t", o=1),
                                            ahi[:, bass.ds(2 * jj + j, 1), :].bitcast(F32),
                                            ALU.subtract).then_inc(s_alo[j], 1)

                def down_part(cc, ahead):
                    for m in range(2, ahead):
                        dve.wait_ge(s_dpart, it * DPARTS + cc * (2 * ND) + m - 1)
                        make_lo(it, m % 2, cc * ND + DOWN0 // 2 + m // 2, DOWN_PARTS[m % ND])
                        if (m - 1) % ND == 0:
                            add_block(cc, (m - 1) // ND - 1)
                    if ahead == 2 * ND:
                        add_block(cc, 1)

                def add_block(cc, half):
                    dve.wait_ge(s_dpart, it * DPARTS + cc * (2 * ND) + (half + 1) * ND)
                    c = cc * 2 + half
                    hc = h[:, bass.ds(c, 1), :]
                    V.tensor_tensor(hc, hc, M[half][:, :].rearrange("p (o t) -> p o t", o=1),
                                    ALU.add).then_inc(s_h2[half], 1)
                    dve.wait_ge(s_h2[half], it * (KD // 2) + cc + 1)
                    dve.wait_ge(s_h2acc[half], it * (KD // 2) + cc)
                    V.tensor_tensor(sqs[half][:, :].rearrange("p (o t) -> p o t", o=1), hc, hc,
                                    ALU.mult).then_inc(s_h2sq[half], 1)
                with dve.Fori(0, CS // 2 - 1) as cc:
                    down_part(cc, 2 * ND + 2)
                down_part(CS // 2 - 1, 2 * ND)

                norm_factor(it, 3)
                dve.wait_ge(s_nmul, it * 3 + 3)
                for k in range(KD):
                    V.scalar_tensor_tensor(out=h[:, k, :], in0=h[:, k, :], scalar=gf[:, k:k + 1],
                                           in1=X[0][:, :], op0=ALU.mult, op1=ALU.mult).then_inc(s_fin, 1)
                for b in range(TB):
                    dve.wait_ge(s_ftr, it * 2 * TB + 2 * b + 2)
                    dve.wait_ge(s_out[b % 2], it * 32 + 16 * (b // 2))
                    V.tensor_copy(os_[b % 2][:, D // 2:D], X[3][:, :]).then_inc(s_osb, 1)

        @block.gpsimd
        def _(pool):
            G = nc.gpsimd
            G.memset(ident[:, :], 0.0).then_inc(s_ini, 1)
            G.memset(ones[:, :], 1.0).then_inc(s_ini, 1)
            G.memset(epst[:, :], EPS).then_inc(s_ini, 1)
            G.memset(keyz[:, :, :, :], 0.0).then_inc(s_ini, 1)
            G.memset(vals[:, :, :], 0.0).then_inc(s_ini, 1)
            G.memset(kstz[:, :, :, :], 0.0).then_inc(s_ini, 1)
            G.memset(state[:, :, :], 0.0).then_inc(s_ini, 1)
            G.memset(causal[:, :], -1.0).then_inc(s_ini, 1)
            G.iota(dist[:, :].bitcast(I32), [[1, 2 * BLOCK]], base=-BLOCK, channel_multiplier=-1).then_inc(s_ini, 1)
            pool.wait_ge(s_ini, 9)
            G.affine_select(out=ident[:, :], in_=ident[:, :], compare_op=ALU.not_equal, fill=1.0, base=0,
                            pattern=[[-1, P]], channel_multiplier=1).then_inc(s_ini, 1)
            G.affine_select(out=causal[:, :], in_=causal[:, :], compare_op=ALU.is_ge, fill=0.0, base=0,
                            pattern=[[1, P]], channel_multiplier=-1).then_inc(s_ini, 1)
            G.tensor_copy(dist0[:, :], dist[:, :].bitcast(I32)).then_inc(s_ini, 1)
            pool.wait_ge(s_ini, 12)
            G.memset(causal[0:CHUNK, CHUNK:P], 0.0).then_inc(s_ini, 1)
            G.affine_select(out=dist0[:, :], in_=dist0[:, :], compare_op=ALU.is_ge, fill=MASKED, base=BLOCK,
                            pattern=[[-1, 2 * BLOCK]], channel_multiplier=1).then_inc(s_dst, 1)
            pool.wait_ge(s_dst, 1)
            G.affine_select(out=dist[:, :], in_=dist0[:, :], compare_op=ALU.is_ge, fill=MASKED, base=-1,
                            pattern=[[1, 2 * BLOCK]], channel_multiplier=-1).then_inc(s_dst, 1)
            pool.wait_ge(s_dst, 2)
            G.tensor_copy(dist0[:, BLOCK:2 * BLOCK], dist[:, BLOCK:2 * BLOCK]).then_inc(s_dst, 1)
            G.memset(dist0[:, 0:BLOCK], MASKED).then_inc(s_dst, 1)
            pool.wait_ge(s_dst, 4)
            pool.wait_ge(s_ini, 13)
            G.memset(zero[:, :], 0.0).then_inc(s_ini, 1)

            def copy(out, in_):
                return G.tensor_tensor(out, in_, ones[:, 0:1].broadcast_to(list(in_.shape)), ALU.mult)

            keys_all = keyz[:, :, :, :].rearrange("p g r t -> p (g r) t")
            with pool.Fori(0, NSB) as it:
                pool.wait_ge(s_score, it * STEPS)
                copy(keys_all[:, :, 0:BLOCK], keys_all[:, :, T:T + BLOCK]).then_inc(s_kcar, 1)
                pool.wait_ge(s_pv, it * STEPS)
                copy(vals[:, 0, :], vals[:, TB, :]).then_inc(s_vcar, 1)

                def key_steps(a):
                    n = it * HEADS + a
                    pool.wait_ge(s_f, n + 1)
                    if a:
                        pool.wait_ge(s_a, n)
                    G.tensor_tensor(key[:, :], ones[:, 0:1].broadcast_to([P, T]), forget[:, :],
                                    ALU.subtract).then_inc(s_key0, 1)
                    pool.wait_ge(s_key0, n + 1)
                    pool.wait_ge(s_inv, n + 1)
                    G.tensor_tensor(key[:, :], key[:, :], cuminv[:, :], ALU.mult).then_inc(s_key, 1)
                    pool.wait_ge(s_key, n + 1)
                    if a:
                        pool.wait_ge(s_ktr, n)
                    ends = cum[a % 2][:, :].rearrange("p (c t) -> p c t", c=NCH)[:, :, CHUNK - 1:CHUNK]
                    G.tensor_tensor(kstate[:, :].rearrange("p (c t) -> p c t", c=NCH),
                                    key[:, :].rearrange("p (c t) -> p c t", c=NCH),
                                    ends.broadcast_to([P, NCH, CHUNK]), ALU.mult).then_inc(s_kst, 1)

                for slot in range(SLOTS):
                    i = slot - P_TURN
                    if 0 <= i < STEPS:
                        pool.wait_ge(s_rd, it * STEPS + i + 1)
                        halves = pr[i % 2][:, :].rearrange("p (h k) -> p h k", h=2)
                        G.tensor_tensor(halves, halves, rd[:, :].rearrange("p (h o) -> p h o", o=1)
                                        .broadcast_to([P, 2, 2 * BLOCK]), ALU.mult).then_inc(s_prob, 1)
                        if i == (PAIRS - 1) * TB + 1:
                            pool.wait_ge(s_bias, it * STEPS + i)
                            copy(dist0[:, :], dist[:, :]).then_inc(s_dist, 1)
                    if 6 <= slot < IN_GROUPS and (slot - 6) % 4 == 0:
                        key_steps((slot - 6) // 4)
                    a = head_at(slot, OUTPUT)
                    if a is not None:
                        n = it * HEADS + a
                        pool.wait_ge(s_o, n + 1)
                        pool.wait_ge(s_st, it * (NCH * HEADS) + NCH * (a + 1))
                        copy(state[:, a, :], st[1][:, 3, :]).then_inc(s_scar, 1)

                acc = sacc[:, 0:T]
                for c in range(KD):
                    pool.wait_ge(s_hsq, it * KD + c + 1)
                    if c == 0:
                        pool.wait_ge(s_out[0], it * 32)
                        copy(acc, sqs[0][:, :]).then_inc(s_hacc, 1)
                    else:
                        pool.wait_ge(s_hacc, it * KD + c)
                        G.tensor_tensor(acc, acc, sqs[c % 2][:, :], ALU.add).then_inc(s_hacc, 1)
                for c in range(KD):
                    pool.wait_ge(s_h2sq[c % 2], it * (KD // 2) + c // 2 + 1)
                    if c == 0:
                        pool.wait_ge(s_nsum, it * 2 + 1)
                        copy(acc, sqs[0][:, :]).then_inc(s_h2acc[0], 1)
                    else:
                        pool.wait_ge(s_h2acc[(c - 1) % 2], it * (KD // 2) + (c - 1) // 2 + 1)
                        G.tensor_tensor(acc, acc, sqs[c % 2][:, :], ALU.add).then_inc(s_h2acc[c % 2], 1)


_INS = ['x', 'ln1_g', 'w_in', 'lb_logits', 'hgrn_norm_g', 'attn_sinks', 'attn_norm_g', 'w_out', 'ln2_g', 'w_gate',
        'w_up', 'w_down', 'final_g']


def kernel(**inputs):
    import numpy as _np
    import concourse.bacc as _bacc
    from concourse import mybir as _mybir
    from concourse.bass_utils import run_bass_kernel_spmd as _run

    nc = _bacc.Bacc("TRN2", target_bir_lowering=False, num_devices=1)
    arrays, args = {}, []
    for name in _INS:
        a = _np.ascontiguousarray(inputs[name])
        arrays[f"in_{name}_dram"] = a
        args.append(nc.dram_tensor(f"in_{name}_dram", a.shape, _mybir.dt.from_np(a.dtype), kind="ExternalInput").ap())
    shape = inputs["x"].shape
    args.append(nc.dram_tensor("out_0_dram", shape, _mybir.dt.float32, kind="ExternalOutput").ap())
    block_program(nc, *args)
    r = _run(nc, [arrays], core_ids=[0])
    return r.results[0]["out_0_dram"]
```

```python
from contextlib import ExitStack

import concourse.bass as bass
from concourse import mybir

F32 = mybir.dt.float32
F32R = mybir.dt.float32r
I32 = mybir.dt.int32
ALU = mybir.AluOpType
ACT = mybir.ActivationFunctionType
AX_X = mybir.AxisListType.X

P = 128
T = 512
TB = T // P
CHUNK = 64
NCH = T // CHUNK
HEADS = 4
KV = 2
PAIRS = 4
BLOCK = 128
EPS = 1e-6
MASKED = -1e30
STEPS = PAIRS * TB

IN_GROUPS = 22
Q_SLOT = (2, 3, 8, 13)
F_SLOT = (4, 9, 14, 18)
SPLIT = 7
OUT_A = 22
A_UNITS = 4
A_KS = ((0, 1), (4, 5), (6, 7), (2, 3))
XT_SLOT = 19
SLOTS = 27
SCORE, P_TURN, PV = 3, 4, 5
SWA_SUM, SWA_MUL = 21, 22
V_TURN, KEYS, UPDATE, OUTPUT, NORM_SUM, NORM_MUL = 3, 3, 4, 5, 6, 7
PREP_PART = 3
FINAL_SUM, FINAL_SPREAD, FINAL_SCALE, FINAL_TURN = 0, 1, 1, 3


def column_of(slot):
    if slot == 0:
        return 2560
    if slot == 1:
        return 2688
    if slot in Q_SLOT:
        return 2048 + P * Q_SLOT.index(slot)
    a, part = head_part(slot)
    return (512, 0, 1024, 1536)[part] + P * a


def head_part(slot):
    for a, first in enumerate(F_SLOT):
        if 0 <= slot - first < 4:
            return a, slot - first
    return None, None


def head_at(slot, offset):
    return F_SLOT.index(slot - offset) if slot - offset in F_SLOT else None


def step_at(slot, first):
    return slot - first if 0 <= slot - first < STEPS else None


def is_first(n):
    return isinstance(n, int) and n == 0


def block_program(nc, x, ln1_g, w_in, lb_logits, hgrn_norm_g, attn_sinks, attn_norm_g, w_out, ln2_g,
                  w_gate, w_up, w_down, final_g, out):
    S, D = x.shape[1], x.shape[2]
    FF = w_gate.shape[2]
    NSB = S // T
    KD = D // P
    KF = FF // P
    CS = D // P
    assert S % T == 0 and KD == 8 and KF % 2 == 0 and TB == CS // 2

    DOWN_PARTS = [min(8, KF - k) for k in range(0, KF, 8)]
    ND = len(DOWN_PARTS)
    OUT_B = OUT_A + A_UNITS
    FFN0 = OUT_B + CS - 4
    DOWN0 = FFN0 + 2 * KF
    UNITS = DOWN0 + CS * ND
    assert DOWN_PARTS[1] == 8
    assert UNITS % 2 == 0 and DOWN0 % 2 == 0 and FFN0 % 2 == 0 and (2 * ND) % 2 == 0
    UH = UNITS // 2
    GROUPS = DOWN0
    DPARTS = CS * ND

    x_t = x.rearrange("o (n p) d -> (o n) p d", p=P)
    x_half = x.rearrange("o (n p) (h d) -> (o n) h p d", p=P, h=2)
    out_t = out.rearrange("o (n p) d -> (o n) p d", p=P)
    w_in_k = w_in.rearrange("o (k p) n -> (o p) k n", p=P)
    w_out_k = w_out.rearrange("o (k p) n -> (o p) k n", p=P)
    w_gate_k = w_gate.rearrange("o (k p) n -> (o p) k n", p=P)
    w_up_k = w_up.rearrange("o (k p) n -> (o p) k n", p=P)
    w_down_k = w_down.rearrange("o (k p) n -> (o p) k n", p=P)

    with ExitStack() as ctx:
        def sb(name, shape, dt=F32):
            return ctx.enter_context(nc.sbuf_tensor(name, shape, dt))

        def sem(name):
            return ctx.enter_context(nc.semaphore(name))

        def sems(name, n):
            return [sem(f"{name}{i}") for i in range(n)]

        h = sb("h", [P, KD, T])
        uhi = sb("uhi", [P, KD, T], F32R)
        ulo = sb("ulo", [P, KD, T], F32R)
        raw = [sb(f"raw{i}", [P, 8, P]) for i in range(2)]
        whi = [sb(f"whi{i}", [P, 8, P], F32R) for i in range(2)]
        wlo = [sb(f"wlo{i}", [P, 8, P], F32R) for i in range(2)]
        xs = [sb(f"xs{i}", [P, D]) for i in range(2)]
        os_ = [sb(f"os{i}", [P, D]) for i in range(2)]
        keyz = sb("keyz", [P, KV, 2, T + BLOCK])
        vals = sb("vals", [P, TB + 1, KV * 64])
        kstz = sb("kstz", [P, TB, 2, P])
        g1row = sb("g1row", [P, D])
        state = sb("state", [P, HEADS, P])
        gu = [sb(f"gu{i}", [P, T]) for i in range(2)]
        dist = sb("dist", [P, 2 * BLOCK])
        dist0 = sb("dist0", [P, 2 * BLOCK])
        ident = sb("ident", [P, P])
        ones = sb("ones", [P, CHUNK])
        causal = sb("causal", [P, P])
        g2 = sb("g2", [P, KD]); gf = sb("gf", [P, KD])
        ga = sb("ga", [P, HEADS]); gb = sb("gb", [P, PAIRS])
        lbl = sb("lbl", [P, 2, HEADS]); lbs = sb("lbs", [P, 4, HEADS])
        f_mul = sb("f_mul", [P, HEADS]); f_add = sb("f_add", [P, HEADS])
        sinks = sb("sinks", [P, 8]); nsinks = sb("nsinks", [P, 8])
        epst = sb("epst", [P, 1])
        zero = sb("zero", [P, 1])
        xss = sb("xss", [P, 1]); xnrm = sb("xnrm", [P, 1]); xrn = sb("xrn", [P, 1])
        nrm = sb("nrm", [P, TB]); rnrm = sb("rnrm", [P, TB])
        hnrm = sb("hnrm", [P, TB]); hrnrm = sb("hrnrm", [P, TB])
        snrm = sb("snrm", [P, TB]); srnrm = sb("srnrm", [P, TB])
        mx = sb("mx", [P, 2]); nm = sb("nm", [P, 2, 2]); nms = sb("nms", [P, 2])
        es = sb("es", [P, 2]); rs = sb("rs", [P, 2, 2]); den = sb("den", [P, 2]); rd = sb("rd", [P, 2])

        act_at = nc.sbuf_base
        act_at = (act_at + 31) // 32 * 32
        ctx.enter_context(nc.sbuf_tensor("arena", [P, 2 * KF, T], F32))
        ahi = nc.alloc_sbuf_tensor_at("ahi", [P, KF, T], F32R, offset=act_at)
        alo = nc.alloc_sbuf_tensor_at("alo", [P, KF, T], F32R, offset=act_at + KF * T * 4)
        yhi, ylo = ahi, alo
        free_tiles = [act_at + 4 * T * k for k in list(range(KD, KF)) + list(range(KF + KD, 2 * KF))]
        if len(free_tiles) < 28:
            extra = ctx.enter_context(nc.sbuf_tensor("extra", [P, 28 - len(free_tiles), T], F32))
            base = nc.sbuf_base - 4 * T * (28 - len(free_tiles))
            free_tiles += [base + 4 * T * k for k in range(28 - len(free_tiles))]

        def tile(name, shape=(P, T)):
            return nc.alloc_sbuf_tensor_at(name, list(shape), F32, offset=free_tiles.pop(0))

        forget, key, cuminv, gateq, ivT, iv, sqo = (
            tile(n) for n in ("forget", "key", "cuminv", "gateq", "ivT", "iv", "sqo"))
        kstate = forget
        amask = tile("amask", (P, TB, P))
        cum = [tile(f"cum{i}") for i in range(2)]
        qdec = [tile(f"qdec{i}") for i in range(2)]
        gate = [tile(f"gate{i}") for i in range(2)]
        qT = [tile(f"qT{i}") for i in range(PAIRS)]
        pr = [tile(f"pr{i}") for i in range(2)]
        pT = [tile(f"pT{i}") for i in range(2)]
        oT = [tile(f"oT{i}") for i in range(PAIRS)]
        st = [tile(f"st{i}", (P, 4, P)) for i in range(2)]
        xdump = os_[1]
        xh = [xs[q // 2][:, (q % 2) * (D // 2):(q % 2 + 1) * (D // 2)] for q in range(4)]
        upn = xs[1][:, 0:T]
        sqs = gu
        factors = os_[1][:, 0:T]
        sacc = os_[0]
        M = [ctx.enter_context(nc.psum_tensor(f"M{i}", [P, T], F32)) for i in range(4)]
        X = [ctx.enter_context(nc.psum_tensor(f"X{i}", [P, T], F32)) for i in range(4)]

        s_par = sem("s_par")
        s_ini = sem("s_ini")
        s_ini2 = sem("s_ini2")
        s_ini3 = sem("s_ini3")
        s_dst = sem("s_dst")
        s_g1 = sem("s_g1")
        s_raw = sems("s_raw", 2)
        s_x = sem("s_x")
        s_out = sems("s_out", 2)
        s_hi = sems("s_hi", 2)
        s_lo = sems("s_lo", 2)
        s_group = sem("s_group")
        s_dpart = sem("s_dpart")

        s_xss = sem("s_xss")
        s_xroot = sem("s_xroot")
        s_xr = sem("s_xr")
        s_xn = sem("s_xn")
        s_ptr0 = sem("s_ptr0")
        s_xh = sems("s_xh", 4)
        s_xtr = sem("s_xtr")
        s_xT = sem("s_xT")
        s_nsum = sem("s_nsum")
        s_root = sem("s_root")
        s_rroot = sem("s_rroot")
        s_fac = sem("s_fac")
        s_nmul = sem("s_nmul")
        s_xuhi = sem("s_xuhi")
        s_xulo = sem("s_xulo")
        s_uhi = sem("s_uhi")
        s_ulo = sem("s_ulo")
        s_kcar = sem("s_kcar")
        s_vcar = sem("s_vcar")
        s_k = sem("s_k")
        s_bvT = sem("s_bvT")
        s_vtr = sem("s_vtr")
        s_vals = sem("s_vals")
        s_q = sem("s_q")
        s_score = sem("s_score")
        s_bias = sem("s_bias")
        s_mx = sem("s_mx")
        s_nm = sem("s_nm")
        s_nms = sem("s_nms")
        s_exp = sem("s_exp")
        s_den = sem("s_den")
        s_rd = sem("s_rd")
        s_prob = sem("s_prob")
        s_ptr = sem("s_ptr")
        s_pT = sem("s_pT")
        s_pv = sem("s_pv")
        s_oT = sem("s_oT")
        s_osq = sem("s_osq")
        s_ssum = sem("s_ssum")
        s_sroot = sem("s_sroot")
        s_srr = sem("s_srr")
        s_smul = sem("s_smul")
        s_yb = sem("s_yb")
        s_ybhi = sem("s_ybhi")
        s_yblo = sem("s_yblo")
        s_dist = sem("s_dist")
        s_tf = sem("s_tf")
        s_tq = sem("s_tq")
        s_iv = sem("s_iv")
        s_tg = sem("s_tg")
        s_f = sem("s_f")
        s_cum = sem("s_cum")
        s_inv = sem("s_inv")
        s_key0 = sem("s_key0")
        s_key = sem("s_key")
        s_kst = sem("s_kst")
        s_qs = sem("s_qs")
        s_qdec = sem("s_qdec")
        s_gs = sem("s_gs")
        s_ivtr = sem("s_ivtr")
        s_ivt = sem("s_ivt")
        s_ktr = sem("s_ktr")
        s_kz = sem("s_kz")
        s_a = sem("s_a")
        s_am = sem("s_am")
        s_upd = sem("s_upd")
        s_st = sem("s_st")
        s_scar = sem("s_scar")
        s_o = sem("s_o")
        s_sq = sem("s_sq")
        s_y1 = sem("s_y1")
        s_asum = sem("s_asum")
        s_aroot = sem("s_aroot")
        s_arr = sem("s_arr")
        s_amul = sem("s_amul")
        s_ya = sem("s_ya")
        s_yahi = sem("s_yahi")
        s_yalo = sem("s_yalo")
        s_h = sem("s_h")
        s_hsq = sem("s_hsq")
        s_hacc = sem("s_hacc")
        s_gate = sems("s_gate", 2)
        s_up = sems("s_up", 2)
        s_silu = sems("s_silu", 2)
        s_prod = sems("s_prod", 2)
        s_ahi = sems("s_ahi", 2)
        s_alo = sems("s_alo", 2)
        s_h2 = sems("s_h2", 2)
        s_h2sq = sems("s_h2sq", 2)
        s_h2acc = sems("s_h2acc", 2)
        s_fin = sem("s_fin")
        s_ftr = sem("s_ftr")
        s_osa = sem("s_osa")
        s_osb = sem("s_osb")
        INI = 14

        block = ctx.enter_context(nc.Block())

        def wait_group_read(eng, it, slot):
            a, part = head_part(slot)
            if slot == 0:
                eng.wait_ge(s_k, it * 4 + 4)
            elif slot == 1:
                eng.wait_ge(s_bvT, it + 1)
            elif slot in Q_SLOT:
                eng.wait_ge(s_q, it * PAIRS + Q_SLOT.index(slot) + 1)
            else:
                eng.wait_ge((s_tf, s_qs, s_iv, s_gs)[part], it * HEADS + a + 1)

        def wait_unit_used(eng, it, n):
            eng.wait_ge(s_group, it * GROUPS + n - 1)

        def over_superblocks(eng, prologue, body):
            prologue()
            if NSB > 1:
                with eng.Fori(0, NSB - 1) as it:
                    body(it, False)
            body(NSB - 1, True)

        @block.sync
        def _(sp):
            sp.dma_start(g1row[:, :], ln1_g[0, :].partition_broadcast(P)).then_inc(s_g1, 16)

            def load(it, s, k, src, nb=8, dst=None):
                if not is_first(it * UH + k):
                    sp.wait_ge(s_lo[s], it * UH + k)
                sp.dma_start(raw[s][:, 0:nb, :] if dst is None else dst, src).then_inc(s_raw[s], 16)

            def load_x(it, b):
                sp.wait_ge(s_xn, it * TB + b + 1)
                sp.dma_start(xs[0][:, :], x_t[bass.ds(it * TB + b, 1), :, :].rearrange("o p d -> (o p) d")
                             ).then_inc(s_x, 16)

            def load_half(it, half, b):
                if half:
                    sp.wait_ge(s_xtr, it * 2 * TB + b + 1)
                else:
                    sp.wait_ge(s_ptr0, it * 2 * TB + 2 * TB)
                sp.dma_start(xh[b], x_half[bass.ds(it * TB + b, 1), half:half + 1, :, :].rearrange("o h p d -> (o h p) d")
                             ).then_inc(s_xh[b], 16)

            def load_in(it, units):
                for n in units:
                    load(it, n % 2, n // 2, w_in_k[:, :, column_of(n):column_of(n) + P])

            load_x(0, 0)
            load_in(0, (0,))
            for dst, src in ((g2, ln2_g), (ga, hgrn_norm_g), (gb, attn_norm_g)):
                sp.dma_start(dst[:, :], src.rearrange("o (k p) -> p (o k)", p=P),
                             allow_slow_non_contiguous=True).then_inc(s_par, 16)
            sp.dma_start(gf[:, :], final_g.rearrange("(k p) -> p k", p=P),
                         allow_slow_non_contiguous=True).then_inc(s_par, 16)
            for l in range(2):
                sp.dma_start(lbl[:, l, :], lb_logits[l, :].rearrange("(k p) -> p k", p=P),
                             allow_slow_non_contiguous=True).then_inc(s_par, 16)
            sp.dma_start(sinks[:, :], attn_sinks[0, :].partition_broadcast(P)).then_inc(s_par, 16)

            def prologue():
                load_in(0, (1,))
                for b in range(1, TB):
                    load_x(0, b)
                load_in(0, range(2, SPLIT + 2))

            def body(it, final):
                for n in range(SPLIT + 2, IN_GROUPS):
                    load_in(it, (n,))
                    if n >= IN_GROUPS - TB:
                        load_half(it, 0, n - (IN_GROUPS - TB))
                for n in range(OUT_A, OUT_B):
                    k0 = A_KS[n - OUT_A][0]
                    load(it, n % 2, n // 2, w_out_k[:, k0:k0 + 2, 0:4 * P],
                         dst=raw[n % 2][:, :, :].rearrange("p (k c) n -> p k (c n)", k=2))
                for c in range(4, CS):
                    n = OUT_B + c - 4
                    load_half(it, 1, c - 4)
                    load(it, n % 2, n // 2, w_out_k[:, :, c * P:(c + 1) * P])
                with sp.Fori(0, KF) as j:
                    load(it, 0, j + FFN0 // 2, w_gate_k[:, :, bass.ds(j * P, P)])
                    load(it, 1, j + FFN0 // 2, w_up_k[:, :, bass.ds(j * P, P)])
                with sp.Fori(0, CS // 2) as cc:
                    if not final:
                        sp.wait_ge(s_xtr, it * 2 * TB + 2 * TB)
                        load_x(it + 1, cc)
                    for m in range(2 * ND):
                        half, part = divmod(m, ND)
                        k0, nb = 8 * part, DOWN_PARTS[part]
                        load(it, m % 2, cc * ND + DOWN0 // 2 + m // 2,
                             w_down_k[:, k0:k0 + nb, bass.ds(cc * 2 * P + half * P, P)], nb)
                if not final:
                    load_in(it + 1, range(SPLIT + 2))

            over_superblocks(sp, prologue, body)

        @block.tensor
        def _(pe):
            mm, tr = nc.tensor.matmul, nc.tensor.transpose

            def product(bank, s, hi, lo, kb, first, last):
                mm(bank, whi[s][:, kb, :], hi, start=first, stop=False)
                mm(bank, whi[s][:, kb, :], lo, start=False, stop=False)
                return mm(bank, wlo[s][:, kb, :], hi, start=False, stop=last)

            def spread(bank, factors, done):
                for b in range(TB):
                    last = mm(bank[:, b * P:(b + 1) * P], factors[:, b:b + 1].broadcast_to([P, P]), ident[:, :],
                              start=True, stop=True)
                last.then_inc(done, 1)

            def sums(bank, squares, done):
                for b in range(TB):
                    for n, sq in enumerate(squares):
                        last = mm(bank[:, b:b + 1], sq[:, b * P:(b + 1) * P], ones[:, 0:1],
                                  start=(n == 0), stop=(n == len(squares) - 1))
                last.then_inc(done, 1)

            def prep(it, b):
                pe.wait_ge(s_xn, it * TB + b + 2)
                for half in range(2):
                    if not is_first(it * 2 * TB + 2 * b):
                        pe.wait_ge(s_xulo, it * 2 * TB + 2 * b - 1 + half)
                    for c in range(4):
                        k = 4 * half + c
                        last = tr(X[2 + half][:, c * P:(c + 1) * P], xs[1][:, k * P:(k + 1) * P], ident[:, :])
                    last.then_inc(s_ptr0, 1)

            def group(it, slot):
                if slot >= 3:
                    wait_group_read(pe, it, slot - 3)
                elif slot < 2:
                    pe.wait_ge(s_h2[slot], it * (KD // 2) + 1)
                pe.wait_ge(s_lo[slot % 2], it * UH + slot // 2 + 1)
                if slot == 0:
                    pe.wait_ge(s_xulo, it * 2 * TB + 2 * TB)
                for k in range(KD):
                    last = product(M[slot % 3][:, :], slot % 2, uhi[:, k, :], ulo[:, k, :], k,
                                   k == 0, k == KD - 1)
                last.then_inc(s_group, 1)

            def out_a(it, n, kks):
                unit = OUT_A + n
                for kk in kks:
                    k = A_KS[n][kk]
                    if k < HEADS:
                        pe.wait_ge(s_yalo, it * HEADS + k + 1)
                    else:
                        pe.wait_ge(s_yblo, it * PAIRS + k - HEADS + 1)
                    for c in range(4):
                        last = product(M[c][:, :], unit % 2, yhi[:, k, :], ylo[:, k, :], 4 * kk + c,
                                       n == 0 and kk == 0, n == A_UNITS - 1 and kk == 1)
                if kks[-1] == 1:
                    last.then_inc(s_group, 1)

            def v_values(it):
                pe.wait_ge(s_bvT, it + 1)
                for b in range(TB):
                    last = tr(X[1][:, b * P:(b + 1) * P], ivT[:, b * P:(b + 1) * P], ident[:, :])
                last.then_inc(s_vtr, 1)

            def scores(it, i):
                p, b = divmod(i, TB)
                if i == 0:
                    pe.wait_ge(s_k, it * 4 + 4)
                if b == 0:
                    pe.wait_ge(s_q, it * PAIRS + p + 1)
                if i:
                    pe.wait_ge(s_bias, it * STEPS + i)
                for par in range(2):
                    last = mm(X[0][:, par * 2 * BLOCK:(par + 1) * 2 * BLOCK], qT[p][:, b * P:(b + 1) * P],
                              keyz[:, p // 2, par, b * P:b * P + 2 * BLOCK], start=True, stop=True)
                last.then_inc(s_score, 1)

            def p_turn(it, i):
                pe.wait_ge(s_prob, it * STEPS + i + 1)
                if i:
                    pe.wait_ge(s_pT, it * STEPS + i)
                else:
                    pe.wait_ge(s_vals, it + 1)
                for n in range(4):
                    last = tr(X[1][:, n * P:(n + 1) * P], pr[i % 2][:, n * P:(n + 1) * P], ident[:, :])
                last.then_inc(s_ptr, 1)

            def pv(it, i):
                p, b = divmod(i, TB)
                g = p // 2
                pe.wait_ge(s_pT, it * STEPS + i + 1)
                if b == 0 and p:
                    pe.wait_ge(s_oT, it * PAIRS + p)
                for par in range(2):
                    for kb in range(2):
                        last = mm(M[3][64 * par:64 * par + 64, b * P:(b + 1) * P],
                                  vals[:, b + kb, 64 * g:64 * g + 64],
                                  pT[i % 2][:, (2 * par + kb) * P:(2 * par + kb + 1) * P],
                                  start=(kb == 0), stop=(kb == 1))
                last.then_inc(s_pv, 1)

            def iv_turn(it, a):
                pe.wait_ge(s_iv, it * HEADS + a + 1)
                if a:
                    pe.wait_ge(s_ya, it * HEADS + a)
                else:
                    pe.wait_ge(s_osb, it * TB + 1)
                for b in range(TB):
                    last = tr(X[3][:, b * P:(b + 1) * P], ivT[:, b * P:(b + 1) * P], ident[:, :])
                last.then_inc(s_ivtr, 1)

            def keys(it, a):
                pe.wait_ge(s_key, it * HEADS + a + 1)
                pe.wait_ge(s_qdec, it * HEADS + a + 1)
                if a:
                    pe.wait_ge(s_y1, it * HEADS + a)
                else:
                    pe.wait_ge(s_osa, it * TB + 1)
                for b in range(TB):
                    last = mm(X[2][:, b * P:(b + 1) * P], key[:, b * P:(b + 1) * P],
                              qdec[a % 2][:, b * P:(b + 1) * P], start=True, stop=True)
                last.then_inc(s_a, 1)

            def key_turn(it, a):
                pe.wait_ge(s_kst, it * HEADS + a + 1)
                pe.wait_ge(s_ivt, it * HEADS + a + 1)
                for b in range(TB):
                    last = tr(X[3][:, b * P:(b + 1) * P], kstate[:, b * P:(b + 1) * P], ident[:, :])
                last.then_inc(s_ktr, 1)

            def update(it, a):
                pe.wait_ge(s_kz, it * 2 * HEADS + 2 * a + 2)
                pe.wait_ge(s_am, it * HEADS + a + 1)
                for half in range(2):
                    for n in range(4):
                        b, c = divmod(4 * half + n, 2)
                        last = mm(X[2 + half][:, n * P:(n + 1) * P], kstz[:, b, c, :], iv[:, b * P:(b + 1) * P],
                                  start=True, stop=True)
                    last.then_inc(s_upd, 1)

            def output(it, a):
                pe.wait_ge(s_st, it * NCH * HEADS + NCH * a + 4)
                for b in range(TB):
                    mm(X[2][:, b * P:(b + 1) * P], iv[:, b * P:(b + 1) * P], amask[:, b, :],
                       start=(b == 0), stop=False, skip_group_check=True)
                for n in range(NCH):
                    if n > 4:
                        pe.wait_ge(s_st, it * NCH * HEADS + NCH * a + n)
                    before = state[:, a, :] if n == 0 else st[(n - 1) // 4][:, (n - 1) % 4, :]
                    last = mm(X[2][:, n * CHUNK:(n + 1) * CHUNK], before,
                              qdec[a % 2][:, n * CHUNK:(n + 1) * CHUNK],
                              start=False, stop=(n == NCH - 1), skip_group_check=True)
                last.then_inc(s_o, 1)

            def head_sum(it, a):
                pe.wait_ge(s_sq, it * HEADS + a + 1)
                pe.wait_ge(s_st, it * NCH * HEADS + NCH * a + NCH)
                sums(X[3], [sqo], s_asum)

            def head_mul(it, a):
                pe.wait_ge(s_arr, it * HEADS + a + 1)
                spread(X[3], hrnrm, s_amul)

            def x_turn(it, j):
                half, b = divmod(j, TB)
                pe.wait_ge(s_xh[b], it * 32 + 16 * half + 16)
                if j:
                    pe.wait_ge(s_xT, it * 2 * TB + j)
                else:
                    pe.wait_ge(s_bias, it * STEPS + STEPS)
                for c in range(4):
                    last = tr(X[0][:, c * P:(c + 1) * P], xh[b][:, c * P:(c + 1) * P], ident[:, :])
                last.then_inc(s_xtr, 1)

            def final_sum(it):
                for half in range(2):
                    pe.wait_ge(s_h2acc[half], it * (KD // 2) + KD // 2 + 1)
                sums(X[2], [sacc], s_nsum)

            def final_spread(it):
                pe.wait_ge(s_rroot, it * 2 + 2)
                spread(X[3], rnrm, s_nmul)

            def final_turn(it, b):
                pe.wait_ge(s_fin, it * KD + KD)
                for half in range(2):
                    if b:
                        pe.wait_ge((s_osa, s_osb)[half], it * TB + b + 1)
                    for c in range(4):
                        last = tr(X[2 + half][:, c * P:(c + 1) * P], h[:, 4 * half + c, b * P:(b + 1) * P],
                                  ident[:, :])
                    last.then_inc(s_ftr, 1)

            def slots(it, first, end, former=None):
                for slot in range(first, end):
                    if slot < IN_GROUPS:
                        group(it, slot)
                    elif slot == OUT_A:
                        for s in (19, 20, 21):
                            wait_group_read(pe, it, s)
                        pe.wait_ge(s_oT, it * PAIRS + PAIRS)
                    if OUT_A <= slot < OUT_A + A_UNITS:
                        unit = slot - OUT_A
                        pe.wait_ge(s_lo[slot % 2], it * UH + slot // 2 + 1)
                        out_a(it, unit, (0, 1) if unit < A_UNITS - 1 else (0,))
                    elif slot == OUT_A + A_UNITS:
                        out_a(it, A_UNITS - 1, (1,))
                    a = head_at(slot, NORM_MUL)
                    if a is not None:
                        head_mul(it, a)
                    a = head_at(slot, UPDATE)
                    if a is not None:
                        key_turn(it, a)
                    if slot == 1:
                        v_values(it)
                    if slot == SWA_SUM:
                        pe.wait_ge(s_osq, it * PAIRS + PAIRS)
                        sums(X[1], qT, s_ssum)
                    if slot == SWA_MUL:
                        pe.wait_ge(s_srr, it + 1)
                        spread(X[1], srnrm, s_smul)
                    for begin, step in ((SCORE, scores), (P_TURN, p_turn), (PV, pv)):
                        i = step_at(slot, begin)
                        if i is not None:
                            step(it, i)
                    for offset, step in ((V_TURN, iv_turn), (KEYS, keys), (UPDATE, update), (OUTPUT, output),
                                         (NORM_SUM, head_sum)):
                        a = head_at(slot, offset)
                        if a is not None:
                            step(it, a)
                    if former is not None:
                        if slot == FINAL_SUM:
                            final_sum(former)
                        if slot == FINAL_SPREAD:
                            final_spread(former)
                        if 0 <= slot - FINAL_TURN < TB:
                            final_turn(former, slot - FINAL_TURN)
                    if 0 <= slot - XT_SLOT < 2 * TB:
                        x_turn(it, slot - XT_SLOT)

            def out_b(it):
                for c, bank in zip(range(4, CS), (1, 2, 3, 0)):
                    n = OUT_B + c - 4
                    if bank == 1:
                        pe.wait_ge(s_yb, it * PAIRS + PAIRS)
                    if bank == 0:
                        pe.wait_ge(s_xT, it * 2 * TB + 2 * TB)
                    pe.wait_ge(s_lo[n % 2], it * UH + n // 2 + 1)
                    for k in range(KD):
                        last = product(X[bank][:, :], n % 2, yhi[:, k, :], ylo[:, k, :], k, k == 0, k == KD - 1)
                    last.then_inc(s_group, 1)

            def ffn_group(it, jj, n):
                pe.wait_ge(s_lo[n % 2], it * UH + FFN0 // 2 + 2 * jj + n // 2 + 1)
                for k in range(KD):
                    if is_first(jj) and n == 0:
                        pe.wait_ge(s_ulo, it * KD + k + 1)
                    last = product(M[n][:, :], n % 2, uhi[:, k, :], ulo[:, k, :], k, k == 0, k == KD - 1)
                last.then_inc(s_group, 1)

            def body(it, final):
                slots(it, SPLIT, SLOTS)
                out_b(it)
                for n in range(4):
                    ffn_group(it, 0, n)
                    if n == 1:
                        pe.wait_ge(s_hacc, it * KD + KD)
                        sums(X[0], [sacc], s_nsum)
                    if n == 2:
                        pe.wait_ge(s_rroot, it * 2 + 1)
                        spread(X[1], rnrm, s_nmul)
                with pe.Fori(1, KF // 2) as jj:
                    for n in range(4):
                        pe.wait_ge((s_gate, s_up)[n % 2][n // 2], it * (KF // 2) + jj)
                        ffn_group(it, jj, n)
                with pe.Fori(0, CS // 2) as cc:
                    for j in range(2):
                        pe.wait_ge(s_alo[j], (it + 1) * (KF // 2))
                    for half in range(2):
                        pe.wait_ge(s_h2[half], it * (KD // 2) + cc + 1)
                        for part in range(ND):
                            m = half * ND + part
                            pe.wait_ge(s_lo[m % 2], it * UH + DOWN0 // 2 + cc * ND + m // 2 + 1)
                            for kb in range(DOWN_PARTS[part]):
                                k = 8 * part + kb
                                last = product(M[half][:, :], m % 2, ahi[:, k, :], alo[:, k, :], kb,
                                               k == 0, k == KF - 1)
                            last.then_inc(s_dpart, 1)
                            if m == PREP_PART and not final:
                                prep(it + 1, cc)
                if not final:
                    slots(it + 1, 0, SPLIT, it)
                else:
                    final_sum(it)
                    final_spread(it)
                    for b in range(TB):
                        final_turn(it, b)

            def prologue():
                pe.wait_ge(s_ini, INI)
                for b in range(TB):
                    prep(0, b)
                slots(0, 0, SPLIT)

            over_superblocks(pe, prologue, body)

        @block.scalar
        def _(act):
            A = nc.scalar.activation
            act.sem_inc(s_osa, 1)
            for q in s_out:
                act.sem_inc(q, 16)
            act.wait_ge(s_ini, INI)

            def make_hi(it, s, k, nb=8):
                act.wait_ge(s_raw[s], it * (UH * 16) + k * 16 + 16)
                A(whi[s][:, 0:nb, :], raw[s][:, 0:nb, :], ACT.Copy).then_inc(s_hi[s], 1)

            def prep(it, b):
                act.wait_ge(s_x, it * TB * 16 + b * 16 + 16)
                if not is_first(it * TB + b):
                    act.wait_ge(s_xr, it * TB + b)
                A(xdump[:, :], xs[0][:, :], ACT.Square, accum_out=xss[:, :]).then_inc(s_xss, 1)
                act.wait_ge(s_xss, it * TB + b + 1)
                A(xnrm[:, :], xss[:, :], ACT.Sqrt, scale=1.0 / D, bias=epst[:, 0:1]).then_inc(s_xroot, 1)

            def head_group(it, a, part, bank):
                if part == 0:
                    if a:
                        act.wait_ge(s_ktr, it * HEADS + a)
                    A(forget[:, :], bank, ACT.Tanh, scale=0.5).then_inc(s_tf, 1)
                if part == 1:
                    if a:
                        act.wait_ge(s_qdec, it * HEADS + a)
                    A(gateq[:, :], bank, ACT.Tanh, scale=0.5).then_inc(s_tq, 1)
                if part == 2:
                    if a:
                        act.wait_ge(s_ivtr, it * HEADS + a)
                    A(ivT[:, :], bank, ACT.Copy).then_inc(s_iv, 1)
                if part == 3:
                    if a >= 2:
                        act.wait_ge(s_yalo, it * HEADS + a - 1)
                    A(gate[a % 2][:, :], bank, ACT.Tanh, scale=0.5).then_inc(s_tg, 1)

            def iv_turn(it, a):
                act.wait_ge(s_ivtr, it * HEADS + a + 1)
                if a:
                    act.wait_ge(s_o, it * HEADS + a)
                A(iv[:, :], X[3][:, :], ACT.Copy).then_inc(s_ivt, 1)

            def key_turn(it, a):
                act.wait_ge(s_ktr, it * HEADS + a + 1)
                if a:
                    act.wait_ge(s_upd, it * 2 * HEADS + 2 * a)
                for c in range(2):
                    r = slice(64 * c, 64 * c + 64)
                    A(kstz[r, :, c, :], X[3][r, :].rearrange("p (b k) -> p b k", b=TB),
                      ACT.Copy).then_inc(s_kz, 1)

            def output(it, a):
                act.wait_ge(s_o, it * HEADS + a + 1)
                if a:
                    act.wait_ge(s_asum, it * HEADS + a)
                A(sqo[:, :], X[2][:, :], ACT.Square).then_inc(s_sq, 1)

            def head_sum(it, a):
                act.wait_ge(s_asum, it * HEADS + a + 1)
                if a:
                    act.wait_ge(s_arr, it * HEADS + a)
                A(hnrm[:, :], X[3][:, 0:TB], ACT.Sqrt, scale=1.0 / P, bias=epst[:, 0:1]).then_inc(s_aroot, 1)

            def head_mul(it, a):
                act.wait_ge(s_ya, it * HEADS + a + 1)
                A(yhi[:, a, :], gate[a % 2][:, :], ACT.Copy).then_inc(s_yahi, 1)

            def scores(it, i):
                w = i % 2
                act.wait_ge(s_nms, it * STEPS + i + 1)
                if i:
                    act.wait_ge(s_den, it * STEPS + i)
                for par in range(2):
                    half = pr[w][:, par * 256:(par + 1) * 256]
                    A(half, half, ACT.Exp, scale=0.125, bias=nm[:, w, par:par + 1],
                      accum_out=rs[:, w, par:par + 1])
                A(es[:, :], nms[:, :], ACT.Exp).then_inc(s_exp, 1)

            def p_turn(it, i):
                act.wait_ge(s_ptr, it * STEPS + i + 1)
                if i >= 2:
                    act.wait_ge(s_pv, it * STEPS + i - 1)
                A(pT[i % 2][:, :], X[1][:, :], ACT.Copy).then_inc(s_pT, 1)

            def pv(it, i):
                if i % TB == TB - 1:
                    p = i // TB
                    act.wait_ge(s_oT, it * PAIRS + p + 1)
                    A(qT[p][:, :], oT[p][:, :], ACT.Square).then_inc(s_osq, 1)

            def x_turn(it, j):
                half, b = divmod(j, TB)
                act.wait_ge(s_xtr, it * 2 * TB + j + 1)
                A(h[:, 4 * half:4 * half + 4, b * P:(b + 1) * P],
                  X[0][:, :].rearrange("p (c t) -> p c t", c=4), ACT.Copy).then_inc(s_xT, 1)

            def final_sum(it):
                act.wait_ge(s_nsum, it * 2 + 2)
                act.wait_ge(s_rroot, it * 2 + 1)
                A(nrm[:, :], X[2][:, 0:TB], ACT.Sqrt, scale=1.0 / D, bias=epst[:, 0:1]).then_inc(s_root, 1)

            def final_turn(it, b):
                act.wait_ge(s_ftr, it * 2 * TB + 2 * b + 1)
                act.wait_ge(s_out[b % 2], it * 32 + 16 * (b // 2) + 16)
                A(os_[b % 2][:, 0:D // 2], X[2][:, :], ACT.Copy).then_inc(s_osa, 1)

            def store(it, b):
                act.wait_ge(s_osa, it * TB + b + 2)
                act.wait_ge(s_osb, it * TB + b + 2)
                act.dma_start(out_t[bass.ds(it * TB + b, 1), :, :].rearrange("o p d -> (o p) d"),
                              os_[b % 2][:, :]).then_inc(s_out[b % 2], 16)

            def slots(it, first, end, former=None):
                for slot in range(first, end):
                    n = slot + 2
                    if n < OUT_B + 1:
                        wait_unit_used(act, it, n)
                        make_hi(it, n % 2, n // 2)
                    bank = M[slot % 3][:, :]
                    if slot < IN_GROUPS:
                        act.wait_ge(s_group, it * GROUPS + slot + 1)
                    if slot == 1:
                        A(ivT[:, :], bank, ACT.Copy).then_inc(s_bvT, 1)
                        act.wait_ge(s_vtr, it + 1)
                        act.wait_ge(s_vcar, it + 1)
                        A(vals[:, 1:TB + 1, :], X[1][:, :].rearrange("p (b k) -> p b k", b=TB),
                          ACT.Copy).then_inc(s_vals, 1)
                    elif slot in Q_SLOT:
                        A(qT[Q_SLOT.index(slot)][:, :], bank, ACT.Copy).then_inc(s_q, 1)
                    a, part = head_part(slot)
                    if a is not None:
                        head_group(it, a, part, bank)
                    a = head_at(slot, NORM_MUL)
                    if a is not None:
                        head_mul(it, a)
                    a = head_at(slot, UPDATE)
                    if a is not None:
                        key_turn(it, a)
                    if slot == SWA_SUM:
                        act.wait_ge(s_ssum, it + 1)
                        A(snrm[:, :], X[1][:, 0:TB], ACT.Sqrt, scale=1.0 / (PAIRS * P),
                          bias=epst[:, 0:1]).then_inc(s_sroot, 1)
                    if slot == SWA_MUL:
                        for p in range(PAIRS):
                            act.wait_ge(s_yb, it * PAIRS + p + 1)
                            A(yhi[:, HEADS + p, :], oT[p][:, :], ACT.Copy).then_inc(s_ybhi, 1)
                    for begin, step in ((SCORE, scores), (P_TURN, p_turn), (PV, pv)):
                        i = step_at(slot, begin)
                        if i is not None:
                            step(it, i)
                    for offset, step in ((V_TURN, iv_turn), (OUTPUT, output), (NORM_SUM, head_sum)):
                        a = head_at(slot, offset)
                        if a is not None:
                            step(it, a)
                    if former is not None:
                        if slot == FINAL_SUM:
                            final_sum(former)
                        if 0 <= slot - FINAL_TURN < TB:
                            final_turn(former, slot - FINAL_TURN)
                            store(former, slot - FINAL_TURN)
                    if 0 <= slot - XT_SLOT < 2 * TB:
                        x_turn(it, slot - XT_SLOT)

            def out_b(it):
                wait_unit_used(act, it, OUT_B + 1)
                make_hi(it, (OUT_B + 1) % 2, (OUT_B + 1) // 2)
                for c in range(CS):
                    n = OUT_B + 2 + c - 4
                    if c >= 4:
                        wait_unit_used(act, it, n)
                        make_hi(it, n % 2, n // 2)
                    act.wait_ge(s_h, it * KD + c + 1)
                    A(uhi[:, c, :], h[:, c, :], ACT.Copy, scale=g2[:, c:c + 1]).then_inc(s_uhi, 1)
                    if c >= 2:
                        act.wait_ge(s_hacc, it * KD + c - 1)
                    A(sqs[c % 2][:, :], h[:, c, :], ACT.Square).then_inc(s_hsq, 1)

            def ffn_hi(it, jj, m):
                act.wait_ge(s_group, it * GROUPS + FFN0 + 4 * jj + m + 1)
                make_hi(it, m % 2, 2 * jj + (FFN0 + 2 + m) // 2)

            def silu(it, jj, j):
                act.wait_ge(s_gate[j], it * (KF // 2) + jj + 1)
                A(gu[j][:, :], gu[j][:, :], ACT.Silu).then_inc(s_silu[j], 1)

            def down_his(it, cc, units):
                for m in units:
                    act.wait_ge(s_dpart, it * DPARTS + cc * (2 * ND) + m - 1)
                    make_hi(it, m % 2, cc * ND + DOWN0 // 2 + m // 2, DOWN_PARTS[m % ND])

            def body(it, final):
                slots(it, SPLIT, SLOTS)
                out_b(it)
                ffn_hi(it, 0, 0)
                ffn_hi(it, 0, 1)
                act.wait_ge(s_nsum, it * 2 + 1)
                A(nrm[:, :], X[0][:, 0:TB], ACT.Sqrt, scale=1.0 / D, bias=epst[:, 0:1]).then_inc(s_root, 1)
                ffn_hi(it, 0, 2)
                silu(it, 0, 0)
                silu(it, 0, 1)
                ffn_hi(it, 0, 3)
                with act.Fori(1, KF // 2) as jj:
                    for m in range(4):
                        ffn_hi(it, jj, m)
                        if m % 2 == 0:
                            silu(it, jj, m // 2)
                if not final:
                    with act.Fori(0, CS // 2) as cc:
                        down_his(it, cc, range(2, 4))
                        act.wait_ge(s_out[1], it * 32 + 16)
                        prep(it + 1, cc)
                        down_his(it, cc, range(4, 2 * ND + 2))
                    slots(it + 1, 0, SPLIT, it)
                else:
                    with act.Fori(0, CS // 2 - 1) as cc:
                        down_his(it, cc, range(2, 2 * ND + 2))
                    down_his(it, CS // 2 - 1, range(2, 2 * ND))
                    final_sum(it)
                    for b in range(TB):
                        final_turn(it, b)
                        store(it, b)
                    for q in s_out:
                        act.wait_ge(q, NSB * 32 + 16)

            def prologue():
                prep(0, 0)
                make_hi(0, 0, 0)
                for b in range(1, TB):
                    prep(0, b)
                make_hi(0, 1, 0)
                act.wait_ge(s_ini2, 3)
                A(lbs[:, 0:2, :], lbs[:, 2:4, :], ACT.Exp).then_inc(s_ini3, 1)
                slots(0, 0, SPLIT)

            over_superblocks(act, prologue, body)

        @block.vector
        def _(dve):
            V = nc.vector
            for s in (*s_h2, s_xn, s_osb):
                dve.sem_inc(s, 1)

            def parameters():
                dve.wait_ge(s_par, 7 * 16)
                V.tensor_tensor(f_mul[:, :], lbl[:, 0, :], lbl[:, 1, :], ALU.max).then_inc(s_ini2, 1)
                dve.wait_ge(s_ini2, 1)
                for l in range(2):
                    V.tensor_tensor(lbs[:, 2 + l, :], lbl[:, l, :], f_mul[:, :], ALU.subtract).then_inc(s_ini2, 1)
                dve.wait_ge(s_ini3, 1)
                V.tensor_tensor(f_add[:, :], lbs[:, 0, :], lbs[:, 1, :], ALU.add).then_inc(s_ini2, 1)
                dve.wait_ge(s_ini2, 4)
                V.reciprocal(f_mul[:, :], f_add[:, :]).then_inc(s_ini2, 1)
                dve.wait_ge(s_ini2, 5)
                V.tensor_tensor(lbs[:, 2, :], lbs[:, 0, :], f_mul[:, :], ALU.mult).then_inc(s_ini2, 1)
                dve.wait_ge(s_ini2, 6)
                V.tensor_scalar(f_mul[:, :], lbs[:, 2, :], -0.5, 0.5, ALU.mult, ALU.add).then_inc(s_ini2, 1)
                V.tensor_scalar(f_add[:, :], lbs[:, 2, :], 0.5, 0.5, ALU.mult, ALU.add).then_inc(s_ini2, 1)
                V.tensor_scalar(ga[:, :], ga[:, :], 0.5, None, ALU.mult).then_inc(s_ini2, 1)
                V.tensor_scalar(nsinks[:, :], sinks[:, :], -1.0, None, ALU.mult).then_inc(s_ini2, 1)
                V.tensor_copy(causal[:, :].bitcast(I32), causal[:, :]).then_inc(s_ini2, 1)
                dve.wait_ge(s_ini2, 11)

            def make_lo(it, s, k, nb=8):
                dve.wait_ge(s_hi[s], it * UH + k + 1)
                V.tensor_tensor(wlo[s][:, 0:nb, :], raw[s][:, 0:nb, :], whi[s][:, 0:nb, :].bitcast(F32),
                                ALU.subtract).then_inc(s_lo[s], 1)

            def prep(it, b):
                dve.wait_ge(s_xroot, it * TB + b + 1)
                V.reciprocal(xrn[:, :], xnrm[:, :]).then_inc(s_xr, 1)
                dve.wait_ge(s_xr, it * TB + b + 1)
                V.scalar_tensor_tensor(out=xs[1][:, :], in0=xs[0][:, :], scalar=xrn[:, 0:1], in1=g1row[:, :],
                                       op0=ALU.mult, op1=ALU.mult).then_inc(s_xn, 1)

            def prep_split(it, b):
                columns = bass.ds(b * P, P)
                for half in range(2):
                    n = it * 2 * TB + 2 * b + half + 1
                    uh, ul = (u[:, 4 * half:4 * half + 4, columns] for u in (uhi, ulo))
                    xT = X[2 + half][:, :].rearrange("p (c t) -> p c t", c=4)
                    dve.wait_ge(s_ptr0, n)
                    V.tensor_scalar(uh, xT, 1.0, None, ALU.mult).then_inc(s_xuhi, 1)
                    dve.wait_ge(s_xuhi, n)
                    V.tensor_tensor(ul, xT, uh.bitcast(F32), ALU.subtract).then_inc(s_xulo, 1)

            def denominators(it, i):
                w = i % 2
                dve.wait_ge(s_exp, it * STEPS + i + 1)
                V.tensor_tensor(den[:, :], rs[:, w, :], es[:, :], ALU.add).then_inc(s_den, 1)
                dve.wait_ge(s_den, it * STEPS + i + 1)
                if i:
                    dve.wait_ge(s_prob, it * STEPS + i)
                V.reciprocal(rd[:, :], den[:, :]).then_inc(s_rd, 1)

            def scores(it, i):
                p, b = divmod(i, TB)
                w = i % 2
                dve.wait_ge(s_score, it * STEPS + i + 1)
                if i >= 2:
                    dve.wait_ge(s_ptr, it * STEPS + i - 1)
                if i == 0 and not is_first(it):
                    dve.wait_ge(s_dist, it)
                d = dist0 if b == 0 else dist
                for par in range(2):
                    slope = 2.0 ** -(2 * p + par + 1)
                    half = slice(par * 256, (par + 1) * 256)
                    last = V.scalar_tensor_tensor(out=pr[w][:, half], in0=d[:, :], scalar=8.0 * slope,
                                                  in1=X[0][:, half], op0=ALU.mult, op1=ALU.add)
                last.then_inc(s_bias, 1)
                dve.wait_ge(s_bias, it * STEPS + i + 1)
                V.tensor_reduce(mx[:, :], pr[w][:, :].rearrange("p (h k) -> p h k", h=2), AX_X,
                                ALU.max).then_inc(s_mx, 1)
                dve.wait_ge(s_mx, it * STEPS + i + 1)
                V.scalar_tensor_tensor(out=nm[:, w, :], in0=mx[:, :], scalar=-0.125,
                                       in1=nsinks[:, 2 * p:2 * p + 2], op0=ALU.mult,
                                       op1=ALU.min).then_inc(s_nm, 1)
                dve.wait_ge(s_nm, it * STEPS + i + 1)
                V.tensor_tensor(nms[:, :], nm[:, w, :], sinks[:, 2 * p:2 * p + 2], ALU.add).then_inc(s_nms, 1)

            def head_group(it, a, part, bank):
                n = it * HEADS + a
                w = a % 2
                if part == 0:
                    dve.wait_ge(s_tf, n + 1)
                    V.tensor_scalar(forget[:, :], forget[:, :], f_mul[:, a:a + 1], f_add[:, a:a + 1],
                                    ALU.mult, ALU.add).then_inc(s_f, 1)
                    dve.wait_ge(s_f, n + 1)
                    if a >= 2:
                        dve.wait_ge(s_kst, n - 1)
                    for c in range(NCH):
                        r = slice(c * CHUNK, (c + 1) * CHUNK)
                        last = V.tensor_tensor_scan(cum[w][:, r], forget[:, r], ones[:, :], 1.0, ALU.mult, ALU.mult)
                    last.then_inc(s_cum, 1)
                    dve.wait_ge(s_cum, n + 1)
                    if a:
                        dve.wait_ge(s_key, n)
                    V.reciprocal(cuminv[:, :], cum[w][:, :]).then_inc(s_inv, 1)
                if part == 1:
                    dve.wait_ge(s_tq, n + 1)
                    V.scalar_tensor_tensor(out=gateq[:, :], in0=gateq[:, :], scalar=1.0, in1=bank,
                                           op0=ALU.add, op1=ALU.mult).then_inc(s_qs, 1)
                    dve.wait_ge(s_qs, n + 1)
                    if a >= 2:
                        dve.wait_ge(s_o, n - 1)
                    V.scalar_tensor_tensor(out=qdec[w][:, :], in0=gateq[:, :], scalar=0.5, in1=cum[w][:, :],
                                           op0=ALU.mult, op1=ALU.mult).then_inc(s_qdec, 1)
                if part == 3:
                    dve.wait_ge(s_tg, n + 1)
                    V.scalar_tensor_tensor(out=gate[w][:, :], in0=gate[w][:, :], scalar=1.0, in1=bank,
                                           op0=ALU.add, op1=ALU.mult).then_inc(s_gs, 1)

            def keys(it, a):
                n = it * HEADS + a
                dve.wait_ge(s_a, n + 1)
                if a:
                    dve.wait_ge(s_o, n)
                V.tensor_tensor(amask[:, :, :].bitcast(I32),
                                X[2][:, :].rearrange("p (b c) -> p b c", b=TB).bitcast(I32),
                                causal[:, :].bitcast(I32).rearrange("p (o c) -> p o c", o=1)
                                .broadcast_to([P, TB, P]), ALU.bitwise_and).then_inc(s_am, 1)

            def update(it, a):
                n = it * HEADS + a
                s0 = it * (NCH * HEADS) + NCH * a
                if a:
                    dve.wait_ge(s_scar, n)
                    dve.wait_ge(s_o, n)
                for c in range(NCH):
                    if c % 4 == 0:
                        dve.wait_ge(s_upd, it * 2 * HEADS + 2 * a + c // 4 + 1)
                    before = state[:, a, :] if c == 0 else st[(c - 1) // 4][:, (c - 1) % 4, :]
                    if c:
                        dve.wait_ge(s_st, s0 + c)
                    last_token = (c + 1) * CHUNK - 1
                    V.scalar_tensor_tensor(out=st[c // 4][:, c % 4, :], in0=before,
                                           scalar=cum[a % 2][:, last_token:last_token + 1],
                                           in1=X[2 + c // 4][:, (c % 4) * P:(c % 4 + 1) * P],
                                           op0=ALU.mult, op1=ALU.add).then_inc(s_st, 1)

            def output(it, a):
                n = it * HEADS + a
                dve.wait_ge(s_sq, n + 1)
                dve.wait_ge(s_gs, n + 1)
                V.scalar_tensor_tensor(out=gate[a % 2][:, :], in0=X[2][:, :], scalar=ga[:, a:a + 1],
                                       in1=gate[a % 2][:, :], op0=ALU.mult, op1=ALU.mult).then_inc(s_y1, 1)

            def head_sum(it, a):
                n = it * HEADS + a
                dve.wait_ge(s_aroot, n + 1)
                if a:
                    dve.wait_ge(s_amul, n)
                V.reciprocal(hrnrm[:, :], hnrm[:, :]).then_inc(s_arr, 1)

            def head_mul(it, a):
                n = it * HEADS + a
                dve.wait_ge(s_amul, n + 1)
                dve.wait_ge(s_y1, n + 1)
                V.tensor_tensor(gate[a % 2][:, :], gate[a % 2][:, :], X[3][:, :], ALU.mult).then_inc(s_ya, 1)

            def head_lo(it, a):
                dve.wait_ge(s_yahi, it * HEADS + a + 1)
                V.tensor_tensor(ylo[:, a, :], gate[a % 2][:, :], yhi[:, a, :].bitcast(F32),
                                ALU.subtract).then_inc(s_yalo, 1)

            def final_sum(it):
                dve.wait_ge(s_root, it * 2 + 2)
                dve.wait_ge(s_nmul, it * 2 + 1)
                V.reciprocal(rnrm[:, :], nrm[:, :]).then_inc(s_rroot, 1)

            def final_scale(it):
                dve.wait_ge(s_nmul, it * 2 + 2)
                for k in range(KD):
                    V.scalar_tensor_tensor(out=h[:, k, :], in0=h[:, k, :], scalar=gf[:, k:k + 1],
                                           in1=X[3][:, :], op0=ALU.mult, op1=ALU.mult).then_inc(s_fin, 1)

            def final_turn(it, b):
                dve.wait_ge(s_ftr, it * 2 * TB + 2 * b + 2)
                dve.wait_ge(s_out[b % 2], it * 32 + 16 * (b // 2) + 16)
                V.tensor_copy(os_[b % 2][:, D // 2:D], X[3][:, :]).then_inc(s_osb, 1)

            def slots(it, first, end, former=None):
                for slot in range(first, end):
                    i = step_at(slot, P_TURN)
                    if i is not None:
                        denominators(it, i)
                    n = slot + 2
                    if n < OUT_B + 1:
                        wait_unit_used(dve, it, n)
                        make_lo(it, n % 2, n // 2)
                    mul = head_at(slot, NORM_MUL)
                    if mul is not None:
                        head_mul(it, mul)
                    bank = M[slot % 3][:, :]
                    if slot == 0:
                        dve.wait_ge(s_group, it * GROUPS + 1)
                        dve.wait_ge(s_kcar, it + 1)
                        for g in range(KV):
                            for par in range(2):
                                V.tensor_copy(keyz[64 * par:64 * par + 64, g, par, BLOCK:BLOCK + T],
                                              M[0][64 * g:64 * g + 64, :]).then_inc(s_k, 1)
                    a, part = head_part(slot)
                    if a is not None:
                        head_group(it, a, part, bank)
                    if slot == SWA_SUM:
                        dve.wait_ge(s_sroot, it + 1)
                        V.reciprocal(srnrm[:, :], snrm[:, :]).then_inc(s_srr, 1)
                    if slot == SWA_MUL:
                        dve.wait_ge(s_smul, it + 1)
                        for p in range(PAIRS):
                            dve.wait_ge(s_osq, it * PAIRS + p + 1)
                            V.scalar_tensor_tensor(out=oT[p][:, :], in0=oT[p][:, :], scalar=gb[:, p:p + 1],
                                                   in1=X[1][:, :], op0=ALU.mult, op1=ALU.mult).then_inc(s_yb, 1)
                        for p in range(PAIRS):
                            dve.wait_ge(s_ybhi, it * PAIRS + p + 1)
                            V.tensor_tensor(ylo[:, HEADS + p, :], oT[p][:, :], yhi[:, HEADS + p, :].bitcast(F32),
                                            ALU.subtract).then_inc(s_yblo, 1)
                    i = step_at(slot, SCORE)
                    if i is not None:
                        scores(it, i)
                    if mul is not None:
                        head_lo(it, mul)
                    i = step_at(slot, PV)
                    if i is not None and i % TB == TB - 1:
                        dve.wait_ge(s_pv, it * STEPS + i + 1)
                        V.tensor_copy(oT[i // TB][:, :], M[3][:, :]).then_inc(s_oT, 1)
                    for offset, step in ((KEYS, keys), (UPDATE, update), (OUTPUT, output), (NORM_SUM, head_sum)):
                        a = head_at(slot, offset)
                        if a is not None:
                            step(it, a)
                    if former is not None:
                        if slot == FINAL_SUM:
                            final_sum(former)
                        if slot == FINAL_SCALE:
                            final_scale(former)
                        if 0 <= slot - FINAL_TURN < TB:
                            final_turn(former, slot - FINAL_TURN)

            def out_b(it):
                wait_unit_used(dve, it, OUT_B + 1)
                make_lo(it, (OUT_B + 1) % 2, (OUT_B + 1) // 2)
                dve.wait_ge(s_xT, it * 2 * TB + 2 * TB)
                for c in range(CS):
                    if c < 4:
                        bank = M[c]
                    else:
                        n = OUT_B + 2 + c - 4
                        wait_unit_used(dve, it, n)
                        make_lo(it, n % 2, n // 2)
                        bank = X[(1, 2, 3, 0)[c - 4]]
                    V.tensor_tensor(h[:, c, :], h[:, c, :], bank[:, :], ALU.add).then_inc(s_h, 1)
                    if c:
                        u_lo(it, c - 1)
                u_lo(it, CS - 1)

            def u_lo(it, c):
                dve.wait_ge(s_uhi, it * KD + c + 1)
                V.scalar_tensor_tensor(out=ulo[:, c, :], in0=h[:, c, :], scalar=g2[:, c:c + 1],
                                       in1=uhi[:, c, :].bitcast(F32), op0=ALU.mult,
                                       op1=ALU.subtract).then_inc(s_ulo, 1)

            def ffn_lo(it, jj, m):
                dve.wait_ge(s_group, it * GROUPS + FFN0 + 4 * jj + m + 1)
                make_lo(it, m % 2, 2 * jj + (FFN0 + 2 + m) // 2)

            def read_gate(it, jj, j):
                if not is_first(jj):
                    dve.wait_ge(s_alo[j], it * (KF // 2) + jj)
                V.tensor_tensor(gu[j][:, :], M[2 * j][:, :], factors, ALU.mult).then_inc(s_gate[j], 1)

            def read_up(it, jj, j):
                done = it * (KF // 2) + jj + 1
                V.tensor_tensor(upn, M[2 * j + 1][:, :], factors, ALU.mult).then_inc(s_up[j], 1)
                dve.wait_ge(s_up[j], done)
                dve.wait_ge(s_silu[j], done)
                V.tensor_tensor(gu[j][:, :], gu[j][:, :], upn, ALU.mult).then_inc(s_prod[j], 1)
                dve.wait_ge(s_prod[j], done)
                block = bass.ds(2 * jj + j, 1)
                wide = gu[j][:, :].rearrange("p (o t) -> p o t", o=1)
                V.tensor_scalar(ahi[:, block, :], wide, 1.0, None, ALU.mult).then_inc(s_ahi[j], 1)
                dve.wait_ge(s_ahi[j], done)
                V.tensor_tensor(alo[:, block, :], wide, ahi[:, block, :].bitcast(F32),
                                ALU.subtract).then_inc(s_alo[j], 1)

            def down_los(it, cc, units):
                for m in units:
                    dve.wait_ge(s_dpart, it * DPARTS + cc * (2 * ND) + m - 1)
                    make_lo(it, m % 2, cc * ND + DOWN0 // 2 + m // 2, DOWN_PARTS[m % ND])
                    if (m - 1) % ND == 0:
                        add_block(it, cc, (m - 1) // ND - 1)

            def add_block(it, cc, half):
                c = cc * 2 + half
                hc = h[:, bass.ds(c, 1), :]
                V.tensor_tensor(hc, hc, M[half][:, :].rearrange("p (o t) -> p o t", o=1),
                                ALU.add).then_inc(s_h2[half], 1)
                dve.wait_ge(s_h2[half], it * (KD // 2) + cc + 2)
                dve.wait_ge(s_h2acc[half], it * (KD // 2) + cc + 1)
                V.tensor_tensor(sqs[half][:, :].rearrange("p (o t) -> p o t", o=1), hc, hc,
                                ALU.mult).then_inc(s_h2sq[half], 1)

            def body(it, final):
                slots(it, SPLIT, SLOTS)
                out_b(it)
                ffn_lo(it, 0, 0)
                ffn_lo(it, 0, 1)
                dve.wait_ge(s_root, it * 2 + 1)
                V.reciprocal(rnrm[:, :], nrm[:, :]).then_inc(s_rroot, 1)
                ffn_lo(it, 0, 2)
                dve.wait_ge(s_nmul, it * 2 + 1)
                dve.wait_ge(s_out[1], it * 32 + 16)
                V.tensor_copy(factors, X[1][:, :]).then_inc(s_fac, 1)
                dve.wait_ge(s_fac, it + 1)
                read_gate(it, 0, 0)
                read_gate(it, 0, 1)
                read_up(it, 0, 0)
                ffn_lo(it, 0, 3)
                read_up(it, 0, 1)
                with dve.Fori(1, KF // 2) as jj:
                    for m in range(4):
                        ffn_lo(it, jj, m)
                        if m % 2 == 0:
                            read_gate(it, jj, m // 2)
                        else:
                            read_up(it, jj, m // 2)
                if not final:
                    with dve.Fori(0, CS // 2) as cc:
                        down_los(it, cc, range(2, 4))
                        prep(it + 1, cc)
                        down_los(it, cc, range(4, PREP_PART + 3))
                        prep_split(it + 1, cc)
                        down_los(it, cc, range(PREP_PART + 3, 2 * ND + 2))
                    slots(it + 1, 0, SPLIT, it)
                else:
                    with dve.Fori(0, CS // 2 - 1) as cc:
                        down_los(it, cc, range(2, 2 * ND + 2))
                    down_los(it, CS // 2 - 1, range(2, 2 * ND))
                    dve.wait_ge(s_dpart, (it + 1) * DPARTS)
                    add_block(it, CS // 2 - 1, 1)
                    final_sum(it)
                    final_scale(it)
                    for b in range(TB):
                        final_turn(it, b)

            def prologue():
                prep(0, 0)
                prep_split(0, 0)
                make_lo(0, 0, 0)
                for b in range(1, TB):
                    prep(0, b)
                    prep_split(0, b)
                make_lo(0, 1, 0)
                parameters()
                slots(0, 0, SPLIT)

            dve.wait_ge(s_ini, INI)
            dve.wait_ge(s_g1, 16)
            over_superblocks(dve, prologue, body)

        @block.gpsimd
        def _(pool):
            G = nc.gpsimd
            for s in s_h2acc:
                pool.sem_inc(s, 1)
            G.memset(ident[:, :], 0.0).then_inc(s_ini, 1)
            G.memset(ones[:, :], 1.0).then_inc(s_ini, 1)
            G.memset(epst[:, :], EPS).then_inc(s_ini, 1)
            G.memset(keyz[:, :, :, :], 0.0).then_inc(s_ini, 1)
            G.memset(vals[:, :, :], 0.0).then_inc(s_ini, 1)
            G.memset(kstz[:, :, :, :], 0.0).then_inc(s_ini, 1)
            G.memset(state[:, :, :], 0.0).then_inc(s_ini, 1)
            G.memset(causal[:, :], -1.0).then_inc(s_ini, 1)
            G.iota(dist[:, :].bitcast(I32), [[1, 2 * BLOCK]], base=-BLOCK, channel_multiplier=-1).then_inc(s_ini, 1)
            pool.wait_ge(s_ini, 9)
            G.affine_select(out=ident[:, :], in_=ident[:, :], compare_op=ALU.not_equal, fill=1.0, base=0,
                            pattern=[[-1, P]], channel_multiplier=1).then_inc(s_ini, 1)
            G.affine_select(out=causal[:, :], in_=causal[:, :], compare_op=ALU.is_ge, fill=0.0, base=0,
                            pattern=[[1, P]], channel_multiplier=-1).then_inc(s_ini, 1)
            G.tensor_copy(dist0[:, :], dist[:, :].bitcast(I32)).then_inc(s_ini, 1)
            pool.wait_ge(s_ini, 12)
            G.memset(causal[0:CHUNK, CHUNK:P], 0.0).then_inc(s_ini, 1)
            G.affine_select(out=dist0[:, :], in_=dist0[:, :], compare_op=ALU.is_ge, fill=MASKED, base=BLOCK,
                            pattern=[[-1, 2 * BLOCK]], channel_multiplier=1).then_inc(s_dst, 1)
            pool.wait_ge(s_dst, 1)
            G.affine_select(out=dist[:, :], in_=dist0[:, :], compare_op=ALU.is_ge, fill=MASKED, base=-1,
                            pattern=[[1, 2 * BLOCK]], channel_multiplier=-1).then_inc(s_dst, 1)
            pool.wait_ge(s_dst, 2)
            G.tensor_copy(dist0[:, BLOCK:2 * BLOCK], dist[:, BLOCK:2 * BLOCK]).then_inc(s_dst, 1)
            G.memset(dist0[:, 0:BLOCK], MASKED).then_inc(s_dst, 1)
            pool.wait_ge(s_dst, 4)
            pool.wait_ge(s_ini, 13)
            G.memset(zero[:, :], 0.0).then_inc(s_ini, 1)

            def copy(out, in_):
                return G.tensor_tensor(out, in_, ones[:, 0:1].broadcast_to(list(in_.shape)), ALU.mult)

            keys_all = keyz[:, :, :, :].rearrange("p g r t -> p (g r) t")

            def key_steps(it, a):
                n = it * HEADS + a
                pool.wait_ge(s_f, n + 1)
                if a:
                    pool.wait_ge(s_a, n)
                G.tensor_tensor(key[:, :], ones[:, 0:1].broadcast_to([P, T]), forget[:, :],
                                ALU.subtract).then_inc(s_key0, 1)
                pool.wait_ge(s_key0, n + 1)
                pool.wait_ge(s_inv, n + 1)
                G.tensor_tensor(key[:, :], key[:, :], cuminv[:, :], ALU.mult).then_inc(s_key, 1)
                pool.wait_ge(s_key, n + 1)
                ends = cum[a % 2][:, :].rearrange("p (c t) -> p c t", c=NCH)[:, :, CHUNK - 1:CHUNK]
                G.tensor_tensor(kstate[:, :].rearrange("p (c t) -> p c t", c=NCH),
                                key[:, :].rearrange("p (c t) -> p c t", c=NCH),
                                ends.broadcast_to([P, NCH, CHUNK]), ALU.mult).then_inc(s_kst, 1)

            def normalise(it, i):
                pool.wait_ge(s_rd, it * STEPS + i + 1)
                halves = pr[i % 2][:, :].rearrange("p (h k) -> p h k", h=2)
                G.tensor_tensor(halves, halves, rd[:, :].rearrange("p (h o) -> p h o", o=1)
                                .broadcast_to([P, 2, 2 * BLOCK]), ALU.mult).then_inc(s_prob, 1)
                if i == (PAIRS - 1) * TB + 1:
                    pool.wait_ge(s_bias, it * STEPS + i)
                    copy(dist0[:, :], dist[:, :]).then_inc(s_dist, 1)

            def carry_state(it, a):
                n = it * HEADS + a
                pool.wait_ge(s_o, n + 1)
                pool.wait_ge(s_st, it * (NCH * HEADS) + NCH * (a + 1))
                copy(state[:, a, :], st[1][:, 3, :]).then_inc(s_scar, 1)

            def slots(it, first, end):
                for slot in range(first, end):
                    if slot == 0:
                        if not is_first(it):
                            pool.wait_ge(s_score, it * STEPS)
                        copy(keys_all[:, :, 0:BLOCK], keys_all[:, :, T:T + BLOCK]).then_inc(s_kcar, 1)
                        if not is_first(it):
                            pool.wait_ge(s_pv, it * STEPS)
                        copy(vals[:, 0, :], vals[:, TB, :]).then_inc(s_vcar, 1)
                    i = step_at(slot, P_TURN)
                    if i is not None:
                        normalise(it, i)
                    for offset, step in ((0, key_steps), (OUTPUT, carry_state)):
                        a = head_at(slot, offset)
                        if a is not None:
                            step(it, a)

            acc = sacc[:, 0:T]

            def body(it, final):
                slots(it, SPLIT, SLOTS)
                for c in range(KD):
                    pool.wait_ge(s_hsq, it * KD + c + 1)
                    if c == 0:
                        pool.wait_ge(s_out[0], it * 32 + 16)
                        copy(acc, sqs[0][:, :]).then_inc(s_hacc, 1)
                    else:
                        pool.wait_ge(s_hacc, it * KD + c)
                        G.tensor_tensor(acc, acc, sqs[c % 2][:, :], ALU.add).then_inc(s_hacc, 1)
                for c in range(KD):
                    pool.wait_ge(s_h2sq[c % 2], it * (KD // 2) + c // 2 + 1)
                    if c == 0:
                        pool.wait_ge(s_nsum, it * 2 + 1)
                        copy(acc, sqs[0][:, :]).then_inc(s_h2acc[0], 1)
                    else:
                        pool.wait_ge(s_h2acc[(c - 1) % 2], it * (KD // 2) + (c - 1) // 2 + 2)
                        G.tensor_tensor(acc, acc, sqs[c % 2][:, :], ALU.add).then_inc(s_h2acc[c % 2], 1)
                if not final:
                    slots(it + 1, 0, SPLIT)

            over_superblocks(pool, lambda: slots(0, 0, SPLIT), body)


_INS = ['x', 'ln1_g', 'w_in', 'lb_logits', 'hgrn_norm_g', 'attn_sinks', 'attn_norm_g', 'w_out', 'ln2_g', 'w_gate',
        'w_up', 'w_down', 'final_g']


def kernel(**inputs):
    import numpy as _np
    import concourse.bacc as _bacc
    from concourse import mybir as _mybir
    from concourse.bass_utils import run_bass_kernel_spmd as _run

    nc = _bacc.Bacc("TRN2", target_bir_lowering=False, num_devices=1)
    arrays, args = {}, []
    for name in _INS:
        a = _np.ascontiguousarray(inputs[name])
        arrays[f"in_{name}_dram"] = a
        args.append(nc.dram_tensor(f"in_{name}_dram", a.shape, _mybir.dt.from_np(a.dtype), kind="ExternalInput").ap())
    shape = inputs["x"].shape
    args.append(nc.dram_tensor("out_0_dram", shape, _mybir.dt.float32, kind="ExternalOutput").ap())
    block_program(nc, *args)
    r = _run(nc, [arrays], core_ids=[0])
    return r.results[0]["out_0_dram"]
```

```python
from contextlib import ExitStack

import concourse.bass as bass
from concourse import mybir

F32 = mybir.dt.float32
F32R = mybir.dt.float32r
I32 = mybir.dt.int32
ALU = mybir.AluOpType
ACT = mybir.ActivationFunctionType
AX_X = mybir.AxisListType.X

P = 128
T = 512
TB = T // P
CHUNK = 64
NCH = T // CHUNK
HEADS = 4
KV = 2
PAIRS = 4
BLOCK = 128
EPS = 1e-6
MASKED = -1e30
STEPS = PAIRS * TB

IN_GROUPS = 22
K_SLOT, V_SLOT = 0, 2
Q_SLOT = (1, 3, 8, 13)
F_SLOT = (4, 9, 14, 18)
SPLIT = 7
OUT_A = 22
A_UNITS = 4
A_KS = ((0, 1), (2, 4), (5, 6), (3, 7))
A_PLAN = {22: (0, 1), 23: (2,), 24: (4, 5), 25: (6,), 26: (7, 3)}
A_LAST = (1, 4, 6, 3)
XT_SLOT = 19
SLOTS = 27
SCORE, PROBS, P_TURN, PV = 2, 3, 4, 5
BV_TURN = 3
SWA_SUM, SWA_MUL = 21, 22
KEY_PRODUCTS, V_TURN, KEYS, UPDATE, OUTPUT, NORM_SUM, NORM_MUL = 2, 3, 3, 4, 5, 6, 7
PREP_PART = 3
FINAL_SUM, FINAL_TURN = 0, 2


def unit_made_at(slot):
    return {23: None, 24: 25, 25: 26, 26: None}.get(slot, slot + 2)


def column_of(slot):
    if slot == K_SLOT:
        return 2560
    if slot == V_SLOT:
        return 2688
    if slot in Q_SLOT:
        return 2048 + P * Q_SLOT.index(slot)
    a, part = head_part(slot)
    return (512, 0, 1024, 1536)[part] + P * a


def head_part(slot):
    for a, first in enumerate(F_SLOT):
        if 0 <= slot - first < 4:
            return a, slot - first
    return None, None


def head_at(slot, offset):
    return F_SLOT.index(slot - offset) if slot - offset in F_SLOT else None


def step_at(slot, first):
    return slot - first if 0 <= slot - first < STEPS else None


def is_first(n):
    return isinstance(n, int) and n == 0


def block_program(nc, x, ln1_g, w_in, lb_logits, hgrn_norm_g, attn_sinks, attn_norm_g, w_out, ln2_g,
                  w_gate, w_up, w_down, final_g, out):
    S, D = x.shape[1], x.shape[2]
    FF = w_gate.shape[2]
    NSB = S // T
    KD = D // P
    KF = FF // P
    CS = D // P
    assert S % T == 0 and KD == 8 and KF % 2 == 0 and TB == CS // 2

    DOWN_PARTS = [min(8, KF - k) for k in range(0, KF, 8)]
    ND = len(DOWN_PARTS)
    OUT_B = OUT_A + A_UNITS
    FFN0 = OUT_B + CS - 4
    DOWN0 = FFN0 + 2 * KF
    UNITS = DOWN0 + CS * ND
    assert DOWN_PARTS[1] == 8
    assert UNITS % 2 == 0 and DOWN0 % 2 == 0 and FFN0 % 2 == 0 and (2 * ND) % 2 == 0
    UH = UNITS // 2
    GROUPS = DOWN0
    DPARTS = CS * ND

    x_t = x.rearrange("o (n p) d -> (o n) p d", p=P)
    x_half = x.rearrange("o (n p) (h d) -> (o n) h p d", p=P, h=2)
    out_t = out.rearrange("o (n p) d -> (o n) p d", p=P)
    w_in_k = w_in.rearrange("o (k p) n -> (o p) k n", p=P)
    w_out_k = w_out.rearrange("o (k p) n -> (o p) k n", p=P)
    w_gate_k = w_gate.rearrange("o (k p) n -> (o p) k n", p=P)
    w_up_k = w_up.rearrange("o (k p) n -> (o p) k n", p=P)
    w_down_k = w_down.rearrange("o (k p) n -> (o p) k n", p=P)

    with ExitStack() as ctx:
        def sb(name, shape, dt=F32):
            return ctx.enter_context(nc.sbuf_tensor(name, shape, dt))

        def sem(name):
            return ctx.enter_context(nc.semaphore(name))

        def sems(name, n):
            return [sem(f"{name}{i}") for i in range(n)]

        h = sb("h", [P, KD, T])
        uhi = sb("uhi", [P, KD, T], F32R)
        ulo = sb("ulo", [P, KD, T], F32R)
        raw = [sb(f"raw{i}", [P, 8, P]) for i in range(2)]
        whi = [sb(f"whi{i}", [P, 8, P], F32R) for i in range(2)]
        wlo = [sb(f"wlo{i}", [P, 8, P], F32R) for i in range(2)]
        xs = [sb(f"xs{i}", [P, D]) for i in range(2)]
        os_ = [sb(f"os{i}", [P, D]) for i in range(2)]
        keyz = sb("keyz", [P, KV, 2, T + BLOCK])
        vals = sb("vals", [P, TB + 1, KV * 64])
        kstz = sb("kstz", [P, TB, 2, P])
        g1row = sb("g1row", [P, D])
        state = sb("state", [P, HEADS, P])
        gu = [sb(f"gu{i}", [P, T]) for i in range(2)]
        dist = sb("dist", [P, 2 * BLOCK])
        dist0 = sb("dist0", [P, 2 * BLOCK])
        ident = sb("ident", [P, P])
        ones = sb("ones", [P, P])
        causal = sb("causal", [P, P])
        g2 = sb("g2", [P, KD]); gf = sb("gf", [P, KD])
        ga = sb("ga", [P, HEADS]); gb = sb("gb", [P, PAIRS])
        lbl = sb("lbl", [P, 2, HEADS]); lbs = sb("lbs", [P, 4, HEADS])
        f_mul = sb("f_mul", [P, HEADS]); f_add = sb("f_add", [P, HEADS])
        sinks = sb("sinks", [P, 8]); nsinks = sb("nsinks", [P, 8])
        epst = sb("epst", [P, 1])
        xss = sb("xss", [P, 1]); xnrm = sb("xnrm", [P, 1]); xrn = sb("xrn", [P, 1])
        nrm = sb("nrm", [P, TB]); rnrm = sb("rnrm", [P, TB])
        hnrm = sb("hnrm", [P, TB]); hrnrm = sb("hrnrm", [P, TB])
        snrm = sb("snrm", [P, TB]); srnrm = sb("srnrm", [P, TB])
        mx = sb("mx", [P, 2]); nm = sb("nm", [P, 2, 2]); nms = sb("nms", [P, 2])
        es = sb("es", [P, 2]); rs = sb("rs", [P, 2, 2]); den = sb("den", [P, 2]); rd = sb("rd", [P, 2])

        act_at = nc.sbuf_base
        act_at = (act_at + 31) // 32 * 32
        ctx.enter_context(nc.sbuf_tensor("arena", [P, 2 * KF, T], F32))
        ahi = nc.alloc_sbuf_tensor_at("ahi", [P, KF, T], F32R, offset=act_at)
        alo = nc.alloc_sbuf_tensor_at("alo", [P, KF, T], F32R, offset=act_at + KF * T * 4)
        yhi, ylo = ahi, alo
        free_tiles = [act_at + 4 * T * k for k in list(range(KD, KF)) + list(range(KF + KD, 2 * KF))]
        if len(free_tiles) < 28:
            extra = ctx.enter_context(nc.sbuf_tensor("extra", [P, 28 - len(free_tiles), T], F32))
            base = nc.sbuf_base - 4 * T * (28 - len(free_tiles))
            free_tiles += [base + 4 * T * k for k in range(28 - len(free_tiles))]

        def tile(name, shape=(P, T)):
            return nc.alloc_sbuf_tensor_at(name, list(shape), F32, offset=free_tiles.pop(0))

        forget, key, cuminv, gateq, ivT, iv, sqo = (
            tile(n) for n in ("forget", "key", "cuminv", "gateq", "ivT", "iv", "sqo"))
        kstate = forget
        amask = tile("amask", (P, TB, P))
        cum = [tile(f"cum{i}") for i in range(2)]
        qdec = [tile(f"qdec{i}") for i in range(2)]
        gate = [tile(f"gate{i}") for i in range(2)]
        qT = [tile(f"qT{i}") for i in range(PAIRS)]
        pr = [tile(f"pr{i}") for i in range(2)]
        pT = [tile(f"pT{i}") for i in range(2)]
        oT = [tile(f"oT{i}") for i in range(PAIRS)]
        st = [tile(f"st{i}", (P, 4, P)) for i in range(2)]
        xdump = os_[1]
        *first_x, first_dump = (nc.alloc_sbuf_tensor_at(f"first{b}", [P, D], F32, offset=act_at + 4 * D * b)
                                for b in range(TB + 1))
        xh = [xs[q // 2][:, (q % 2) * (D // 2):(q % 2 + 1) * (D // 2)] for q in range(4)]
        upn = xs[1][:, 0:T]
        sqs = gu
        factors = os_[1][:, 0:T]
        sacc = os_[0]
        M = [ctx.enter_context(nc.psum_tensor(f"M{i}", [P, T], F32)) for i in range(4)]
        X = [ctx.enter_context(nc.psum_tensor(f"X{i}", [P, T], F32)) for i in range(4)]

        LAST_BANKS = (X[2:4], M[2:4], M[0:2], X[0:2])
        s_par = sem("s_par")
        s_idn = sem("s_idn")
        s_ini = sem("s_ini")
        s_ini2 = sem("s_ini2")
        s_ini3 = sem("s_ini3")
        s_dst = sem("s_dst")
        s_g1 = sem("s_g1")
        s_raw = sems("s_raw", 2)
        s_x0 = sems("s_x0_", TB)
        s_x = sem("s_x")
        s_out = sems("s_out", 2)
        s_hi = sems("s_hi", 2)
        s_lo = sems("s_lo", 2)
        s_group = sem("s_group")
        s_dpart = sem("s_dpart")

        s_xss = sem("s_xss")
        s_xroot = sem("s_xroot")
        s_xr = sem("s_xr")
        s_xn = sem("s_xn")
        s_ptr0 = sem("s_ptr0")
        s_xh = sems("s_xh", 4)
        s_xtr = sem("s_xtr")
        s_xT = sem("s_xT")
        s_nsum = sem("s_nsum")
        s_root = sem("s_root")
        s_rroot = sem("s_rroot")
        s_xuhi = sem("s_xuhi")
        s_xulo = sem("s_xulo")
        s_uhi = sem("s_uhi")
        s_ulo = sem("s_ulo")
        s_kcar = sem("s_kcar")
        s_vcar = sem("s_vcar")
        s_k = sem("s_k")
        s_bvT = sem("s_bvT")
        s_vtr = sem("s_vtr")
        s_vals = sem("s_vals")
        s_q = sem("s_q")
        s_score = sem("s_score")
        s_bias = sem("s_bias")
        s_mx = sem("s_mx")
        s_nm = sem("s_nm")
        s_nms = sem("s_nms")
        s_exp = sem("s_exp")
        s_den = sem("s_den")
        s_rd = sem("s_rd")
        s_prob = sem("s_prob")
        s_ptr = sem("s_ptr")
        s_pT = sem("s_pT")
        s_pv = sem("s_pv")
        s_oT = sem("s_oT")
        s_osq = sem("s_osq")
        s_oacc = sem("s_oacc")
        s_ssum = sem("s_ssum")
        s_sroot = sem("s_sroot")
        s_srr = sem("s_srr")
        s_smul = sem("s_smul")
        s_yb = sem("s_yb")
        s_ybhi = sem("s_ybhi")
        s_yblo = sem("s_yblo")
        s_dist = sem("s_dist")
        s_tf = sem("s_tf")
        s_tq = sem("s_tq")
        s_iv = sem("s_iv")
        s_tg = sem("s_tg")
        s_f = sem("s_f")
        s_cum = sem("s_cum")
        s_inv = sem("s_inv")
        s_key0 = sem("s_key0")
        s_key = sem("s_key")
        s_kst = sem("s_kst")
        s_qs = sem("s_qs")
        s_qdec = sem("s_qdec")
        s_gs = sem("s_gs")
        s_ivtr = sem("s_ivtr")
        s_ivt = sem("s_ivt")
        s_ktr = sem("s_ktr")
        s_kz = sem("s_kz")
        s_a = sem("s_a")
        s_am = sem("s_am")
        s_upd = sem("s_upd")
        s_st = sem("s_st")
        s_scar = sem("s_scar")
        s_o = sem("s_o")
        s_sq = sem("s_sq")
        s_y1 = sem("s_y1")
        s_asum = sem("s_asum")
        s_aroot = sem("s_aroot")
        s_arr = sem("s_arr")
        s_amul = sem("s_amul")
        s_ya = sem("s_ya")
        s_yahi = sem("s_yahi")
        s_yalo = sem("s_yalo")
        s_h = sem("s_h")
        s_hsq = sem("s_hsq")
        s_hacc = sem("s_hacc")
        s_gate = sems("s_gate", 2)
        s_up = sems("s_up", 2)
        s_silu = sems("s_silu", 2)
        s_prod = sems("s_prod", 2)
        s_ahi = sems("s_ahi", 2)
        s_alo = sems("s_alo", 2)
        s_h2 = sems("s_h2", 2)
        s_h2sq = sems("s_h2sq", 2)
        s_h2acc = sems("s_h2acc", 2)
        s_fin = sems("s_fin", 2)
        s_ftr = sem("s_ftr")
        s_osa = sem("s_osa")
        s_osb = sem("s_osb")
        INI, DST = 10, 4

        block = ctx.enter_context(nc.Block())

        def wait_group_read(eng, it, slot):
            a, part = head_part(slot)
            if slot == K_SLOT:
                eng.wait_ge(s_k, it * 4 + 4)
            elif slot == V_SLOT:
                eng.wait_ge(s_bvT, it + 1)
            elif slot in Q_SLOT:
                eng.wait_ge(s_q, it * PAIRS + Q_SLOT.index(slot) + 1)
            else:
                eng.wait_ge((s_tf, s_qs, s_iv, s_gs)[part], it * HEADS + a + 1)

        def wait_unit_used(eng, it, n):
            eng.wait_ge(s_group, it * GROUPS + n - 1)

        def over_superblocks(eng, prologue, body):
            prologue()
            if NSB > 1:
                with eng.Fori(0, NSB - 1) as it:
                    body(it, False)
            body(NSB - 1, True)

        @block.sync
        def _(sp):
            sp.dma_start(g1row[:, :], ln1_g[0, :].partition_broadcast(P)).then_inc(s_g1, 16)

            def load(it, s, k, src, nb=8, dst=None):
                if not is_first(it * UH + k):
                    sp.wait_ge(s_lo[s], it * UH + k)
                sp.dma_start(raw[s][:, 0:nb, :] if dst is None else dst, src).then_inc(s_raw[s], 16)

            def load_x(it, b, dst, done):
                sp.dma_start(dst[:, :], x_t[bass.ds(it * TB + b, 1), :, :].rearrange("o p d -> (o p) d")
                             ).then_inc(done, 16)

            def load_half(it, half, b):
                if half:
                    sp.wait_ge(s_xtr, it * 2 * TB + b + 1)
                else:
                    sp.wait_ge(s_ptr0, it * 2 * TB + 2 * TB)
                sp.dma_start(xh[b], x_half[bass.ds(it * TB + b, 1), half:half + 1, :, :].rearrange("o h p d -> (o h p) d")
                             ).then_inc(s_xh[b], 16)

            def load_in(it, units):
                for n in units:
                    load(it, n % 2, n // 2, w_in_k[:, :, column_of(n):column_of(n) + P])

            for b in range(2):
                load_x(0, b, first_x[b], s_x0[b])
            load_in(0, (0,))
            for dst, src in ((g2, ln2_g), (ga, hgrn_norm_g), (gb, attn_norm_g)):
                sp.dma_start(dst[:, :], src.rearrange("o (k p) -> p (o k)", p=P),
                             allow_slow_non_contiguous=True).then_inc(s_par, 16)
            sp.dma_start(gf[:, :], final_g.rearrange("(k p) -> p k", p=P),
                         allow_slow_non_contiguous=True).then_inc(s_par, 16)
            for l in range(2):
                sp.dma_start(lbl[:, l, :], lb_logits[l, :].rearrange("(k p) -> p k", p=P),
                             allow_slow_non_contiguous=True).then_inc(s_par, 16)
            sp.dma_start(sinks[:, :], attn_sinks[0, :].partition_broadcast(P)).then_inc(s_par, 16)

            def prologue():
                load_in(0, (1,))
                for b in range(2, TB):
                    load_x(0, b, first_x[b], s_x0[b])
                load_in(0, range(2, SPLIT + 2))

            def body(it, final):
                for n in range(SPLIT + 2, IN_GROUPS):
                    load_in(it, (n,))
                    if n >= IN_GROUPS - TB:
                        load_half(it, 0, n - (IN_GROUPS - TB))
                for n in range(OUT_A, OUT_B):
                    k0, k1 = A_KS[n - OUT_A]
                    load(it, n % 2, n // 2, w_out_k[:, k0:k1 + 1:k1 - k0, 0:4 * P],
                         dst=raw[n % 2][:, :, :].rearrange("p (k c) n -> p k (c n)", k=2))
                for c in range(4, CS):
                    n = OUT_B + c - 4
                    load_half(it, 1, c - 4)
                    load(it, n % 2, n // 2, w_out_k[:, :, c * P:(c + 1) * P])
                with sp.Fori(0, KF) as j:
                    load(it, 0, j + FFN0 // 2, w_gate_k[:, :, bass.ds(j * P, P)])
                    load(it, 1, j + FFN0 // 2, w_up_k[:, :, bass.ds(j * P, P)])
                with sp.Fori(0, CS // 2) as cc:
                    if not final:
                        sp.wait_ge(s_xtr, it * 2 * TB + 2 * TB)
                        sp.wait_ge(s_xn, (it + 1) * TB + cc + 1)
                        load_x(it + 1, cc, xs[0], s_x)
                    for m in range(2 * ND):
                        half, part = divmod(m, ND)
                        k0, nb = 8 * part, DOWN_PARTS[part]
                        load(it, m % 2, cc * ND + DOWN0 // 2 + m // 2,
                             w_down_k[:, k0:k0 + nb, bass.ds(cc * 2 * P + half * P, P)], nb)
                if not final:
                    load_in(it + 1, range(SPLIT + 2))

            over_superblocks(sp, prologue, body)

        @block.tensor
        def _(pe):
            mm, tr = nc.tensor.matmul, nc.tensor.transpose

            def product(bank, s, hi, lo, kb, first, last):
                mm(bank, whi[s][:, kb, :], hi, start=first, stop=False)
                mm(bank, whi[s][:, kb, :], lo, start=False, stop=False)
                return mm(bank, wlo[s][:, kb, :], hi, start=False, stop=last)

            def spread(bank, factors, done):
                for b in range(TB):
                    last = mm(bank[:, b * P:(b + 1) * P], factors[:, b:b + 1].broadcast_to([P, P]), ident[:, :],
                              start=True, stop=True)
                last.then_inc(done, 1)

            def sums_spread(bank, squares, done):
                mm(bank[:, :], ones[:, :], squares, start=True, stop=True).then_inc(done, 1)

            def sums(bank, squares, done):
                for b in range(TB):
                    last = mm(bank[:, b:b + 1], squares[:, b * P:(b + 1) * P], ones[:, 0:1], start=True, stop=True)
                last.then_inc(done, 1)

            def prep(it, b, tile=xs[1]):
                pe.wait_ge(s_xn, it * TB + b + 2)
                for half in range(2):
                    if not is_first(it * 2 * TB + 2 * b):
                        pe.wait_ge(s_xulo, it * 2 * TB + 2 * b - 1 + half)
                    for c in range(4):
                        k = 4 * half + c
                        last = tr(X[2 + half][:, c * P:(c + 1) * P], tile[:, k * P:(k + 1) * P], ident[:, :])
                    last.then_inc(s_ptr0, 1)

            def group(it, slot):
                if slot >= 3:
                    wait_group_read(pe, it, slot - 3)
                elif slot < 2:
                    pe.wait_ge(s_h2[slot], it * (KD // 2) + 1)
                pe.wait_ge(s_lo[slot % 2], it * UH + slot // 2 + 1)
                if slot == 0:
                    pe.wait_ge(s_xulo, it * 2 * TB + 2 * TB)
                for k in range(KD):
                    last = product(M[slot % 3][:, :], slot % 2, uhi[:, k, :], ulo[:, k, :], k,
                                   k == 0, k == KD - 1)
                last.then_inc(s_group, 1)

            def out_a(it, k, first, last_k):
                n = [k in ks for ks in A_KS].index(True)
                unit = OUT_A + n
                kk = A_KS[n].index(k)
                if k < HEADS:
                    pe.wait_ge(s_yalo, it * HEADS + k + 1)
                else:
                    pe.wait_ge(s_yblo, it * PAIRS + k - HEADS + 1)
                pe.wait_ge(s_lo[unit % 2], it * UH + unit // 2 + 1)
                for c in (1, 2, 0, 3):
                    if first and c < 3:
                        wait_group_read(pe, it, {1: 19, 2: 20, 0: 21}[c])
                    if first and c == 3:
                        pe.wait_ge(s_oT, it * PAIRS + PAIRS)
                    last = product(M[c][:, :], unit % 2, yhi[:, k, :], ylo[:, k, :], 4 * kk + c, first, last_k)
                return last

            def v_values(it):
                pe.wait_ge(s_bvT, it + 1)
                if not is_first(it):
                    pe.wait_ge(s_rroot, it * 2)
                for b in range(TB):
                    last = tr(X[1][:, b * P:(b + 1) * P], ivT[:, b * P:(b + 1) * P], ident[:, :])
                last.then_inc(s_vtr, 1)

            def scores(it, i):
                p, b = divmod(i, TB)
                if i == 0:
                    pe.wait_ge(s_k, it * 4 + 4)
                if b == 0:
                    pe.wait_ge(s_q, it * PAIRS + p + 1)
                if i:
                    pe.wait_ge(s_bias, it * STEPS + i)
                for par in range(2):
                    last = mm(X[0][:, par * 2 * BLOCK:(par + 1) * 2 * BLOCK], qT[p][:, b * P:(b + 1) * P],
                              keyz[:, p // 2, par, b * P:b * P + 2 * BLOCK], start=True, stop=True)
                last.then_inc(s_score, 1)

            def p_turn(it, i):
                pe.wait_ge(s_prob, it * STEPS + i + 1)
                if i:
                    pe.wait_ge(s_pT, it * STEPS + i)
                else:
                    pe.wait_ge(s_vals, it + 1)
                for n in range(4):
                    last = tr(X[1][:, n * P:(n + 1) * P], pr[i % 2][:, n * P:(n + 1) * P], ident[:, :])
                last.then_inc(s_ptr, 1)

            def pv(it, i):
                p, b = divmod(i, TB)
                g = p // 2
                pe.wait_ge(s_pT, it * STEPS + i + 1)
                if b == 0 and p:
                    pe.wait_ge(s_oT, it * PAIRS + p)
                for par in range(2):
                    for kb in range(2):
                        last = mm(M[3][64 * par:64 * par + 64, b * P:(b + 1) * P],
                                  vals[:, b + kb, 64 * g:64 * g + 64],
                                  pT[i % 2][:, (2 * par + kb) * P:(2 * par + kb + 1) * P],
                                  start=(kb == 0), stop=(kb == 1))
                last.then_inc(s_pv, 1)

            def iv_turn(it, a):
                pe.wait_ge(s_iv, it * HEADS + a + 1)
                if a:
                    pe.wait_ge(s_ya, it * HEADS + a)
                else:
                    pe.wait_ge(s_osb, it * TB + 1)
                for b in range(TB):
                    last = tr(X[3][:, b * P:(b + 1) * P], ivT[:, b * P:(b + 1) * P], ident[:, :])
                last.then_inc(s_ivtr, 1)

            def keys(it, a):
                pe.wait_ge(s_key, it * HEADS + a + 1)
                pe.wait_ge(s_qdec, it * HEADS + a + 1)
                if a:
                    pe.wait_ge(s_y1, it * HEADS + a)
                else:
                    pe.wait_ge(s_osa, it * TB + 1)
                for b in range(TB):
                    last = mm(X[2][:, b * P:(b + 1) * P], key[:, b * P:(b + 1) * P],
                              qdec[a % 2][:, b * P:(b + 1) * P], start=True, stop=True)
                last.then_inc(s_a, 1)

            def key_turn(it, a):
                pe.wait_ge(s_kst, it * HEADS + a + 1)
                pe.wait_ge(s_ivt, it * HEADS + a + 1)
                for b in range(TB):
                    last = tr(X[3][:, b * P:(b + 1) * P], kstate[:, b * P:(b + 1) * P], ident[:, :])
                last.then_inc(s_ktr, 1)

            def update(it, a):
                pe.wait_ge(s_kz, it * 2 * HEADS + 2 * a + 2)
                pe.wait_ge(s_am, it * HEADS + a + 1)
                for half in range(2):
                    for n in range(4):
                        b, c = divmod(4 * half + n, 2)
                        last = mm(X[2 + half][:, n * P:(n + 1) * P], kstz[:, b, c, :], iv[:, b * P:(b + 1) * P],
                                  start=True, stop=True)
                    last.then_inc(s_upd, 1)

            def output(it, a):
                pe.wait_ge(s_st, it * NCH * HEADS + NCH * a + 4)
                for b in range(TB):
                    mm(X[2][:, b * P:(b + 1) * P], iv[:, b * P:(b + 1) * P], amask[:, b, :],
                       start=(b == 0), stop=False, skip_group_check=True)
                for n in range(NCH):
                    if n > 4:
                        pe.wait_ge(s_st, it * NCH * HEADS + NCH * a + n)
                    before = state[:, a, :] if n == 0 else st[(n - 1) // 4][:, (n - 1) % 4, :]
                    last = mm(X[2][:, n * CHUNK:(n + 1) * CHUNK], before,
                              qdec[a % 2][:, n * CHUNK:(n + 1) * CHUNK],
                              start=False, stop=(n == NCH - 1), skip_group_check=True)
                last.then_inc(s_o, 1)

            def head_sum(it, a):
                pe.wait_ge(s_sq, it * HEADS + a + 1)
                pe.wait_ge(s_st, it * NCH * HEADS + NCH * a + NCH)
                sums(X[3], sqo, s_asum)

            def head_mul(it, a):
                pe.wait_ge(s_arr, it * HEADS + a + 1)
                spread(X[3], hrnrm, s_amul)

            def x_turn(it, j):
                half, b = divmod(j, TB)
                pe.wait_ge(s_xh[b], it * 32 + 16 * half + 16)
                if j:
                    pe.wait_ge(s_xT, it * 2 * TB + j)
                else:
                    pe.wait_ge(s_bias, it * STEPS + STEPS)
                for c in range(4):
                    last = tr(X[0][:, c * P:(c + 1) * P], xh[b][:, c * P:(c + 1) * P], ident[:, :])
                last.then_inc(s_xtr, 1)

            def final_sum(it):
                for half in range(2):
                    pe.wait_ge(s_h2acc[half], it * (KD // 2) + KD // 2 + 1)
                sums(X[1], sacc, s_nsum)

            def final_turn(it, b, banks):
                for s in s_fin:
                    pe.wait_ge(s, it * (KD // 2) + KD // 2)
                for half, bank in enumerate(banks):
                    for c in range(4):
                        last = tr(bank[:, c * P:(c + 1) * P], h[:, 4 * half + c, b * P:(b + 1) * P],
                                  ident[:, :])
                    last.then_inc(s_ftr, 1)

            def slots(it, first, end, former=None):
                for slot in range(first, end):
                    if slot < IN_GROUPS:
                        group(it, slot)
                    for k in A_PLAN.get(slot, ()):
                        last = out_a(it, k, k == A_PLAN[OUT_A][0], k == A_PLAN[SLOTS - 1][-1])
                        if k in A_LAST:
                            last.then_inc(s_group, 1)
                        if k == A_PLAN[OUT_A][0]:
                            key_turn(it, HEADS - 1)
                    a = head_at(slot, NORM_MUL)
                    if a is not None:
                        head_mul(it, a)
                    a = head_at(slot, UPDATE)
                    if a is not None and slot != OUT_A:
                        key_turn(it, a)
                    if slot == BV_TURN:
                        v_values(it)
                    if slot == SWA_SUM:
                        pe.wait_ge(s_oacc, it * (PAIRS - 1) + PAIRS - 1)
                        sums(X[1], qT[0], s_ssum)
                    if slot == SWA_MUL:
                        pe.wait_ge(s_srr, it + 1)
                        spread(X[1], srnrm, s_smul)
                    for begin, step in ((SCORE, scores), (P_TURN, p_turn), (PV, pv)):
                        i = step_at(slot, begin)
                        if i is not None:
                            step(it, i)
                    for offset, step in ((KEYS, keys), (V_TURN, iv_turn), (UPDATE, update), (OUTPUT, output),
                                         (NORM_SUM, head_sum)):
                        a = head_at(slot, offset)
                        if a is not None:
                            step(it, a)
                    if former is not None:
                        if slot == FINAL_SUM:
                            final_sum(former)
                        b = slot - FINAL_TURN
                        if 0 <= b < TB:
                            if b:
                                pe.wait_ge(s_osa, former * TB + b + 1)
                                pe.wait_ge(s_osb, former * TB + b + 1)
                            final_turn(former, b, X[2:4])
                    if 0 <= slot - XT_SLOT < 2 * TB:
                        x_turn(it, slot - XT_SLOT)

            def out_b(it):
                for c, bank in zip(range(4, CS), (1, 2, 3, 0)):
                    n = OUT_B + c - 4
                    if bank == 1:
                        pe.wait_ge(s_yb, it * PAIRS + PAIRS)
                    if bank == 0:
                        pe.wait_ge(s_xT, it * 2 * TB + 2 * TB)
                    pe.wait_ge(s_lo[n % 2], it * UH + n // 2 + 1)
                    for k in range(KD):
                        last = product(X[bank][:, :], n % 2, yhi[:, k, :], ylo[:, k, :], k, k == 0, k == KD - 1)
                    last.then_inc(s_group, 1)

            def ffn_group(it, jj, n):
                pe.wait_ge(s_lo[n % 2], it * UH + FFN0 // 2 + 2 * jj + n // 2 + 1)
                for k in range(KD):
                    if is_first(jj) and n == 0:
                        pe.wait_ge(s_ulo, it * KD + k + 1)
                    last = product(M[n][:, :], n % 2, uhi[:, k, :], ulo[:, k, :], k, k == 0, k == KD - 1)
                last.then_inc(s_group, 1)

            def body(it, final):
                slots(it, SPLIT, SLOTS)
                out_b(it)
                for n in range(4):
                    ffn_group(it, 0, n)
                    if n == 1:
                        pe.wait_ge(s_hacc, it * KD + KD)
                        sums_spread(X[0], sacc[:, 0:T], s_nsum)
                with pe.Fori(1, KF // 2) as jj:
                    for n in range(4):
                        pe.wait_ge((s_gate, s_up)[n % 2][n // 2], it * (KF // 2) + jj)
                        ffn_group(it, jj, n)
                with pe.Fori(0, CS // 2) as cc:
                    for half in range(2):
                        pe.wait_ge(s_h2[half], it * (KD // 2) + cc + 1)
                        for part in range(ND):
                            m = half * ND + part
                            pe.wait_ge(s_lo[m % 2], it * UH + DOWN0 // 2 + cc * ND + m // 2 + 1)
                            if part in (0, ND - 1):
                                for j in range(2):
                                    pe.wait_ge(s_alo[j], it * (KF // 2) + KF // 2 - (part == 0))
                            for kb in range(DOWN_PARTS[part]):
                                k = 8 * part + kb
                                last = product(M[half][:, :], m % 2, ahi[:, k, :], alo[:, k, :], kb,
                                               k == 0, k == KF - 1)
                            last.then_inc(s_dpart, 1)
                            if m == PREP_PART and not final:
                                prep(it + 1, cc)
                if not final:
                    slots(it + 1, 0, SPLIT, it)
                else:
                    final_turn(it, 0, LAST_BANKS[0])
                    final_sum(it)
                    for b in range(1, TB):
                        if b == TB - 1:
                            pe.wait_ge(s_rroot, it * 2 + 2)
                        final_turn(it, b, LAST_BANKS[b])

            def prologue():
                pe.wait_ge(s_idn, 3)
                for b in range(TB):
                    prep(0, b, first_x[b])
                pe.wait_ge(s_ini, INI)
                slots(0, 0, SPLIT)

            over_superblocks(pe, prologue, body)

        @block.scalar
        def _(act):
            A = nc.scalar.activation
            act.sem_inc(s_osa, 1)
            for q in s_out:
                act.sem_inc(q, 16)

            def make_hi(it, s, k, nb=8):
                act.wait_ge(s_raw[s], it * (UH * 16) + k * 16 + 16)
                A(whi[s][:, 0:nb, :], raw[s][:, 0:nb, :], ACT.Copy).then_inc(s_hi[s], 1)

            def prep(it, b, src=xs[0], dump=xdump):
                if is_first(it):
                    act.wait_ge(s_x0[b], 16)
                else:
                    act.wait_ge(s_x, (it - 1) * (TB * 16) + b * 16 + 16)
                if not is_first(it * TB + b):
                    act.wait_ge(s_xr, it * TB + b)
                A(dump[:, :], src[:, :], ACT.Square, accum_out=xss[:, :]).then_inc(s_xss, 1)
                act.wait_ge(s_xss, it * TB + b + 1)
                A(xnrm[:, :], xss[:, :], ACT.Sqrt, scale=1.0 / D, bias=epst[:, 0:1]).then_inc(s_xroot, 1)

            def first_hi(b):
                for half in range(2):
                    act.wait_ge(s_ptr0, 2 * b + half + 1)
                    A(uhi[:, 4 * half:4 * half + 4, b * P:(b + 1) * P],
                      X[2 + half][:, :].rearrange("p (c t) -> p c t", c=4), ACT.Copy).then_inc(s_xuhi, 1)

            def head_group(it, a, part, bank):
                if part == 0:
                    if a:
                        act.wait_ge(s_ktr, it * HEADS + a)
                    A(forget[:, :], bank, ACT.Tanh, scale=0.5).then_inc(s_tf, 1)
                if part == 1:
                    if a:
                        act.wait_ge(s_qdec, it * HEADS + a)
                    A(gateq[:, :], bank, ACT.Tanh, scale=0.5).then_inc(s_tq, 1)
                if part == 2:
                    if a:
                        act.wait_ge(s_ivtr, it * HEADS + a)
                    A(ivT[:, :], bank, ACT.Copy).then_inc(s_iv, 1)
                if part == 3:
                    if a >= 2:
                        act.wait_ge(s_yalo, it * HEADS + a - 1)
                    A(gate[a % 2][:, :], bank, ACT.Tanh, scale=0.5).then_inc(s_tg, 1)

            def iv_turn(it, a):
                act.wait_ge(s_ivtr, it * HEADS + a + 1)
                if a:
                    act.wait_ge(s_o, it * HEADS + a)
                A(iv[:, :], X[3][:, :], ACT.Copy).then_inc(s_ivt, 1)

            def key_turn(it, a):
                act.wait_ge(s_ktr, it * HEADS + a + 1)
                if a:
                    act.wait_ge(s_upd, it * 2 * HEADS + 2 * a)
                for c in range(2):
                    r = slice(64 * c, 64 * c + 64)
                    A(kstz[r, :, c, :], X[3][r, :].rearrange("p (b k) -> p b k", b=TB),
                      ACT.Copy).then_inc(s_kz, 1)

            def output(it, a):
                act.wait_ge(s_o, it * HEADS + a + 1)
                if a:
                    act.wait_ge(s_asum, it * HEADS + a)
                A(sqo[:, :], X[2][:, :], ACT.Square).then_inc(s_sq, 1)

            def head_sum(it, a):
                act.wait_ge(s_asum, it * HEADS + a + 1)
                if a:
                    act.wait_ge(s_arr, it * HEADS + a)
                A(hnrm[:, :], X[3][:, 0:TB], ACT.Sqrt, scale=1.0 / P, bias=epst[:, 0:1]).then_inc(s_aroot, 1)

            def head_mul(it, a):
                act.wait_ge(s_ya, it * HEADS + a + 1)
                A(yhi[:, a, :], gate[a % 2][:, :], ACT.Copy).then_inc(s_yahi, 1)

            def scores(it, i):
                w = i % 2
                act.wait_ge(s_nms, it * STEPS + i + 1)
                if i:
                    act.wait_ge(s_den, it * STEPS + i)
                for par in range(2):
                    half = pr[w][:, par * 256:(par + 1) * 256]
                    A(half, half, ACT.Exp, scale=0.125, bias=nm[:, w, par:par + 1],
                      accum_out=rs[:, w, par:par + 1])
                A(es[:, :], nms[:, :], ACT.Exp).then_inc(s_exp, 1)

            def p_turn(it, i):
                act.wait_ge(s_ptr, it * STEPS + i + 1)
                if i >= 2:
                    act.wait_ge(s_pv, it * STEPS + i - 1)
                A(pT[i % 2][:, :], X[1][:, :], ACT.Copy).then_inc(s_pT, 1)

            def pv(it, i):
                if i % TB == TB - 1:
                    p = i // TB
                    act.wait_ge(s_oT, it * PAIRS + p + 1)
                    A(qT[p][:, :], oT[p][:, :], ACT.Square).then_inc(s_osq, 1)

            def swa_hi(it, p):
                act.wait_ge(s_yb, it * PAIRS + p + 1)
                A(yhi[:, HEADS + p, :], oT[p][:, :], ACT.Copy).then_inc(s_ybhi, 1)

            def x_turn(it, j):
                half, b = divmod(j, TB)
                act.wait_ge(s_xtr, it * 2 * TB + j + 1)
                A(h[:, 4 * half:4 * half + 4, b * P:(b + 1) * P],
                  X[0][:, :].rearrange("p (c t) -> p c t", c=4), ACT.Copy).then_inc(s_xT, 1)

            def final_sum(it):
                act.wait_ge(s_nsum, it * 2 + 2)
                act.wait_ge(s_rroot, it * 2 + 1)
                A(nrm[:, :], X[1][:, 0:TB], ACT.Sqrt, scale=1.0 / D, bias=epst[:, 0:1]).then_inc(s_root, 1)

            def final_turn(it, b, banks):
                act.wait_ge(s_rroot, it * 2 + 2)
                act.wait_ge(s_ftr, it * 2 * TB + 2 * b + 1)
                act.wait_ge(s_out[b % 2], it * 32 + 16 * (b // 2) + 16)
                A(os_[b % 2][:, 0:D // 2], banks[0][:, :], ACT.Copy, scale=rnrm[:, b:b + 1]).then_inc(s_osa, 1)

            def store(it, b):
                act.wait_ge(s_osa, it * TB + b + 2)
                act.wait_ge(s_osb, it * TB + b + 2)
                act.dma_start(out_t[bass.ds(it * TB + b, 1), :, :].rearrange("o p d -> (o p) d"),
                              os_[b % 2][:, :]).then_inc(s_out[b % 2], 16)

            def slots(it, first, end, former=None):
                for slot in range(first, end):
                    a = head_at(slot, UPDATE)
                    if a is not None:
                        key_turn(it, a)
                    n = unit_made_at(slot)
                    if n is not None:
                        wait_unit_used(act, it, n)
                        make_hi(it, n % 2, n // 2)
                    bank = M[slot % 3][:, :]
                    if slot < IN_GROUPS:
                        act.wait_ge(s_group, it * GROUPS + slot + 1)
                    if slot == V_SLOT:
                        A(ivT[:, :], bank, ACT.Copy).then_inc(s_bvT, 1)
                    if slot == BV_TURN:
                        act.wait_ge(s_vtr, it + 1)
                        act.wait_ge(s_vcar, it + 1)
                        A(vals[:, 1:TB + 1, :], X[1][:, :].rearrange("p (b k) -> p b k", b=TB),
                          ACT.Copy).then_inc(s_vals, 1)
                    if slot in Q_SLOT:
                        A(qT[Q_SLOT.index(slot)][:, :], bank, ACT.Copy).then_inc(s_q, 1)
                    a, part = head_part(slot)
                    if a is not None:
                        head_group(it, a, part, bank)
                    a = head_at(slot, NORM_MUL)
                    if a is not None:
                        head_mul(it, a)
                    if slot == SWA_SUM:
                        act.wait_ge(s_ssum, it + 1)
                        A(snrm[:, :], X[1][:, 0:TB], ACT.Sqrt, scale=1.0 / (PAIRS * P),
                          bias=epst[:, 0:1]).then_inc(s_sroot, 1)
                    if slot == SWA_MUL:
                        swa_hi(it, 0)
                    for begin, step in ((P_TURN, p_turn), (SCORE, scores), (PV, pv)):
                        i = step_at(slot, begin)
                        if i is not None:
                            step(it, i)
                    for offset, step in ((V_TURN, iv_turn), (OUTPUT, output), (NORM_SUM, head_sum)):
                        a = head_at(slot, offset)
                        if a is not None:
                            step(it, a)
                    if former is not None:
                        if slot == FINAL_SUM:
                            final_sum(former)
                        if 0 <= slot - FINAL_TURN < TB:
                            final_turn(former, slot - FINAL_TURN, X[2:4])
                            store(former, slot - FINAL_TURN)
                    if 0 <= slot - XT_SLOT < 2 * TB:
                        x_turn(it, slot - XT_SLOT)
                    if slot == SWA_MUL:
                        for p in range(1, PAIRS):
                            swa_hi(it, p)

            def out_b(it):
                wait_unit_used(act, it, OUT_B + 1)
                make_hi(it, (OUT_B + 1) % 2, (OUT_B + 1) // 2)
                for c in range(CS):
                    n = OUT_B + 2 + c - 4
                    if c >= 4:
                        wait_unit_used(act, it, n)
                        make_hi(it, n % 2, n // 2)
                    act.wait_ge(s_h, it * KD + c + 1)
                    A(uhi[:, c, :], h[:, c, :], ACT.Copy, scale=g2[:, c:c + 1]).then_inc(s_uhi, 1)
                    if c >= 2:
                        act.wait_ge(s_hacc, it * KD + c - 1)
                    A(sqs[c % 2][:, :], h[:, c, :], ACT.Square).then_inc(s_hsq, 1)

            def ffn_hi(it, jj, m):
                act.wait_ge(s_group, it * GROUPS + FFN0 + 4 * jj + m + 1)
                make_hi(it, m % 2, 2 * jj + (FFN0 + 2 + m) // 2)

            def silu(it, jj, j):
                act.wait_ge(s_gate[j], it * (KF // 2) + jj + 1)
                A(gu[j][:, :], gu[j][:, :], ACT.Silu).then_inc(s_silu[j], 1)

            def down_his(it, cc, units):
                for m in units:
                    act.wait_ge(s_dpart, it * DPARTS + cc * (2 * ND) + m - 1)
                    make_hi(it, m % 2, cc * ND + DOWN0 // 2 + m // 2, DOWN_PARTS[m % ND])

            def body(it, final):
                slots(it, SPLIT, SLOTS)
                out_b(it)
                ffn_hi(it, 0, 0)
                ffn_hi(it, 0, 1)
                act.wait_ge(s_nsum, it * 2 + 1)
                act.wait_ge(s_out[1], it * 32 + 16)
                A(factors, X[0][:, :], ACT.Sqrt, scale=1.0 / D, bias=epst[:, 0:1]).then_inc(s_root, 1)
                ffn_hi(it, 0, 2)
                silu(it, 0, 0)
                silu(it, 0, 1)
                ffn_hi(it, 0, 3)
                with act.Fori(1, KF // 2) as jj:
                    for m in range(4):
                        ffn_hi(it, jj, m)
                        if m % 2 == 0:
                            silu(it, jj, m // 2)
                if not final:
                    with act.Fori(0, CS // 2) as cc:
                        down_his(it, cc, range(2, 4))
                        act.wait_ge(s_alo[1], (it + 1) * (KF // 2))
                        act.wait_ge(s_out[1], it * 32 + 16)
                        prep(it + 1, cc)
                        down_his(it, cc, range(4, 2 * ND + 2))
                    slots(it + 1, 0, SPLIT, it)
                else:
                    with act.Fori(0, CS // 2 - 1) as cc:
                        down_his(it, cc, range(2, 2 * ND + 2))
                    down_his(it, CS // 2 - 1, range(2, 2 * ND))
                    A(xnrm[:, :], epst[:, :], ACT.Sqrt).then_inc(s_ini3, 1)
                    final_sum(it)
                    for b in range(TB):
                        final_turn(it, b, LAST_BANKS[b])
                        store(it, b)
                    for q in s_out:
                        act.wait_ge(q, NSB * 32 + 16)

            def prologue():
                act.wait_ge(s_idn, 3)
                A(nrm[:, 0:1], epst[:, :], ACT.Sqrt).then_inc(s_ini3, 1)
                for b in range(TB):
                    prep(0, b, first_x[b], first_dump)
                    if b:
                        first_hi(b - 1)
                    if b < 2:
                        make_hi(0, b, 0)
                first_hi(TB - 1)
                act.wait_ge(s_ini, INI)
                act.wait_ge(s_ini2, 3)
                A(lbs[:, 0:2, :], lbs[:, 2:4, :], ACT.Exp).then_inc(s_ini3, 1)
                slots(0, 0, SPLIT)

            over_superblocks(act, prologue, body)

        @block.vector
        def _(dve):
            V = nc.vector
            for s in (*s_h2, s_xn, s_osb):
                dve.sem_inc(s, 1)

            def parameters():
                dve.wait_ge(s_par, 7 * 16)
                V.tensor_tensor(f_mul[:, :], lbl[:, 0, :], lbl[:, 1, :], ALU.max).then_inc(s_ini2, 1)
                dve.wait_ge(s_ini2, 1)
                for l in range(2):
                    V.tensor_tensor(lbs[:, 2 + l, :], lbl[:, l, :], f_mul[:, :], ALU.subtract).then_inc(s_ini2, 1)
                dve.wait_ge(s_ini3, 2)
                V.tensor_tensor(f_add[:, :], lbs[:, 0, :], lbs[:, 1, :], ALU.add).then_inc(s_ini2, 1)
                dve.wait_ge(s_ini2, 4)
                V.reciprocal(f_mul[:, :], f_add[:, :]).then_inc(s_ini2, 1)
                dve.wait_ge(s_ini2, 5)
                V.tensor_tensor(lbs[:, 2, :], lbs[:, 0, :], f_mul[:, :], ALU.mult).then_inc(s_ini2, 1)
                dve.wait_ge(s_ini2, 6)
                V.tensor_scalar(f_mul[:, :], lbs[:, 2, :], -0.5, 0.5, ALU.mult, ALU.add).then_inc(s_ini2, 1)
                V.tensor_scalar(f_add[:, :], lbs[:, 2, :], 0.5, 0.5, ALU.mult, ALU.add).then_inc(s_ini2, 1)
                V.tensor_scalar(ga[:, :], ga[:, :], 0.5, None, ALU.mult).then_inc(s_ini2, 1)
                V.tensor_scalar(nsinks[:, :], sinks[:, :], -1.0, None, ALU.mult).then_inc(s_ini2, 1)
                V.tensor_copy(causal[:, :].bitcast(I32), causal[:, :]).then_inc(s_ini2, 1)
                dve.wait_ge(s_ini2, 11)

            def make_lo(it, s, k, nb=8):
                dve.wait_ge(s_hi[s], it * UH + k + 1)
                V.tensor_tensor(wlo[s][:, 0:nb, :], raw[s][:, 0:nb, :], whi[s][:, 0:nb, :].bitcast(F32),
                                ALU.subtract).then_inc(s_lo[s], 1)

            def prep(it, b, src=xs[0], dst=xs[1]):
                dve.wait_ge(s_xroot, it * TB + b + 1)
                if not is_first(it * TB + b):
                    dve.wait_ge(s_xn, it * TB + b + 1)
                V.reciprocal(xrn[:, :], xnrm[:, :]).then_inc(s_xr, 1)
                dve.wait_ge(s_xr, it * TB + b + 1)
                V.scalar_tensor_tensor(out=dst[:, :], in0=src[:, :], scalar=xrn[:, 0:1], in1=g1row[:, :],
                                       op0=ALU.mult, op1=ALU.mult).then_inc(s_xn, 1)

            def prep_split(it, b):
                columns = bass.ds(b * P, P)
                for half in range(2):
                    n = it * 2 * TB + 2 * b + half + 1
                    uh, ul = (u[:, 4 * half:4 * half + 4, columns] for u in (uhi, ulo))
                    xT = X[2 + half][:, :].rearrange("p (c t) -> p c t", c=4)
                    dve.wait_ge(s_ptr0, n)
                    if not is_first(it):
                        V.tensor_scalar(uh, xT, 1.0, None, ALU.mult).then_inc(s_xuhi, 1)
                    dve.wait_ge(s_xuhi, n)
                    V.tensor_tensor(ul, xT, uh.bitcast(F32), ALU.subtract).then_inc(s_xulo, 1)

            def denominators(it, i):
                w = i % 2
                dve.wait_ge(s_exp, it * STEPS + i + 1)
                V.tensor_tensor(den[:, :], rs[:, w, :], es[:, :], ALU.add).then_inc(s_den, 1)
                dve.wait_ge(s_den, it * STEPS + i + 1)
                if i:
                    dve.wait_ge(s_prob, it * STEPS + i)
                V.reciprocal(rd[:, :], den[:, :]).then_inc(s_rd, 1)

            def scores(it, i):
                p, b = divmod(i, TB)
                w = i % 2
                dve.wait_ge(s_score, it * STEPS + i + 1)
                if i >= 2:
                    dve.wait_ge(s_ptr, it * STEPS + i - 1)
                if i == 0 and not is_first(it):
                    dve.wait_ge(s_dist, it)
                d = dist0 if b == 0 else dist
                for par in range(2):
                    slope = 2.0 ** -(2 * p + par + 1)
                    half = slice(par * 256, (par + 1) * 256)
                    last = V.scalar_tensor_tensor(out=pr[w][:, half], in0=d[:, :], scalar=8.0 * slope,
                                                  in1=X[0][:, half], op0=ALU.mult, op1=ALU.add)
                last.then_inc(s_bias, 1)
                dve.wait_ge(s_bias, it * STEPS + i + 1)
                V.tensor_reduce(mx[:, :], pr[w][:, :].rearrange("p (h k) -> p h k", h=2), AX_X,
                                ALU.max).then_inc(s_mx, 1)
                dve.wait_ge(s_mx, it * STEPS + i + 1)
                V.scalar_tensor_tensor(out=nm[:, w, :], in0=mx[:, :], scalar=-0.125,
                                       in1=nsinks[:, 2 * p:2 * p + 2], op0=ALU.mult,
                                       op1=ALU.min).then_inc(s_nm, 1)
                dve.wait_ge(s_nm, it * STEPS + i + 1)
                V.tensor_tensor(nms[:, :], nm[:, w, :], sinks[:, 2 * p:2 * p + 2], ALU.add).then_inc(s_nms, 1)

            def head_group(it, a, part, bank):
                n = it * HEADS + a
                w = a % 2
                if part == 0:
                    dve.wait_ge(s_tf, n + 1)
                    V.tensor_scalar(forget[:, :], forget[:, :], f_mul[:, a:a + 1], f_add[:, a:a + 1],
                                    ALU.mult, ALU.add).then_inc(s_f, 1)
                    dve.wait_ge(s_f, n + 1)
                    if a >= 2:
                        dve.wait_ge(s_kst, n - 1)
                    for c in range(NCH):
                        r = slice(c * CHUNK, (c + 1) * CHUNK)
                        last = V.tensor_tensor_scan(cum[w][:, r], forget[:, r], ones[:, 0:CHUNK], 1.0, ALU.mult, ALU.mult)
                    last.then_inc(s_cum, 1)
                if part == 1:
                    dve.wait_ge(s_tq, n + 1)
                    V.scalar_tensor_tensor(out=gateq[:, :], in0=gateq[:, :], scalar=1.0, in1=bank,
                                           op0=ALU.add, op1=ALU.mult).then_inc(s_qs, 1)
                    dve.wait_ge(s_qs, n + 1)
                    if a >= 2:
                        dve.wait_ge(s_o, n - 1)
                    V.scalar_tensor_tensor(out=qdec[w][:, :], in0=gateq[:, :], scalar=0.5, in1=cum[w][:, :],
                                           op0=ALU.mult, op1=ALU.mult).then_inc(s_qdec, 1)
                if part in (1, 2):
                    half = slice((part - 1) * (T // 2), part * (T // 2))
                    dve.wait_ge(s_cum, n + 1)
                    if a:
                        dve.wait_ge(s_key, n)
                    V.reciprocal(cuminv[:, half], cum[w][:, half]).then_inc(s_inv, 1)
                if part == 3:
                    dve.wait_ge(s_tg, n + 1)
                    V.scalar_tensor_tensor(out=gate[w][:, :], in0=gate[w][:, :], scalar=1.0, in1=bank,
                                           op0=ALU.add, op1=ALU.mult).then_inc(s_gs, 1)

            def keys(it, a):
                n = it * HEADS + a
                dve.wait_ge(s_a, n + 1)
                if a:
                    dve.wait_ge(s_o, n)
                V.tensor_tensor(amask[:, :, :].bitcast(I32),
                                X[2][:, :].rearrange("p (b c) -> p b c", b=TB).bitcast(I32),
                                causal[:, :].bitcast(I32).rearrange("p (o c) -> p o c", o=1)
                                .broadcast_to([P, TB, P]), ALU.bitwise_and).then_inc(s_am, 1)

            def update(it, a):
                n = it * HEADS + a
                s0 = it * (NCH * HEADS) + NCH * a
                if a:
                    dve.wait_ge(s_scar, n)
                    dve.wait_ge(s_o, n)
                for c in range(NCH):
                    if c % 4 == 0:
                        dve.wait_ge(s_upd, it * 2 * HEADS + 2 * a + c // 4 + 1)
                    before = state[:, a, :] if c == 0 else st[(c - 1) // 4][:, (c - 1) % 4, :]
                    if c:
                        dve.wait_ge(s_st, s0 + c)
                    last_token = (c + 1) * CHUNK - 1
                    V.scalar_tensor_tensor(out=st[c // 4][:, c % 4, :], in0=before,
                                           scalar=cum[a % 2][:, last_token:last_token + 1],
                                           in1=X[2 + c // 4][:, (c % 4) * P:(c % 4 + 1) * P],
                                           op0=ALU.mult, op1=ALU.add).then_inc(s_st, 1)

            def output(it, a):
                n = it * HEADS + a
                dve.wait_ge(s_sq, n + 1)
                dve.wait_ge(s_gs, n + 1)
                V.scalar_tensor_tensor(out=gate[a % 2][:, :], in0=X[2][:, :], scalar=ga[:, a:a + 1],
                                       in1=gate[a % 2][:, :], op0=ALU.mult, op1=ALU.mult).then_inc(s_y1, 1)

            def head_sum(it, a):
                n = it * HEADS + a
                dve.wait_ge(s_aroot, n + 1)
                if a:
                    dve.wait_ge(s_amul, n)
                V.reciprocal(hrnrm[:, :], hnrm[:, :]).then_inc(s_arr, 1)

            def head_mul(it, a):
                n = it * HEADS + a
                dve.wait_ge(s_amul, n + 1)
                dve.wait_ge(s_y1, n + 1)
                V.tensor_tensor(gate[a % 2][:, :], gate[a % 2][:, :], X[3][:, :], ALU.mult).then_inc(s_ya, 1)

            def head_lo(it, a):
                dve.wait_ge(s_yahi, it * HEADS + a + 1)
                V.tensor_tensor(ylo[:, a, :], gate[a % 2][:, :], yhi[:, a, :].bitcast(F32),
                                ALU.subtract).then_inc(s_yalo, 1)

            def swa_mul(it, p):
                dve.wait_ge(s_osq, it * PAIRS + p + 1)
                V.scalar_tensor_tensor(out=oT[p][:, :], in0=oT[p][:, :], scalar=gb[:, p:p + 1],
                                       in1=X[1][:, :], op0=ALU.mult, op1=ALU.mult).then_inc(s_yb, 1)

            def swa_lo(it, p):
                dve.wait_ge(s_ybhi, it * PAIRS + p + 1)
                V.tensor_tensor(ylo[:, HEADS + p, :], oT[p][:, :], yhi[:, HEADS + p, :].bitcast(F32),
                                ALU.subtract).then_inc(s_yblo, 1)

            def final_sum(it):
                dve.wait_ge(s_root, it * 2 + 2)
                V.reciprocal(rnrm[:, :], nrm[:, :]).then_inc(s_rroot, 1)

            def final_turn(it, b, banks):
                dve.wait_ge(s_rroot, it * 2 + 2)
                dve.wait_ge(s_ftr, it * 2 * TB + 2 * b + 2)
                dve.wait_ge(s_out[b % 2], it * 32 + 16 * (b // 2) + 16)
                V.tensor_scalar(os_[b % 2][:, D // 2:D], banks[1][:, :], rnrm[:, b:b + 1], None,
                                ALU.mult).then_inc(s_osb, 1)

            def slots(it, first, end, former=None):
                for slot in range(first, end):
                    i = step_at(slot, PROBS)
                    if i is not None:
                        denominators(it, i)
                    mul = head_at(slot, NORM_MUL)
                    if mul is not None:
                        head_mul(it, mul)
                    n = unit_made_at(slot)
                    if n is not None:
                        wait_unit_used(dve, it, n)
                        make_lo(it, n % 2, n // 2)
                    bank = M[slot % 3][:, :]
                    if slot == 0:
                        dve.wait_ge(s_group, it * GROUPS + 1)
                        dve.wait_ge(s_kcar, it + 1)
                        for g in range(KV):
                            for par in range(2):
                                V.tensor_copy(keyz[64 * par:64 * par + 64, g, par, BLOCK:BLOCK + T],
                                              M[0][64 * g:64 * g + 64, :]).then_inc(s_k, 1)
                    i = step_at(slot, SCORE)
                    if i is not None:
                        scores(it, i)
                    a, part = head_part(slot)
                    if a is not None:
                        head_group(it, a, part, bank)
                    if mul is not None:
                        head_lo(it, mul)
                    if slot == SWA_SUM:
                        dve.wait_ge(s_sroot, it + 1)
                        V.reciprocal(srnrm[:, :], snrm[:, :]).then_inc(s_srr, 1)
                    if slot == SWA_MUL:
                        dve.wait_ge(s_smul, it + 1)
                        swa_mul(it, 0)
                    i = step_at(slot, PV)
                    if i is not None and i % TB == TB - 1:
                        dve.wait_ge(s_pv, it * STEPS + i + 1)
                        V.tensor_copy(oT[i // TB][:, :], M[3][:, :]).then_inc(s_oT, 1)
                    for offset, step in ((KEYS, keys), (UPDATE, update), (OUTPUT, output), (NORM_SUM, head_sum)):
                        a = head_at(slot, offset)
                        if a is not None:
                            step(it, a)
                    if slot == SWA_MUL:
                        swa_lo(it, 0)
                        for p in range(1, PAIRS):
                            swa_mul(it, p)
                        for p in range(1, PAIRS):
                            swa_lo(it, p)
                    if former is not None:
                        if slot == FINAL_SUM:
                            final_sum(former)
                        if 0 <= slot - FINAL_TURN < TB:
                            final_turn(former, slot - FINAL_TURN, X[2:4])

            def out_b(it):
                wait_unit_used(dve, it, OUT_B + 1)
                make_lo(it, (OUT_B + 1) % 2, (OUT_B + 1) // 2)
                dve.wait_ge(s_xT, it * 2 * TB + 2 * TB)
                for c in range(CS):
                    if c < 4:
                        bank = M[c]
                    else:
                        n = OUT_B + 2 + c - 4
                        wait_unit_used(dve, it, n)
                        make_lo(it, n % 2, n // 2)
                        bank = X[(1, 2, 3, 0)[c - 4]]
                    V.tensor_tensor(h[:, c, :], h[:, c, :], bank[:, :], ALU.add).then_inc(s_h, 1)
                    if c:
                        u_lo(it, c - 1)
                u_lo(it, CS - 1)

            def u_lo(it, c):
                dve.wait_ge(s_uhi, it * KD + c + 1)
                V.scalar_tensor_tensor(out=ulo[:, c, :], in0=h[:, c, :], scalar=g2[:, c:c + 1],
                                       in1=uhi[:, c, :].bitcast(F32), op0=ALU.mult,
                                       op1=ALU.subtract).then_inc(s_ulo, 1)

            def ffn_lo(it, jj, m):
                dve.wait_ge(s_group, it * GROUPS + FFN0 + 4 * jj + m + 1)
                make_lo(it, m % 2, 2 * jj + (FFN0 + 2 + m) // 2)

            def read_gate(it, jj, j):
                if not is_first(jj):
                    dve.wait_ge(s_alo[j], it * (KF // 2) + jj)
                V.tensor_tensor(gu[j][:, :], M[2 * j][:, :], factors, ALU.mult).then_inc(s_gate[j], 1)

            def read_up(it, jj, j):
                done = it * (KF // 2) + jj + 1
                V.tensor_tensor(upn, M[2 * j + 1][:, :], factors, ALU.mult).then_inc(s_up[j], 1)
                dve.wait_ge(s_up[j], done)
                dve.wait_ge(s_silu[j], done)
                V.tensor_tensor(gu[j][:, :], gu[j][:, :], upn, ALU.mult).then_inc(s_prod[j], 1)
                dve.wait_ge(s_prod[j], done)
                block = bass.ds(2 * jj + j, 1)
                wide = gu[j][:, :].rearrange("p (o t) -> p o t", o=1)
                V.tensor_scalar(ahi[:, block, :], wide, 1.0, None, ALU.mult).then_inc(s_ahi[j], 1)
                dve.wait_ge(s_ahi[j], done)
                V.tensor_tensor(alo[:, block, :], wide, ahi[:, block, :].bitcast(F32),
                                ALU.subtract).then_inc(s_alo[j], 1)

            def down_los(it, cc, units):
                for m in units:
                    dve.wait_ge(s_dpart, it * DPARTS + cc * (2 * ND) + m - 1)
                    make_lo(it, m % 2, cc * ND + DOWN0 // 2 + m // 2, DOWN_PARTS[m % ND])
                    if (m - 1) % ND == 0:
                        add_block(it, cc, (m - 1) // ND - 1)

            def add_block(it, cc, half):
                c = cc * 2 + half
                hc = h[:, bass.ds(c, 1), :]
                V.tensor_tensor(hc, hc, M[half][:, :].rearrange("p (o t) -> p o t", o=1),
                                ALU.add).then_inc(s_h2[half], 1)
                dve.wait_ge(s_h2[half], it * (KD // 2) + cc + 2)
                dve.wait_ge(s_h2acc[half], it * (KD // 2) + cc + 1)
                V.tensor_tensor(sqs[half][:, :].rearrange("p (o t) -> p o t", o=1), hc, hc,
                                ALU.mult).then_inc(s_h2sq[half], 1)
                dve.wait_ge(s_h2sq[half], it * (KD // 2) + cc + 1)
                V.tensor_scalar(hc, hc, gf[:, bass.ds(c, 1)], None, ALU.mult).then_inc(s_fin[half], 1)

            def body(it, final):
                slots(it, SPLIT, SLOTS)
                out_b(it)
                ffn_lo(it, 0, 0)
                ffn_lo(it, 0, 1)
                dve.wait_ge(s_root, it * 2 + 1)
                V.reciprocal(factors, factors).then_inc(s_rroot, 1)
                ffn_lo(it, 0, 2)
                dve.wait_ge(s_rroot, it * 2 + 1)
                read_gate(it, 0, 0)
                read_gate(it, 0, 1)
                read_up(it, 0, 0)
                ffn_lo(it, 0, 3)
                read_up(it, 0, 1)
                with dve.Fori(1, KF // 2) as jj:
                    for m in range(4):
                        ffn_lo(it, jj, m)
                        if m % 2 == 0:
                            read_gate(it, jj, m // 2)
                        else:
                            read_up(it, jj, m // 2)
                if not final:
                    with dve.Fori(0, CS // 2) as cc:
                        down_los(it, cc, range(2, 4))
                        prep(it + 1, cc)
                        down_los(it, cc, range(4, PREP_PART + 3))
                        prep_split(it + 1, cc)
                        down_los(it, cc, range(PREP_PART + 3, 2 * ND + 2))
                    slots(it + 1, 0, SPLIT, it)
                else:
                    with dve.Fori(0, CS // 2 - 1) as cc:
                        down_los(it, cc, range(2, 2 * ND + 2))
                    down_los(it, CS // 2 - 1, range(2, 2 * ND))
                    dve.wait_ge(s_dpart, (it + 1) * DPARTS)
                    add_block(it, CS // 2 - 1, 1)
                    final_sum(it)
                    for b in range(TB):
                        final_turn(it, b, LAST_BANKS[b])

            def prologue():
                for b in range(TB):
                    prep(0, b, first_x[b], first_x[b])
                    if b:
                        prep_split(0, b - 1)
                    if b < 2:
                        make_lo(0, b, 0)
                prep_split(0, TB - 1)
                dve.wait_ge(s_ini, INI)
                dve.wait_ge(s_dst, DST)
                parameters()
                slots(0, 0, SPLIT)

            dve.wait_ge(s_g1, 16)
            over_superblocks(dve, prologue, body)

        @block.gpsimd
        def _(pool):
            G = nc.gpsimd
            for s in s_h2acc:
                pool.sem_inc(s, 1)
            G.memset(ident[:, :], 0.0).then_inc(s_idn, 1)
            G.memset(epst[:, :], EPS).then_inc(s_idn, 1)
            pool.wait_ge(s_idn, 2)
            G.affine_select(out=ident[:, :], in_=ident[:, :], compare_op=ALU.not_equal, fill=1.0, base=0,
                            pattern=[[-1, P]], channel_multiplier=1).then_inc(s_idn, 1)
            G.memset(ones[:, :], 1.0).then_inc(s_ini, 1)
            G.memset(keyz[:, :, :, :], 0.0).then_inc(s_ini, 1)
            G.memset(vals[:, :, :], 0.0).then_inc(s_ini, 1)
            G.memset(kstz[:, :, :, :], 0.0).then_inc(s_ini, 1)
            G.memset(state[:, :, :], 0.0).then_inc(s_ini, 1)
            G.memset(causal[:, :], -1.0).then_inc(s_ini, 1)
            G.iota(dist[:, :].bitcast(I32), [[1, 2 * BLOCK]], base=-BLOCK, channel_multiplier=-1).then_inc(s_ini, 1)
            pool.wait_ge(s_ini, 7)
            G.affine_select(out=causal[:, :], in_=causal[:, :], compare_op=ALU.is_ge, fill=0.0, base=0,
                            pattern=[[1, P]], channel_multiplier=-1).then_inc(s_ini, 1)
            G.tensor_copy(dist0[:, :], dist[:, :].bitcast(I32)).then_inc(s_ini, 1)
            pool.wait_ge(s_ini, 9)
            G.memset(causal[0:CHUNK, CHUNK:P], 0.0).then_inc(s_ini, 1)
            G.affine_select(out=dist0[:, :], in_=dist0[:, :], compare_op=ALU.is_ge, fill=MASKED, base=BLOCK,
                            pattern=[[-1, 2 * BLOCK]], channel_multiplier=1).then_inc(s_dst, 1)
            pool.wait_ge(s_dst, 1)
            G.affine_select(out=dist[:, :], in_=dist0[:, :], compare_op=ALU.is_ge, fill=MASKED, base=-1,
                            pattern=[[1, 2 * BLOCK]], channel_multiplier=-1).then_inc(s_dst, 1)
            pool.wait_ge(s_dst, 2)
            G.tensor_copy(dist0[:, BLOCK:2 * BLOCK], dist[:, BLOCK:2 * BLOCK]).then_inc(s_dst, 1)
            G.memset(dist0[:, 0:BLOCK], MASKED).then_inc(s_dst, 1)
            pool.wait_ge(s_dst, 4)
            pool.wait_ge(s_ini, 10)

            def copy(out, in_):
                return G.tensor_tensor(out, in_, ones[:, 0:1].broadcast_to(list(in_.shape)), ALU.mult)

            keys_all = keyz[:, :, :, :].rearrange("p g r t -> p (g r) t")

            def key_steps(it, a):
                n = it * HEADS + a
                pool.wait_ge(s_f, n + 1)
                if a:
                    pool.wait_ge(s_a, n)
                G.tensor_tensor(key[:, :], ones[:, 0:1].broadcast_to([P, T]), forget[:, :],
                                ALU.subtract).then_inc(s_key0, 1)
                pool.wait_ge(s_key0, n + 1)
                pool.wait_ge(s_inv, 2 * n + 2)
                G.tensor_tensor(key[:, :], key[:, :], cuminv[:, :], ALU.mult).then_inc(s_key, 1)
                pool.wait_ge(s_key, n + 1)
                ends = cum[a % 2][:, :].rearrange("p (c t) -> p c t", c=NCH)[:, :, CHUNK - 1:CHUNK]
                G.tensor_tensor(kstate[:, :].rearrange("p (c t) -> p c t", c=NCH),
                                key[:, :].rearrange("p (c t) -> p c t", c=NCH),
                                ends.broadcast_to([P, NCH, CHUNK]), ALU.mult).then_inc(s_kst, 1)

            def normalise(it, i):
                pool.wait_ge(s_rd, it * STEPS + i + 1)
                halves = pr[i % 2][:, :].rearrange("p (h k) -> p h k", h=2)
                G.tensor_tensor(halves, halves, rd[:, :].rearrange("p (h o) -> p h o", o=1)
                                .broadcast_to([P, 2, 2 * BLOCK]), ALU.mult).then_inc(s_prob, 1)
                if i == (PAIRS - 1) * TB + 1:
                    pool.wait_ge(s_bias, it * STEPS + i)
                    copy(dist0[:, :], dist[:, :]).then_inc(s_dist, 1)

            def carry_state(it, a):
                n = it * HEADS + a
                pool.wait_ge(s_o, n + 1)
                pool.wait_ge(s_st, it * (NCH * HEADS) + NCH * (a + 1))
                copy(state[:, a, :], st[1][:, 3, :]).then_inc(s_scar, 1)

            def slots(it, first, end):
                for slot in range(first, end):
                    if slot == 0:
                        if not is_first(it):
                            pool.wait_ge(s_score, it * STEPS)
                        copy(keys_all[:, :, 0:BLOCK], keys_all[:, :, T:T + BLOCK]).then_inc(s_kcar, 1)
                        if not is_first(it):
                            pool.wait_ge(s_pv, it * STEPS)
                        copy(vals[:, 0, :], vals[:, TB, :]).then_inc(s_vcar, 1)
                    i = step_at(slot, PROBS)
                    if i is not None:
                        normalise(it, i)
                    for offset, step in ((KEY_PRODUCTS, key_steps), (OUTPUT, carry_state)):
                        a = head_at(slot, offset)
                        if a is not None:
                            step(it, a)
                    i = step_at(slot, PV + 1)
                    if i is not None and i % TB == TB - 1 and i >= TB:
                        p = i // TB
                        pool.wait_ge(s_osq, it * PAIRS + p + 1)
                        if p >= 2:
                            pool.wait_ge(s_oacc, it * (PAIRS - 1) + p - 1)
                        G.tensor_tensor(qT[0][:, :], qT[0][:, :], qT[p][:, :], ALU.add).then_inc(s_oacc, 1)

            acc = sacc[:, 0:T]

            def body(it, final):
                slots(it, SPLIT, SLOTS)
                for c in range(KD):
                    pool.wait_ge(s_hsq, it * KD + c + 1)
                    if c == 0:
                        pool.wait_ge(s_out[0], it * 32 + 16)
                        copy(acc, sqs[0][:, :]).then_inc(s_hacc, 1)
                    else:
                        pool.wait_ge(s_hacc, it * KD + c)
                        G.tensor_tensor(acc, acc, sqs[c % 2][:, :], ALU.add).then_inc(s_hacc, 1)
                for c in range(KD):
                    pool.wait_ge(s_h2sq[c % 2], it * (KD // 2) + c // 2 + 1)
                    if c == 0:
                        pool.wait_ge(s_nsum, it * 2 + 1)
                        copy(acc, sqs[0][:, :]).then_inc(s_h2acc[0], 1)
                    else:
                        pool.wait_ge(s_h2acc[(c - 1) % 2], it * (KD // 2) + (c - 1) // 2 + 2)
                        G.tensor_tensor(acc, acc, sqs[c % 2][:, :], ALU.add).then_inc(s_h2acc[c % 2], 1)
                if not final:
                    slots(it + 1, 0, SPLIT)

            over_superblocks(pool, lambda: slots(0, 0, SPLIT), body)


_INS = ['x', 'ln1_g', 'w_in', 'lb_logits', 'hgrn_norm_g', 'attn_sinks', 'attn_norm_g', 'w_out', 'ln2_g', 'w_gate',
        'w_up', 'w_down', 'final_g']


def kernel(**inputs):
    import numpy as _np
    import concourse.bacc as _bacc
    from concourse import mybir as _mybir
    from concourse.bass_utils import run_bass_kernel_spmd as _run

    nc = _bacc.Bacc("TRN2", target_bir_lowering=False, num_devices=1)
    arrays, args = {}, []
    for name in _INS:
        a = _np.ascontiguousarray(inputs[name])
        arrays[f"in_{name}_dram"] = a
        args.append(nc.dram_tensor(f"in_{name}_dram", a.shape, _mybir.dt.from_np(a.dtype), kind="ExternalInput").ap())
    shape = inputs["x"].shape
    args.append(nc.dram_tensor("out_0_dram", shape, _mybir.dt.float32, kind="ExternalOutput").ap())
    block_program(nc, *args)
    r = _run(nc, [arrays], core_ids=[0])
    return r.results[0]["out_0_dram"]
```
